# Optimizing a Trainium2 kernel written in Bass

```python
import math
import jax, jax.numpy as jnp
from jax import lax
import numpy as np

D_MODEL = 1024
BATCH = 1
SEQ = 256
DEPTH = 2

N_MIXERS = 2
N_EVEN = (DEPTH + 1) // 2
N_ODD = DEPTH // 2
ALPHA = (2.0 * DEPTH) ** 0.25
BETA_INIT = (8.0 * DEPTH) ** -0.25
LN_EPS = 1e-5

GDN_K_HEADS = 4
GDN_V_HEADS = 8
GDN_HEAD_K = 128
GDN_HEAD_V = 128
GDN_KDIM = GDN_K_HEADS * GDN_HEAD_K
GDN_VDIM = GDN_V_HEADS * GDN_HEAD_V
GDN_CONV = 4
GDN_CHUNK = 64
GDN_QKV = 2 * GDN_KDIM + GDN_VDIM
GDN_IN = GDN_QKV + GDN_VDIM + 2 * GDN_V_HEADS
GDN_EPS = 1e-6

SWA_Q_HEADS = 16
SWA_KV_HEADS = 2
SWA_GROUP = SWA_Q_HEADS // SWA_KV_HEADS
SWA_HEAD_DIM = 64
SWA_WINDOW = 128
SWA_BLOCK = 128
SWA_QDIM = SWA_Q_HEADS * SWA_HEAD_DIM
SWA_KVDIM = SWA_KV_HEADS * SWA_HEAD_DIM
SWA_IN = SWA_QDIM + 2 * SWA_KVDIM

REL_BUCKETS = 32
REL_MAX_DIST = 128

FFN_DIM = 2816
N_EXPERTS = 8
TOP_K = 2
EXPERT_DIM = 3584


def layer_norm(x, g, b):
    xf = x.astype(jnp.float32)
    mu = jnp.mean(xf, axis=-1, keepdims=True)
    var = jnp.mean(jnp.square(xf - mu), axis=-1, keepdims=True)
    return ((xf - mu) * lax.rsqrt(var + LN_EPS) * g.astype(jnp.float32) + b.astype(jnp.float32)).astype(x.dtype)

def l2_normalize(x):
    xf = x.astype(jnp.float32)
    return xf * lax.rsqrt(jnp.sum(xf * xf, axis=-1, keepdims=True) + GDN_EPS)

def causal_depthwise_conv(x, w):
    width = w.shape[0]
    return lax.conv_general_dilated(
        x, w[:, None, :].astype(x.dtype), window_strides=(1,), padding=[(width - 1, 0)],
        dimension_numbers=('NWC', 'WIO', 'NWC'), feature_group_count=x.shape[-1])

def gated_delta_rule_chunked(q, k, v, g, beta):
    bsz, t, h, dk = q.shape
    dv = v.shape[-1]
    c = GDN_CHUNK
    n = t // c
    f32 = jnp.float32

    def blocks(a):
        a = a.astype(f32).reshape((bsz, n, c, h) + a.shape[3:])
        return jnp.moveaxis(a, 2, 3)

    q, k, v, g, beta = blocks(q), blocks(k), blocks(v), blocks(g), blocks(beta)
    g_cum = jnp.cumsum(g, axis=-1)
    causal = jnp.tril(jnp.ones((c, c), dtype=bool))
    strict = jnp.tril(jnp.ones((c, c), dtype=bool), -1)
    diff = g_cum[..., :, None] - g_cum[..., None, :]
    decay = jnp.exp(jnp.where(causal, diff, -jnp.inf))
    k_beta = k * beta[..., None]
    v_beta = v * beta[..., None]
    a_kk = jnp.where(strict, jnp.einsum('bnhid,bnhjd->bnhij', k_beta, k) * decay, 0.0)
    eye = jnp.eye(c, dtype=f32)
    t_inv = lax.linalg.triangular_solve(eye + a_kk, jnp.broadcast_to(eye, a_kk.shape),
                                        left_side=True, lower=True, unit_diagonal=True)
    u = jnp.einsum('bnhij,bnhje->bnhie', t_inv, v_beta)
    w = jnp.einsum('bnhij,bnhjd->bnhid', t_inv, k_beta * jnp.exp(g_cum)[..., None])
    a_qk = jnp.einsum('bnhid,bnhjd->bnhij', q, k) * decay
    g_last = g_cum[..., -1]
    q_dec = q * jnp.exp(g_cum)[..., None]
    k_dec = k * jnp.exp(g_last[..., None] - g_cum)[..., None]
    xs = (jnp.moveaxis(q_dec, 1, 0), jnp.moveaxis(k_dec, 1, 0), jnp.moveaxis(u, 1, 0),
          jnp.moveaxis(w, 1, 0), jnp.moveaxis(a_qk, 1, 0), jnp.moveaxis(jnp.exp(g_last), 1, 0))

    def step(s, inp):
        qd, kd, uc, wc, aqk, dl = inp
        v_new = uc - jnp.einsum('bhcd,bhde->bhce', wc, s)
        o = jnp.einsum('bhcd,bhde->bhce', qd, s) + jnp.einsum('bhcs,bhse->bhce', aqk, v_new)
        s = s * dl[..., None, None] + jnp.einsum('bhcd,bhce->bhde', kd, v_new)
        return s, o

    s0 = jnp.zeros((bsz, h, dk, dv), f32)
    _, o = lax.scan(step, s0, xs)
    o = jnp.moveaxis(o, 0, 1)
    return jnp.moveaxis(o, 2, 3).reshape(bsz, t, h, dv)

def gated_deltanet(x, w_in, conv_w, a_log, dt_bias, norm_w, w_out):
    bsz, t, _ = x.shape
    proj = x @ w_in
    o1 = GDN_QKV
    o2 = o1 + GDN_VDIM
    o3 = o2 + GDN_V_HEADS
    qkv = jax.nn.silu(causal_depthwise_conv(proj[..., :o1], conv_w))
    z = proj[..., o1:o2].reshape(bsz, t, GDN_V_HEADS, GDN_HEAD_V)
    b_logit = proj[..., o2:o3]
    a_logit = proj[..., o3:]
    q = qkv[..., :GDN_KDIM].reshape(bsz, t, GDN_K_HEADS, GDN_HEAD_K)
    k = qkv[..., GDN_KDIM:2 * GDN_KDIM].reshape(bsz, t, GDN_K_HEADS, GDN_HEAD_K)
    v = qkv[..., 2 * GDN_KDIM:].reshape(bsz, t, GDN_V_HEADS, GDN_HEAD_V)
    rep = GDN_V_HEADS // GDN_K_HEADS
    q = jnp.repeat(l2_normalize(q) * (GDN_HEAD_K ** -0.5), rep, axis=2)
    k = jnp.repeat(l2_normalize(k), rep, axis=2)
    beta = jax.nn.sigmoid(b_logit.astype(jnp.float32))
    g = -jnp.exp(a_log.astype(jnp.float32)) * jax.nn.softplus(
        a_logit.astype(jnp.float32) + dt_bias.astype(jnp.float32))
    o = gated_delta_rule_chunked(q, k, v, g, beta)
    o = o * lax.rsqrt(jnp.mean(o * o, axis=-1, keepdims=True) + GDN_EPS) * norm_w.astype(jnp.float32)
    o = o * jax.nn.silu(z.astype(jnp.float32))
    return o.reshape(bsz, t, GDN_VDIM).astype(x.dtype) @ w_out

def t5_bucket(dist):
    max_exact = REL_BUCKETS // 2
    df = jnp.maximum(dist, 1).astype(jnp.float32)
    large = max_exact + (jnp.log(df / max_exact) / math.log(REL_MAX_DIST / max_exact)
                         * (REL_BUCKETS - max_exact)).astype(jnp.int32)
    large = jnp.minimum(large, REL_BUCKETS - 1)
    return jnp.where(dist < max_exact, dist, large)

def swa_sink_attention(x, w_in, b_in, sinks, rel_bias, w_out):
    bsz, t, _ = x.shape
    nb = t // SWA_BLOCK
    proj = x @ w_in + b_in
    q = proj[..., :SWA_QDIM].reshape(bsz, nb, SWA_BLOCK, SWA_KV_HEADS, SWA_GROUP, SWA_HEAD_DIM)
    k = proj[..., SWA_QDIM:SWA_QDIM + SWA_KVDIM]
    v = proj[..., SWA_QDIM + SWA_KVDIM:]

    def band(a):
        ab = a.reshape(bsz, nb, SWA_BLOCK, SWA_KV_HEADS, SWA_HEAD_DIM)
        prev = jnp.pad(ab, ((0, 0), (1, 0), (0, 0), (0, 0), (0, 0)))[:, :-1]
        return jnp.concatenate([prev, ab], axis=2)

    kb, vb = band(k), band(v)
    s = jnp.einsum('bnqkgd,bnskd->bnkgqs', q, kb).astype(jnp.float32) * (SWA_HEAD_DIM ** -0.5)
    qi = jnp.arange(SWA_BLOCK)[:, None]
    kj = jnp.arange(2 * SWA_BLOCK)[None, :]
    dist = qi + SWA_BLOCK - kj
    bias = rel_bias.astype(jnp.float32)[t5_bucket(jnp.maximum(dist, 0))]
    bias = jnp.transpose(bias, (2, 0, 1)).reshape(SWA_KV_HEADS, SWA_GROUP, SWA_BLOCK, 2 * SWA_BLOCK)
    band_ok = (dist >= 0) & (dist < SWA_WINDOW)
    blk = jnp.arange(nb)[:, None, None]
    mask = band_ok[None] & ((blk > 0) | (kj >= SWA_BLOCK)[None])
    s = jnp.where(mask[None, :, None, None], s + bias, -jnp.inf)
    sink = jnp.broadcast_to(sinks.astype(jnp.float32).reshape(SWA_KV_HEADS, SWA_GROUP, 1, 1),
                            s.shape[:-1] + (1,))
    p = jax.nn.softmax(jnp.concatenate([s, sink], axis=-1), axis=-1)[..., :-1]
    o = jnp.einsum('bnkgqs,bnskd->bnqkgd', p.astype(vb.dtype), vb).reshape(bsz, t, SWA_QDIM)
    return o @ w_out

def swiglu(x, w_gate, w_up, w_down):
    return (jax.nn.silu(x @ w_gate) * (x @ w_up)) @ w_down

def moe_swiglu(x, w_router, w_gate, w_up, w_down):
    bsz, t, d = x.shape
    xf = x.reshape(bsz * t, d)
    logits = (xf @ w_router).astype(jnp.float32)
    top_val, top_idx = lax.top_k(logits, TOP_K)
    top_w = jax.nn.softmax(top_val, axis=-1)
    gates = jnp.einsum('nk,nke->ne', top_w, jax.nn.one_hot(top_idx, N_EXPERTS, dtype=jnp.float32))
    out = jnp.zeros_like(xf)
    for e in range(N_EXPERTS):
        h = jax.nn.silu(xf @ w_gate[e]) * (xf @ w_up[e])
        out = out + gates[:, e:e + 1].astype(xf.dtype) * (h @ w_down[e])
    return out.reshape(bsz, t, d)

def first_inputs(seed: int = 0) -> dict:
    key = jax.random.key(seed)
    ks = jax.random.split(key, 24)

    def nrm(k, shape, scale):
        return jax.random.normal(k, shape, jnp.float32) * scale

    x = nrm(ks[0], (BATCH, SEQ, D_MODEL), 1.0)
    a_w_in = nrm(ks[1], (N_EVEN, D_MODEL, GDN_IN), D_MODEL ** -0.5)
    a_conv_w = nrm(ks[2], (N_EVEN, GDN_CONV, GDN_QKV), GDN_CONV ** -0.5)
    a_a_log = jnp.log(jax.random.uniform(ks[3], (N_EVEN, GDN_V_HEADS), jnp.float32, 1.0, 16.0))
    dt = jnp.exp(jax.random.uniform(ks[4], (N_EVEN, GDN_V_HEADS), jnp.float32,
                                    math.log(1e-3), math.log(1e-1)))
    a_dt_bias = dt + jnp.log(-jnp.expm1(-dt))
    a_norm_w = 1.0 + nrm(ks[5], (N_EVEN, GDN_HEAD_V), 0.02)
    a_w_out = nrm(ks[6], (N_EVEN, GDN_VDIM, D_MODEL), GDN_VDIM ** -0.5 * BETA_INIT)
    b_w_in = nrm(ks[7], (N_ODD, D_MODEL, SWA_IN), D_MODEL ** -0.5)
    b_b_in = nrm(ks[8], (N_ODD, SWA_IN), 0.02)
    b_sinks = nrm(ks[9], (N_ODD, SWA_Q_HEADS), 1.0)
    b_w_out = nrm(ks[10], (N_ODD, SWA_QDIM, D_MODEL), SWA_QDIM ** -0.5 * BETA_INIT)
    rel_bias = nrm(ks[11], (REL_BUCKETS, SWA_Q_HEADS), 0.3)
    ffn_w_gate = nrm(ks[12], (N_EVEN, D_MODEL, FFN_DIM), D_MODEL ** -0.5)
    ffn_w_up = nrm(ks[13], (N_EVEN, D_MODEL, FFN_DIM), D_MODEL ** -0.5)
    ffn_w_down = nrm(ks[14], (N_EVEN, FFN_DIM, D_MODEL), FFN_DIM ** -0.5 * BETA_INIT)
    moe_router = nrm(ks[15], (N_ODD, D_MODEL, N_EXPERTS), D_MODEL ** -0.5)
    moe_w_gate = nrm(ks[16], (N_ODD, N_EXPERTS, D_MODEL, EXPERT_DIM), D_MODEL ** -0.5)
    moe_w_up = nrm(ks[17], (N_ODD, N_EXPERTS, D_MODEL, EXPERT_DIM), D_MODEL ** -0.5)
    moe_w_down = nrm(ks[18], (N_ODD, N_EXPERTS, EXPERT_DIM, D_MODEL), EXPERT_DIM ** -0.5 * BETA_INIT)
    ln_g = 1.0 + nrm(ks[19], (DEPTH, 2, D_MODEL), 0.02)
    ln_b = nrm(ks[20], (DEPTH, 2, D_MODEL), 0.02)
    return {'x': x, 'a_w_in': a_w_in, 'a_conv_w': a_conv_w, 'a_a_log': a_a_log, 'a_dt_bias': a_dt_bias,
            'a_norm_w': a_norm_w, 'a_w_out': a_w_out, 'b_w_in': b_w_in, 'b_b_in': b_b_in,
            'b_sinks': b_sinks, 'b_w_out': b_w_out, 'rel_bias': rel_bias, 'ffn_w_gate': ffn_w_gate,
            'ffn_w_up': ffn_w_up, 'ffn_w_down': ffn_w_down, 'moe_router': moe_router,
            'moe_w_gate': moe_w_gate, 'moe_w_up': moe_w_up, 'moe_w_down': moe_w_down,
            'ln_g': ln_g, 'ln_b': ln_b}

def first_block(x, a_w_in, a_conv_w, a_a_log, a_dt_bias, a_norm_w, a_w_out, b_w_in, b_b_in, b_sinks,
              b_w_out, rel_bias, ffn_w_gate, ffn_w_up, ffn_w_down, moe_router, moe_w_gate, moe_w_up,
              moe_w_down, ln_g, ln_b):
    for i in range(DEPTH):
        j = i // N_MIXERS
        if i % N_MIXERS == 0:
            h = gated_deltanet(x, a_w_in[j], a_conv_w[j], a_a_log[j], a_dt_bias[j], a_norm_w[j], a_w_out[j])
        else:
            h = swa_sink_attention(x, b_w_in[j], b_b_in[j], b_sinks[j], rel_bias, b_w_out[j])
        x = layer_norm(ALPHA * x + h, ln_g[i, 0], ln_b[i, 0])
        if i % 2 == 0:
            f = swiglu(x, ffn_w_gate[j], ffn_w_up[j], ffn_w_down[j])
        else:
            f = moe_swiglu(x, moe_router[j], moe_w_gate[j], moe_w_up[j], moe_w_down[j])
        x = layer_norm(ALPHA * x + f, ln_g[i, 1], ln_b[i, 1])
    return x


N_HEADS = 8
HEAD_DIM = 128
ATTN_WIDTH = N_HEADS * HEAD_DIM
IDX_HEADS = 16
IDX_DIM = 64
TOPK_MAX = 256
Q_BLOCK = 128
D_RNN = 1408
RNN_BLOCKS = 16
RNN_BLOCK_DIM = D_RNN // RNN_BLOCKS
CONV_WIDTH = 4
LRU_C = 8.0
ROPE_THETA = 10000.0
NORM_EPS = 1e-6

SPLIT_SIZES = (ATTN_WIDTH, ATTN_WIDTH, ATTN_WIDTH, ATTN_WIDTH,
               IDX_HEADS * IDX_DIM, IDX_DIM, IDX_HEADS,
               D_RNN, D_RNN, D_MODEL, D_MODEL)
N_IN = sum(SPLIT_SIZES)


def rmsnorm(x, g):
    xf = x.astype(jnp.float32)
    y = xf * lax.rsqrt(jnp.mean(xf * xf, axis=-1, keepdims=True) + NORM_EPS)
    return (y * g.astype(jnp.float32)).astype(x.dtype)

def rope_tables(positions, dim):
    inv = ROPE_THETA ** (-jnp.arange(0, dim, 2, dtype=jnp.float32) / dim)
    ang = positions.astype(jnp.float32)[..., None] * inv
    return jnp.cos(ang), jnp.sin(ang)

def apply_rope(x, cos, sin):
    extra = x.ndim - cos.ndim
    shape = cos.shape[:2] + (1,) * extra + cos.shape[2:]
    c, s = cos.reshape(shape), sin.reshape(shape)
    x1, x2 = jnp.split(x.astype(jnp.float32), 2, axis=-1)
    return jnp.concatenate([x1 * c - x2 * s, x2 * c + x1 * s], axis=-1).astype(x.dtype)

def dsa_attention(q, k, v, iq, ik, iw):
    B, S, H, Dh = q.shape
    topk = min(TOPK_MAX, S // 4)
    n_blk = S // Q_BLOCK
    key_pos = jnp.arange(S)
    scale = HEAD_DIM ** -0.5
    iw = iw.astype(jnp.float32) * (IDX_HEADS ** -0.5) * (IDX_DIM ** -0.5)

    def block(i):
        q0 = i * Q_BLOCK
        qb = lax.dynamic_slice_in_dim(q, q0, Q_BLOCK, axis=1)
        iqb = lax.dynamic_slice_in_dim(iq, q0, Q_BLOCK, axis=1)
        iwb = lax.dynamic_slice_in_dim(iw, q0, Q_BLOCK, axis=1)
        qpos = q0 + jnp.arange(Q_BLOCK)
        causal = key_pos[None, :] <= qpos[:, None]
        dots = jnp.einsum('bqhd,bsd->bqhs', iqb, ik, preferred_element_type=jnp.float32)
        idx_score = jnp.einsum('bqh,bqhs->bqs', iwb, jax.nn.relu(dots))
        idx_score = jnp.where(causal[None], idx_score, -jnp.inf)
        _, sel = lax.top_k(idx_score, topk)
        valid = sel <= qpos[None, :, None]
        k_sel = jax.vmap(lambda kb, ib: kb[ib])(k, sel)
        v_sel = jax.vmap(lambda vb, ib: vb[ib])(v, sel)
        logits = jnp.einsum('bqhd,bqkhd->bhqk', qb, k_sel, preferred_element_type=jnp.float32) * scale
        logits = jnp.where(valid[:, None], logits, -jnp.inf)
        p = jax.nn.softmax(logits, axis=-1)
        return jnp.einsum('bhqk,bqkhd->bqhd', p.astype(v.dtype), v_sel)

    out = lax.map(block, jnp.arange(n_blk))
    return out.transpose(1, 0, 2, 3, 4).reshape(B, S, H, Dh)

def causal_depthwise_conv_2(x, w, b):
    y = lax.conv_general_dilated(
        x, w[:, None, :].astype(x.dtype), window_strides=(1,),
        padding=[(CONV_WIDTH - 1, 0)], dimension_numbers=('NWC', 'WIO', 'NWC'),
        feature_group_count=x.shape[-1])
    return y + b.astype(x.dtype)

def rg_lru(x, w_r, b_r, w_i, b_i, lam):
    B, S, _ = x.shape
    xb = x.reshape(B, S, RNN_BLOCKS, RNN_BLOCK_DIM)
    r = jax.nn.sigmoid((jnp.einsum('bsnc,ncd->bsnd', xb, w_r).reshape(B, S, D_RNN) + b_r).astype(jnp.float32))
    i = jax.nn.sigmoid((jnp.einsum('bsnc,ncd->bsnd', xb, w_i).reshape(B, S, D_RNN) + b_i).astype(jnp.float32))
    log_a = -LRU_C * r * jax.nn.softplus(-lam.astype(jnp.float32))
    a = jnp.exp(log_a)
    u = jnp.sqrt(-jnp.expm1(2.0 * log_a)) * (i * x.astype(jnp.float32))

    def combine(left, right):
        a_l, b_l = left
        a_r, b_r = right
        return a_l * a_r, a_r * b_l + b_r

    _, h = lax.associative_scan(combine, (a, u), axis=1)
    return h.astype(x.dtype)

def second_inputs(seed: int = 0) -> dict:
    key = jax.random.key(seed)
    ks = jax.random.split(key, 16)
    f32 = jnp.float32
    x = jax.random.normal(ks[0], (BATCH, SEQ, D_MODEL), f32)
    positions = jnp.broadcast_to(jnp.arange(SEQ, dtype=jnp.int32), (BATCH, SEQ))
    norm_g = 1.0 + 0.02 * jax.random.normal(ks[1], (DEPTH, D_MODEL), f32)
    w_in = jax.random.normal(ks[2], (DEPTH, D_MODEL, N_IN), f32) * D_MODEL ** -0.5
    conv_w = jax.random.normal(ks[3], (DEPTH, CONV_WIDTH, D_RNN), f32) * CONV_WIDTH ** -0.5
    conv_b = 0.01 * jax.random.normal(ks[4], (DEPTH, D_RNN), f32)
    w_rg = jax.random.normal(ks[5], (DEPTH, RNN_BLOCKS, RNN_BLOCK_DIM, RNN_BLOCK_DIM), f32) * RNN_BLOCK_DIM ** -0.5
    b_rg = 0.01 * jax.random.normal(ks[6], (DEPTH, D_RNN), f32)
    w_ig = jax.random.normal(ks[7], (DEPTH, RNN_BLOCKS, RNN_BLOCK_DIM, RNN_BLOCK_DIM), f32) * RNN_BLOCK_DIM ** -0.5
    b_ig = 0.01 * jax.random.normal(ks[8], (DEPTH, D_RNN), f32)
    a0 = jax.random.uniform(ks[9], (DEPTH, D_RNN), f32, 0.9, 0.999)
    p = a0 ** (1.0 / LRU_C)
    lru_lambda = jnp.log(p) - jnp.log1p(-p)
    w_out_attn = jax.random.normal(ks[10], (DEPTH, ATTN_WIDTH, D_MODEL), f32) * ATTN_WIDTH ** -0.5
    w_out_rnn = jax.random.normal(ks[11], (DEPTH, D_RNN, D_MODEL), f32) * D_RNN ** -0.5
    w_o = jax.random.normal(ks[12], (DEPTH, D_MODEL, D_MODEL), f32) * D_MODEL ** -0.5
    final_g = 1.0 + 0.02 * jax.random.normal(ks[13], (D_MODEL,), f32)
    return {"x": x, "positions": positions, "norm_g": norm_g, "w_in": w_in,
            "conv_w": conv_w, "conv_b": conv_b, "w_rg": w_rg, "b_rg": b_rg,
            "w_ig": w_ig, "b_ig": b_ig, "lru_lambda": lru_lambda,
            "w_out_attn": w_out_attn, "w_out_rnn": w_out_rnn, "w_o": w_o,
            "final_g": final_g}

def second_block(x, positions, norm_g, w_in, conv_w, conv_b, w_rg, b_rg, w_ig, b_ig,
              lru_lambda, w_out_attn, w_out_rnn, w_o, final_g):
    B, S, _ = x.shape
    offsets = np.cumsum(SPLIT_SIZES)[:-1].tolist()
    cos_a, sin_a = rope_tables(positions, HEAD_DIM)
    cos_i, sin_i = rope_tables(positions, IDX_DIM)
    for l in range(DEPTH):
        h = rmsnorm(x, norm_g[l])
        proj = h @ w_in[l]
        q, k, v, ga, iq, ik, iw, xr, gr, ma, mb = jnp.split(proj, offsets, axis=-1)
        q = apply_rope(q.reshape(B, S, N_HEADS, HEAD_DIM), cos_a, sin_a)
        k = apply_rope(k.reshape(B, S, N_HEADS, HEAD_DIM), cos_a, sin_a)
        v = v.reshape(B, S, N_HEADS, HEAD_DIM)
        iq = apply_rope(iq.reshape(B, S, IDX_HEADS, IDX_DIM), cos_i, sin_i)
        ik = apply_rope(ik, cos_i, sin_i)
        attn = dsa_attention(q, k, v, iq, ik, iw).reshape(B, S, ATTN_WIDTH)
        y_a = (attn * jax.nn.silu(ga)) @ w_out_attn[l]
        xr = causal_depthwise_conv_2(xr, conv_w[l], conv_b[l])
        hr = rg_lru(xr, w_rg[l], b_rg[l], w_ig[l], b_ig[l], lru_lambda[l])
        y_b = (hr * jax.nn.silu(gr)) @ w_out_rnn[l]
        merged = jax.nn.sigmoid(ma) * y_a + jax.nn.sigmoid(mb) * y_b
        x = x + merged @ w_o[l]
    return rmsnorm(x, final_g)


def setup_inputs(seed=0):
    out = dict(first_inputs(seed))
    for name, value in second_inputs(seed + 1).items():
        if name != "x":
            out[name + "_2"] = value
    return out


def reference(
    x, a_w_in, a_conv_w, a_a_log, a_dt_bias, a_norm_w, a_w_out, b_w_in, b_b_in, b_sinks,
    b_w_out, rel_bias, ffn_w_gate, ffn_w_up, ffn_w_down, moe_router, moe_w_gate, moe_w_up,
    moe_w_down, ln_g, ln_b, positions_2, norm_g_2, w_in_2, conv_w_2, conv_b_2, w_rg_2, b_rg_2,
    w_ig_2, b_ig_2, lru_lambda_2, w_out_attn_2, w_out_rnn_2, w_o_2, final_g_2,
):
    x = first_block(
        x, a_w_in, a_conv_w, a_a_log, a_dt_bias, a_norm_w, a_w_out, b_w_in, b_b_in, b_sinks,
        b_w_out, rel_bias, ffn_w_gate, ffn_w_up, ffn_w_down, moe_router, moe_w_gate, moe_w_up,
        moe_w_down, ln_g, ln_b,
    )
    return second_block(
        x, positions_2, norm_g_2, w_in_2, conv_w_2, conv_b_2, w_rg_2, b_rg_2, w_ig_2, b_ig_2,
        lru_lambda_2, w_out_attn_2, w_out_rnn_2, w_o_2, final_g_2,
    )


_drawn_inputs = setup_inputs


def setup_inputs(seed=0):
    import zlib

    import numpy as np

    out = dict(_drawn_inputs(seed))
    spreads = {}
    factors = {'a_norm_w': 4.74,
     'b_b_in': 3.161,
     'b_sinks': 3.87,
     'norm_g_2': 3.681,
     'conv_b_2': 3.017,
     'b_rg_2': 8.0,
     'b_ig_2': 8.0,
     'final_g_2': 2.776}
    for name, (base, spread) in spreads.items():
        noise = np.random.default_rng([zlib.crc32(name.encode()), seed]).standard_normal(out[name].shape)
        drawn = base * np.exp(spread * noise) if base else spread * noise
        out[name] = __import__('jax').numpy.asarray(drawn.astype(out[name].dtype))
    for name, factor in factors.items():
        out[name] = (out[name] * factor).astype(out[name].dtype)
    return out
```

```python
from contextlib import ExitStack

import concourse.bass as bass
from concourse import mybir
from concourse.alu_op_type import AluOpType as ALU

F32 = mybir.dt.float32
I32 = mybir.dt.int32
U32 = mybir.dt.uint32
ACT = mybir.ActivationFunctionType
AX_X = mybir.AxisListType.X

T = 256
D = 1024
ALPHA = 4.0 ** 0.25
LN_EPS = 1e-5
EPS = 1e-6
NEG = -1.0e30
RING = 6
SLOT = 4096
WORK = 28000
NE = 8
FE = 3584

C_ID, C_ONE, C_ROTA, C_ROTI, C_TRIL, C_LT, C_IOTA = range(7)
G_CUM, G_STRICT, G_BLOCK, G_LEVEL = 0, 1, 2, 3


class Queue:

    def __init__(self, sem):
        self.sem, self.n, self.q, self.seen = sem, 0, [], {}

    def wait(self, *tokens):
        for t in tokens:
            if t is None:
                continue
            if isinstance(t, list):
                self.wait(*t)
                continue
            sem, val = t
            if self.seen.get(sem.name, 0) < val:
                self.seen[sem.name] = val
                self.q.append(("wait", sem, val))

    def __call__(self, fn, *args, after=(), mark=True, **kw):
        self.wait(*after)
        if mark:
            self.n += 1
        self.q.append(("op", fn, args, kw, self.sem if mark else None, 1))
        return (self.sem, self.n)

    def dma(self, fn, out, in_, sem, after=(), **kw):
        self.wait(*after)
        self.q.append(("op", fn, (out, in_), kw, sem, 16))

    @property
    def last(self):
        return (self.sem, self.n) if self.n else None


def emit(eng, q):
    for item in q:
        if item[0] == "wait":
            eng.wait_ge(item[1], item[2])
        elif item[0] == "op":
            ins = item[1](*item[2], **item[3])
            if item[4] is not None:
                ins.then_inc(item[4], item[5])
        else:
            flag = eng.value_load(item[1])
            with eng.If(flag > 0):
                emit(eng, item[2])


def program(nc, p, out, debug=None, stop=99):
    ctx = ExitStack()
    with ctx:
        _program(nc, ctx, p, out, debug or {}, stop)


def _program(nc, ctx, p, out, debug, stop):
    def sem(name):
        return ctx.enter_context(nc.semaphore(name))

    ring = ctx.enter_context(nc.sbuf_tensor("ring", [128, RING, SLOT], F32))
    work = ctx.enter_context(nc.sbuf_tensor("work", [128, WORK], F32))
    bank = [ctx.enter_context(nc.psum_tensor(f"bank{i}", [128, 512], F32)) for i in range(8)]

    PE, V, A, G, SP = (Queue(sem(n)) for n in ("s_pe", "s_dve", "s_act", "s_pool", "s_sp"))
    te, ve, ac, gp, sy = nc.tensor, nc.vector, nc.scalar, nc.gpsimd, nc.sync
    queues = {"PE": PE, "V": V, "A": A, "G": G, "SP": SP}

    class Stack:
        at = 0

    def take(n):
        a = Stack.at
        Stack.at += n
        assert Stack.at <= WORK, Stack.at
        return work[:, a:a + n]

    def v3(ap, a):
        return ap.rearrange("p (a b) -> p a b", a=a)

    def v4(ap, a, b):
        return ap.rearrange("p (a b c) -> p a b c", a=a, b=b)

    free = [None] * 8

    class Ring:
        n = 0
        s = [sem(f"s_ring{i}") for i in range(RING)]
        count = [0] * RING
        used = [None] * RING

    def load(parts):
        i = Ring.n % RING
        Ring.n += 1
        at, views = 0, []
        for cols, rows, shape, src in parts:
            dst = ring[0:rows, i, at:at + cols]
            if len(shape) == 2:
                dst = dst.rearrange("p (a b) -> p a b", a=shape[0])
            SP.dma(sy.dma_start, dst, src, Ring.s[i], after=[Ring.used[i]])
            Ring.count[i] += 16
            views.append(dst)
            at += cols
        assert at <= SLOT
        return views, (Ring.s[i], Ring.count[i]), i

    class Misc:
        n = 0

    def small(pairs, after=(), name=None, q=None):
        s = sem(name or f"s_m{Misc.n}")
        Misc.n += 1
        for dst, src in pairs:
            (q or G).dma((sy if q is SP else gp).dma_start, dst, src, s, after=after)
        return (s, 16 * len(pairs))

    def mm(o, l, r, start, stop, after=(), mark=False):
        return PE(te.matmul, o, l, r, start=start, stop=stop, after=after, mark=mark)

    def tr(o, i, after=(), mark=False):
        n = i.shape[0]
        return PE(te.transpose, o, i, ident[0:n, 0:n], after=after, mark=mark)

    def dump(name, ap, after):
        if name in debug:
            t = small([(debug[name], ap)], after=after, q=SP)
            dumps.append(t)
            for q in (PE, V, A, G):
                q.wait(t)
    dumps = []

    consts = take(7 * 128)
    X = v3(take(2 * D), 2)
    XT = v3(take(8 * T), 8)

    def C(k):
        return consts[:, k * 128:(k + 1) * 128]
    ident, ones = C(C_ID), C(C_ONE)
    base = Stack.at

    t_const = small([(consts, p["c_main"])], q=SP)
    t_x = small([(X, p["x"].rearrange("o (a p) d -> p (o a) d", p=128))], q=SP)

    class Alt:
        n = 0

    def copy(o, i, after=()):
        Alt.n += 1
        if Alt.n % 2:
            return V(ve.tensor_copy, o, i, after=after)
        return A(ac.copy, o, i, after=after)

    def rows_to_cols(src, dst, after, banks=(6, 7)):
        done = []
        for t in range(2):
            for g in range(2):
                b = banks[g]
                for j in range(4):
                    k = 4 * g + j
                    tk = tr(bank[b][:, j * 128:(j + 1) * 128], src[:, t, k * 128:(k + 1) * 128],
                            after=[after[t], free[b]] if j == 0 else (), mark=(j == 3))
                free[b] = copy(dst[:, 4 * g:4 * g + 4, t * 128:(t + 1) * 128], v3(bank[b][:, :], 4), after=[tk])
                done.append(free[b])
        return done

    def fm_tiles(xt, src, c0, n, width, banks, evac, x_ready, per=4, kt=8):
        first = True
        i = 0
        nb = 0
        while i < n:
            m4 = min(per, n - i)
            cols = m4 * width
            (w,), t_w, slot = load([(kt * cols, 128, (kt, cols),
                                     src[:, c0 + i * width:c0 + i * width + cols].rearrange("(k p) c -> p k c", p=128))])
            j = 0
            while j < m4:
                m2 = min(2, m4 - j)
                b = banks[nb % len(banks)]
                nb += 1
                for jj in range(m2):
                    for k in range(kt):
                        last = k == kt - 1 and jj == m2 - 1
                        tk = mm(bank[b][0:width, jj * T:(jj + 1) * T], w[:, k, (j + jj) * width:(j + jj + 1) * width],
                                xt[:, k, :], k == 0, k == kt - 1,
                                after=[t_w, free[b]] + ([x_ready] if first else []) if k == 0 and jj == 0 else (), mark=last)
                        first = False
                free[b] = evac(i + j, bank[b][0:width, 0:m2 * T].rearrange("p (a b) -> p a b", a=m2), m2, tk)
                j += m2
            Ring.used[slot] = PE.last
            i += m4

    def rm_proj(xt, src, c0, n, banks, evac, x_ready, kt=8):
        nb = 0
        for c in range(n // 512):
            (w,), t_w, slot = load([(kt * 512, 128, (kt, 512),
                                     src[:, c0 + c * 512:c0 + (c + 1) * 512].rearrange("(k p) c -> p k c", p=128))])
            for t in range(2):
                b = banks[nb % len(banks)]
                nb += 1
                for k in range(kt):
                    tk = mm(bank[b][:, :], xt[:, k, t * 128:(t + 1) * 128], w[:, k, :], k == 0, k == kt - 1,
                            after=[t_w, free[b], x_ready] if k == 0 else (), mark=(k == kt - 1))
                free[b] = evac(t, c, bank[b][:, :], tk)
            Ring.used[slot] = PE.last

    def norm_rows(src, y, t, gb, t_gb, tmp, ready):
        st, mv, rs = tmp[:, 0:12], tmp[:, 12:14], tmp[:, 14:16]
        for h in range(2):
            V(ve.bn_stats, st[:, 6 * h:6 * h + 6], y[:, 512 * h:512 * h + 512], after=[ready])
        V(ve.bn_aggr, mv, v3(st, 2), after=[V.last])
        V(ve.tensor_scalar, rs[:, 0:1], mv[:, 1:2], LN_EPS, None, ALU.add, after=[V.last])
        k = A(ac.activation, rs[:, 1:2], rs[:, 0:1], ACT.Sqrt, after=[V.last])
        V(ve.reciprocal, rs[:, 0:1], rs[:, 1:2], after=[k])
        V(ve.tensor_scalar, y, y, mv[:, 0:1], rs[:, 0:1], ALU.subtract, ALU.mult, after=[V.last])
        V(ve.tensor_tensor, y, y, gb[:, 0, :], ALU.mult, after=[V.last, t_gb])
        return V(ve.tensor_tensor, y, y, gb[:, 1, :], ALU.add, after=[V.last])

    def residual_norm(banks4, t_mm, gb, t_gb, tmps):
        done = []
        for t in range(2):
            for h in range(2):
                b = banks4[2 * t + h]
                xs = X[:, t, 512 * h:512 * h + 512]
                free[b] = V(ve.scalar_tensor_tensor, xs, xs, ALPHA, bank[b][:, :], ALU.mult, ALU.add, after=[t_mm[t], PE.last])
            done.append(norm_rows(X, X[:, t, :], t, gb, t_gb, tmps[t], V.last))
        return done

    def bcast(src, n):
        return src.partition_broadcast(n)

    t_xt = rows_to_cols(X, XT, [[t_const, t_x]] * 2)

    def gdn(x_ready):
        Stack.at = base
        cg = take(9 * 128)

        def CG(k):
            return cg[:, k * 128:(k + 1) * 128]
        gb = v3(take(2 * D), 2)
        nw = take(128)
        ab = take(16)
        wba = v3(take(8 * 16), 8)
        prow = take(128)
        cw = take(64)
        gates = take(13 * 16)
        qkv = v3(take(16 * T), 16)
        Z = v3(take(2 * D), 2)

        t_p = small([(cg, p["c_gdn"]),
                     (prow[0:64, :], p["a_conv_w"][0].rearrange("j (i c) -> (j i) c", c=128)),
                     (wba, p["a_w_in"][0][:, 3072:3088].rearrange("(k p) c -> p k c", p=128)),
                     (ab[:, 0:8], bcast(p["a_a_log"][0], 128)),
                     (ab[:, 8:16], bcast(p["a_dt_bias"][0], 128)),
                     (nw, bcast(p["a_norm_w"][0], 128))])
        t_gb = small([(gb[:, 0, :], bcast(p["ln_g"][0, 0], 128)), (gb[:, 1, :], bcast(p["ln_b"][0, 0], 128))])
        k = tr(bank[0][:, 0:64], prow[0:64, :], after=[t_p, x_ready], mark=True)
        free[0] = V(ve.tensor_copy, cw, bank[0][:, 0:64], after=[k])
        t_cw = V.last
        for t in range(2):
            for kk in range(8):
                k = mm(bank[1][:, 16 * t:16 * t + 16], XT[:, kk, t * 128:(t + 1) * 128], wba[:, kk, :], kk == 0, kk == 7,
                       mark=(kk == 7), after=[x_ready])
        free[1] = V(ve.tensor_copy, v3(gates[:, 0:32], 2), v3(bank[1][:, 0:32], 2), after=[k])
        bav = v3(gates[:, 0:32], 2)
        beta = v3(gates[:, 32:48], 2)
        g_, gc, egc, kds, t1, t2, t3 = (v3(gates[:, 48 + 16 * i:64 + 16 * i], 2) for i in range(7))
        dl = v3(gates[:, 160:192], 4)
        ea = gates[:, 192:200]
        A(ac.activation, beta, bav[:, :, 0:8], ACT.Sigmoid, after=[V.last])
        t_beta = A.last
        abx = ab[:, 8:16].unsqueeze(1).broadcast_to([128, 2, 8])
        V(ve.tensor_tensor, t1, bav[:, :, 8:16], abx, ALU.add, after=[V.last, t_p])
        V(ve.tensor_scalar, t2, t1, -1.0, None, ALU.mult, after=[V.last])
        V(ve.tensor_tensor, t2, t1, t2, ALU.min, after=[V.last])
        k = A(ac.activation, t2, t2, ACT.Exp, after=[V.last])
        A(ac.activation, ea, ab[:, 0:8], ACT.Exp, after=[t_p])
        log1p(t2, t3, g_, k)
        V(ve.tensor_scalar, t1, t1, 0.0, None, ALU.max, after=[V.last])
        V(ve.tensor_tensor, t1, t1, t2, ALU.add, after=[V.last])
        V(ve.tensor_scalar, ea, ea, -1.0, None, ALU.mult, after=[A.last])
        t_g = V(ve.tensor_tensor, g_, t1, ea.unsqueeze(1).broadcast_to([128, 2, 8]), ALU.mult, after=[V.last])
        gv = gates[:, 48:64]
        mm(bank[1][:, 0:16], CG(G_CUM), gv, True, True, after=[t_g, free[1]])
        mm(bank[1][:, 16:32], CG(G_BLOCK), gv, True, True)
        for c in range(4):
            r = 64 * (c % 2)
            k = mm(bank[6 + c % 2][:, 8 * (c // 2):8 * (c // 2) + 8], ones[r:r + 64, :], g_[r:r + 64, c // 2, :], True, True,
                   mark=(c == 3), after=[free[6 + c % 2]])
        V(ve.tensor_copy, gc, v3(bank[1][:, 0:16], 2), after=[k])
        V(ve.tensor_tensor, kds, v3(bank[1][:, 16:32], 2), gc, ALU.subtract, after=[V.last])
        A(ac.activation, kds, kds, ACT.Exp, after=[V.last])
        A(ac.activation, egc, gc, ACT.Exp)
        free[1] = V.last
        for c in range(2):
            free[6 + c] = A(ac.activation, dl[:, c::2, :], v3(bank[6 + c][:, 0:16], 2), ACT.Exp)
        V(ve.tensor_tensor, egc, egc, beta, ALU.mult, after=[A.last])
        t_gates = V.last

        def conv(i0, ps, m, tk):
            for j in range(m):
                i = i0 + j
                o = qkv[:, i, :]
                V(ve.tensor_scalar, o, ps[:, j, :], cw[:, 48 + i:49 + i], None, ALU.mult, after=[tk, t_cw])
                for s in (1, 2, 3):
                    V(ve.scalar_tensor_tensor, o[:, s:], ps[:, j, 0:T - s], cw[:, 16 * (3 - s) + i:16 * (3 - s) + i + 1],
                      o[:, s:], ALU.mult, ALU.add, after=[V.last])
            kk = V.last
            A(ac.activation, qkv[:, i0:i0 + m, :], qkv[:, i0:i0 + m, :], ACT.Silu, after=[kk])
            silu_done.append(A.last)
            return kk
        silu_done = []
        wi = p["a_w_in"][0]
        fm_tiles(XT, wi, 0, 16, 128, (2, 3, 4, 5), conv, x_ready)

        def z_evac(t, c, ps, tk):
            return A(ac.activation, Z[:, t, 512 * c:512 * c + 512], ps, ACT.Silu, after=[tk])
        rm_proj(XT, wi, 2048, 1024, (2, 3, 4, 5), z_evac, x_ready)
        t_z = A.last
        for t in range(2):
            V(ve.tensor_tensor, Z[:, t, :].rearrange("p (h e) -> p h e", h=8), Z[:, t, :].rearrange("p (h e) -> p h e", h=8),
              nw.unsqueeze(1).broadcast_to([128, 8, 128]), ALU.mult, after=[t_z])
        sq = v3(take(2 * T), 2)
        mark0 = Stack.at
        t_q = None
        for i in range(0, 8, 2):
            x2 = qkv[:, i:i + 2, :]
            V(ve.tensor_tensor, sq, x2, x2, ALU.mult, after=[silu_done[i // 2], t_q])
            t_q = mm(bank[6 + (i // 2) % 2][:, :], ones, sq.rearrange("p a b -> p (a b)"), True, True, mark=True,
                     after=[V.last, free[6 + (i // 2) % 2]])
            b = bank[6 + (i // 2) % 2]
            V(ve.tensor_scalar, b[:, :], b[:, :], EPS, None, ALU.add, after=[t_q])
            k = A(ac.activation, b[:, :], b[:, :], ACT.Sqrt, after=[V.last])
            V(ve.reciprocal, b[:, :], b[:, :], after=[k])
            free[6 + (i // 2) % 2] = V(ve.scalar_tensor_tensor, x2.rearrange("p a b -> p (a b)"), x2.rearrange("p a b -> p (a b)"),
                                       128.0 ** -0.5 if i < 4 else 1.0, b[:, :], ALU.mult, ALU.mult, after=[V.last])
        t_qk = V.last
        dump("gdn_qkv", qkv, [t_qk, A.last])
        dump("gdn_gc", gc, [t_gates])
        Stack.at = mark0 - 2 * T

        def heads(ap):
            return ap.rearrange("p (h e) -> p h e", e=128)
        AQ, AM, TM, TT = (heads(take(1024)) for _ in range(4))
        KB, KD, VB = (heads(take(1024)) for _ in range(3))
        QD = heads(take(1024))
        B1 = heads(take(512))
        B2 = heads(take(512))
        S = heads(take(1024))
        OT = v3(take(8 * T), 8)
        O = AQ
        small_t = take(32)
        NW = AM
        have_s = False
        t_s = None
        for t in range(2):
            ts = slice(t * 128, (t + 1) * 128)
            pe_prev = PE.last
            v_prev, a_prev = V.last, A.last
            for kh in range(4):
                k = tr(bank[0][:, kh * 128:(kh + 1) * 128], qkv[:, 4 + kh, ts], after=[t_qk, free[0]], mark=(kh == 3))
            free[0] = A(ac.copy, B2, v3(bank[0][:, :], 4), after=[k, v_prev, pe_prev])
            t_kr = A.last
            for h in range(8):
                V(ve.tensor_scalar, KB[:, h, :], B2[:, h // 2, :], egc[:, t, h:h + 1], None, ALU.mult,
                  after=[t_kr, t_gates, pe_prev])
                A(ac.activation, KD[:, h, :], B2[:, h // 2, :], ACT.Copy, scale=kds[:, t, h:h + 1],
                  after=[t_kr, t_gates, pe_prev])
            for hg in range(2):
                for j in range(4):
                    k = tr(bank[1][:, j * 128:(j + 1) * 128], qkv[:, 8 + 4 * hg + j, ts], after=[silu_done, free[1]], mark=(j == 3))
                for j in range(4):
                    h = 4 * hg + j
                    A(ac.activation, VB[:, h, :], bank[1][:, j * 128:(j + 1) * 128], ACT.Copy, scale=beta[:, t, h:h + 1],
                      after=[k, pe_prev, t_beta, v_prev])
                free[1] = A.last
            for kh in range(4):
                kt_ = qkv[:, 4 + kh, ts]
                mm(bank[2][:, kh * 128:(kh + 1) * 128], kt_, kt_, True, True, after=[free[2], free[3], t_qk])
                k = mm(bank[3][:, kh * 128:(kh + 1) * 128], kt_, qkv[:, kh, ts], True, True, mark=(kh == 3))
            t_kk = k
            for hg in range(2):
                hs = slice(4 * hg, 4 * hg + 4)
                b = 4 + hg
                for j in range(4):
                    h = 4 * hg + j
                    V(ve.tensor_scalar, B1[:, j, :], ones, g_[:, t, h:h + 1], None, ALU.mult, after=[PE.last])
                    k = mm(bank[b][:, j * 128:(j + 1) * 128], B1[:, j, :], CG(G_CUM), True, True, after=[V.last, free[b]], mark=True)
                R = v3(bank[b][:, :], 4)
                A(ac.activation, B2, R, ACT.Exp, after=[k, V.last])
                qh = qkv[:, 2 * hg:2 * hg + 2, ts].unsqueeze(2).broadcast_to([128, 2, 2, 128])
                V(ve.tensor_tensor, QD[:, hs, :].rearrange("p (a b) e -> p a b e", b=2), B2.rearrange("p (a b) e -> p a b e", b=2),
                  qh, ALU.mult, after=[A.last, pe_prev])
                t_qd = V.last
                for j in range(4):
                    h = 4 * hg + j
                    V(ve.tensor_scalar, AQ[:, h, :], R[:, j, :], gc[:, t, h:h + 1], 0.0, ALU.subtract, ALU.min, after=[k, pe_prev, a_prev])
                    V(ve.tensor_scalar, AM[:, h, :], R[:, j, :], gc[:, t, h:h + 1], 0.0, ALU.subtract, ALU.max, after=[k, pe_prev])
                free[b] = V.last
                A(ac.activation, AQ[:, hs, :], AQ[:, hs, :], ACT.Exp, after=[V.last])
                t_e1 = A.last
                A(ac.activation, AM[:, hs, :], AM[:, hs, :], ACT.Exp, scale=-1.0, after=[V.last])
                t_e2 = A.last

                def msk(i):
                    return CG(i).unsqueeze(1).broadcast_to([128, 4, 128])
                V(ve.tensor_tensor, AQ[:, hs, :], AQ[:, hs, :], msk(G_CUM), ALU.mult, after=[t_e1])
                V(ve.tensor_tensor, AM[:, hs, :], AM[:, hs, :], msk(G_STRICT), ALU.mult, after=[t_e2])
                kq = v3(bank[3][:, 256 * hg:256 * hg + 256], 2).unsqueeze(2).broadcast_to([128, 2, 2, 128])
                V(ve.tensor_tensor, AQ[:, hs, :].rearrange("p (a b) e -> p a b e", b=2),
                  AQ[:, hs, :].rearrange("p (a b) e -> p a b e", b=2), kq, ALU.mult, after=[V.last, t_kk])
                for j in range(4):
                    h = 4 * hg + j
                    V(ve.scalar_tensor_tensor, AM[:, h, :], bank[2][:, (h // 2) * 128:(h // 2 + 1) * 128], beta[:, t, h:h + 1],
                      AM[:, h, :], ALU.mult, ALU.mult, after=[V.last, t_beta])
            free[2] = free[3] = V.last
            t_a = V.last
            if t == 0:
                dump("gdn_A", AM, [t_a])
                dump("gdn_AQ", AQ, [t_a])
            for lv in range(6):
                for hg in range(2):
                    hs = slice(4 * hg, 4 * hg + 4)
                    bb, b1, b2, b3 = (B1, 2, 3, 4) if hg == 0 else (B2, 5, 6, 7)
                    if lv == 0:
                        V(ve.tensor_tensor, bb, AM[:, hs, :], CG(G_LEVEL).unsqueeze(1).broadcast_to([128, 4, 128]), ALU.mult,
                          after=[t_a, PE.last, A.last])
                        t_b = V.last
                        idb = ident.unsqueeze(1).broadcast_to([128, 4, 128])
                        V(ve.tensor_tensor, TM[:, hs, :], idb, bb, ALU.subtract, after=[t_b])
                        for j in range(4):
                            k = tr(bank[b1][:, j * 128:(j + 1) * 128], bb[:, j, :], after=[t_b, free[b1]], mark=(j == 3))
                        free[b1] = V(ve.tensor_tensor, TT[:, hs, :], idb, v3(bank[b1][:, :], 4), ALU.subtract, after=[k, pe_prev])
                        tt_ready[hg] = V.last
                        b_used[hg] = k
                        continue
                    last = lv == 5
                    t_b = V(ve.tensor_tensor, bb, AM[:, hs, :], CG(G_LEVEL + lv).unsqueeze(1).broadcast_to([128, 4, 128]), ALU.mult,
                            after=[b_used[hg]])
                    for j in range(4):
                        k = mm(bank[b1][:, j * 128:(j + 1) * 128], bb[:, j, :], TT[:, 4 * hg + j, :], True, True,
                               after=[t_b, free[b1], tt_ready[hg]], mark=(j == 3))
                    free[b1] = A(ac.copy, bb, v3(bank[b1][:, :], 4), after=[k])
                    t_m = A.last
                    if not last:
                        for j in range(4):
                            k = mm(bank[b2][:, j * 128:(j + 1) * 128], bb[:, j, :], TM[:, 4 * hg + j, :], True, True,
                                   after=[t_m, free[b2]], mark=(j == 3))
                    for j in range(4):
                        k3 = mm(bank[b3][:, j * 128:(j + 1) * 128], TM[:, 4 * hg + j, :], bb[:, j, :], True, True,
                                after=[t_m, free[b3]], mark=(j == 3))
                    b_used[hg] = k3
                    free[b3] = V(ve.tensor_tensor, TT[:, hs, :], TT[:, hs, :], v3(bank[b3][:, :], 4), ALU.subtract, after=[k3])
                    if not last:
                        free[b2] = V(ve.tensor_tensor, TM[:, hs, :], TM[:, hs, :], v3(bank[b2][:, :], 4), ALU.subtract, after=[k3])
                    tt_ready[hg] = V.last
            for hg in range(2):
                b = (2, 5)[hg]
                for j in range(4):
                    h = 4 * hg + j
                    k = mm(bank[b][:, j * 128:(j + 1) * 128], KB[:, h, :], TT[:, h, :], True, True, after=[tt_ready[hg], free[b]], mark=(j == 3))
                free[b] = A(ac.mul, NW[:, 4 * hg:4 * hg + 4, :], v3(bank[b][:, :], 4), -1.0, after=[k, V.last])
            t_nw = A.last
            if t == 0:
                dump("gdn_TT", TT, [V.last])
            for c in range(2):
                r = 64 * c
                rs = slice(r, r + 64)
                for h in range(8):
                    b = h // 4
                    o = bank[b][rs, (h % 4) * 128:(h % 4 + 1) * 128]
                    mm(o, TT[rs, h, rs], VB[rs, h, :], True, not have_s, after=[free[b], t_nw, t_s])
                    if have_s:
                        mm(o, NW[:, h, rs], S[:, h, :], False, True)
                    PE.q[-1] = PE.q[-1][:4] + (PE.sem, 1)
                    PE.n += 1
                k = PE.last
                V(ve.tensor_copy, VB[rs, 0:4, :], v3(bank[0][rs, :], 4), after=[k])
                A(ac.copy, VB[rs, 4:8, :], v3(bank[1][rs, :], 4), after=[k])
                free[0], free[1] = V.last, A.last
                t_vn = [V.last, A.last]
                for h in range(8):
                    b = 2 + h // 4
                    o = bank[b][rs, (h % 4) * 128:(h % 4 + 1) * 128]
                    if have_s:
                        mm(o, QD[:, h, rs], S[:, h, :], True, False, after=[free[b]])
                        k = mm(o, AQ[rs, h, rs], VB[rs, h, :], False, True, after=[t_vn], mark=(h == 7))
                    else:
                        k = mm(o, AQ[rs, h, rs], VB[rs, h, :], True, True, after=[free[b], t_vn], mark=(h == 7))
                t_o = k
                if not (t == 1 and c == 1):
                    for h in range(8):
                        b = 4 + h // 4
                        k = mm(bank[b][:, (h % 4) * 128:(h % 4 + 1) * 128], KD[rs, h, :], VB[rs, h, :], True, True,
                               after=[free[b], t_vn], mark=(h % 4 == 3))
                        if h % 4 == 3:
                            k_s = k
                            for j in range(4):
                                hh = h - 3 + j
                                s_, ps = S[:, hh, :], bank[b][:, j * 128:(j + 1) * 128]
                                if have_s:
                                    V(ve.scalar_tensor_tensor, s_, s_, dl[:, 2 * t + c, hh:hh + 1], ps, ALU.mult, ALU.add, after=[k_s])
                                else:
                                    V(ve.tensor_copy, s_, ps, after=[k_s])
                            free[b] = V.last
                    t_s = V.last
                    have_s = True
            for hg in range(2):
                A(ac.copy, O[:, 4 * hg:4 * hg + 4, :], v3(bank[2 + hg][:, :], 4), after=[PE.last])
                free[2 + hg] = A.last
            ss, sr = small_t[:, 0:8], small_t[:, 8:16]
            V(ve.tensor_tensor, QD, O, O, ALU.mult, after=[A.last, PE.last])
            V(ve.tensor_reduce, ss, QD, AX_X, ALU.add, after=[V.last])
            V(ve.tensor_scalar, ss, ss, 1.0 / 128, EPS, ALU.mult, ALU.add, after=[V.last])
            A(ac.activation, sr, ss, ACT.Sqrt, after=[V.last])
            V(ve.reciprocal, ss, sr, after=[A.last])
            V(ve.tensor_tensor, O, O, ss.unsqueeze(2).broadcast_to([128, 8, 128]), ALU.mult, after=[V.last])
            V(ve.tensor_tensor, O, O, Z[:, t, :].rearrange("p (h e) -> p h e", h=8), ALU.mult, after=[V.last])
            k0 = V.last
            for g in range(2):
                b = 6 + g
                for j in range(4):
                    k = tr(bank[b][:, j * 128:(j + 1) * 128], O[:, 4 * g + j, :], after=[k0, free[b]], mark=(j == 3))
                free[b] = copy(OT[:, 4 * g:4 * g + 4, ts], v3(bank[b][:, :], 4), after=[k])
        t_ot = [V.last, A.last]
        dump("gdn_o", OT, t_ot)

        def keep(t, c, ps, tk):
            toks[t] = tk
            return None
        toks = [None, None]
        out_proj(OT, p["a_w_out"][0], (0, 1, 2, 3), t_ot)
        done = residual_norm((0, 1, 2, 3), [PE.last] * 2, gb, t_gb, [small_t[:, 0:16], small_t[:, 16:32]])
        return done

    tt_ready, b_used = [None, None], [None, None]

    def log1p(y, u, d, ready):
        V(ve.tensor_scalar, u, y, 1.0, None, ALU.add, after=[ready])
        V(ve.tensor_scalar, d, u, 1.0, 1e-30, ALU.subtract, ALU.add, after=[V.last])
        A(ac.activation, u, u, ACT.Ln, after=[V.last])
        V(ve.reciprocal, d, d, after=[V.last])
        V(ve.tensor_scalar, u, u, 1e-30, None, ALU.add, after=[A.last])
        V(ve.tensor_tensor, u, u, d, ALU.mult, after=[V.last])
        V(ve.tensor_tensor, y, y, u, ALU.mult, after=[V.last])

    def out_proj(ot, w, banks4, ready, kt=8, first=True, last=True, k0=0):
        for g in range(0, kt, 4):
            m = min(4, kt - g)
            (wv,), t_w, slot = load([(m * 1024, 128, (m, 1024), w[g * 128:(g + m) * 128, :].rearrange("(k p) c -> p k c", p=128))])
            for j in range(m):
                for t in range(2):
                    for h in range(2):
                        b = banks4[2 * t + h]
                        mm(bank[b][:, :], ot[:, g + j, t * 128:(t + 1) * 128], wv[:, j, 512 * h:512 * h + 512],
                           first and g + j == 0, last and g + j == kt - 1, after=[t_w, ready, free[b]],
                           mark=(j == m - 1 and t == 1 and h == 1))
            Ring.used[slot] = PE.last

    def ffn(x_ready):
        Stack.at = base
        gb = v3(take(2 * D), 2)
        t_gb = small([(gb[:, 0, :], bcast(p["ln_g"][0, 1], 128)), (gb[:, 1, :], bcast(p["ln_b"][0, 1], 128))],
                     after=[V.last, PE.last, A.last])
        sg = v4(take(4 * T), 2, 2)
        hT = take(2 * 4 * T).rearrange("p (a b c) -> p a b c", a=2, b=4)
        tm = take(32)
        groups = [(512 * i, 4) for i in range(5)] + [(2560, 2)]
        wg, wu, wd = p["ffn_w_gate"][0], p["ffn_w_up"][0], p["ffn_w_down"][0]
        h_ready = [None, None]
        h_used = [None, None]
        A_prev = [None, None]

        def down(gi):
            c0, m = groups[gi]
            (w,), t_w, slot = load([(m * 1024, 128, (m, 1024), wd[c0:c0 + m * 128, :].rearrange("(k p) c -> p k c", p=128))])
            for j in range(m):
                for t in range(2):
                    for h in range(2):
                        b = 2 * t + h
                        k = mm(bank[b][:, :], hT[:, gi % 2, j, t * 128:(t + 1) * 128], w[:, j, 512 * h:512 * h + 512],
                               gi == 0 and j == 0, gi == len(groups) - 1 and j == m - 1,
                               after=[t_w, h_ready[gi % 2], free[b]], mark=(j == m - 1))
            h_used[gi % 2] = k
            Ring.used[slot] = k
        nb = 0
        for gi, (c0, m) in enumerate(groups):
            cols = m * 128
            (g1,), t_w, s1 = load([(8 * cols, 128, (8, cols), wg[:, c0:c0 + cols].rearrange("(k p) c -> p k c", p=128))])
            (u1,), t_u, s2 = load([(8 * cols, 128, (8, cols), wu[:, c0:c0 + cols].rearrange("(k p) c -> p k c", p=128))])
            for j in range(m):
                b = 4 + nb % 4
                for q, (w, tw) in enumerate(((g1, t_w), (u1, t_u))):
                    for k_ in range(8):
                        k = mm(bank[b][:, q * T:(q + 1) * T], w[:, k_, j * 128:(j + 1) * 128], XT[:, k_, :], k_ == 0, k_ == 7,
                               after=[tw, free[b], x_ready], mark=(k_ == 7))
                s_ = sg[:, nb % 2, 0, :]
                A(ac.activation, s_, bank[b][:, 0:T], ACT.Silu, after=[k, A_prev[nb % 2]])
                free[b] = V(ve.tensor_tensor, hT[:, gi % 2, j, :], s_, bank[b][:, T:2 * T], ALU.mult, after=[A.last, h_used[gi % 2]])
                A_prev[nb % 2] = V.last
                nb += 1
            Ring.used[s1] = Ring.used[s2] = PE.last
            h_ready[gi % 2] = V.last
            if gi:
                down(gi - 1)
        down(len(groups) - 1)
        return residual_norm((0, 1, 2, 3), [PE.last] * 2, gb, t_gb, [tm[:, 0:16], tm[:, 16:32]])

    def load_views(cols, rows, shape, parts):
        i = Ring.n % RING
        Ring.n += 1
        dst = ring[0:rows, i, 0:cols].rearrange("p (a b) -> p a b", a=shape[0])
        for cut, src in parts:
            SP.dma(sy.dma_start, cut(dst), src, Ring.s[i], after=[Ring.used[i]])
            Ring.count[i] += 16
        return dst, (Ring.s[i], Ring.count[i]), i

    def swa(x_ready):
        Stack.at = base
        gb = v3(take(2 * D), 2)
        bias = v3(take(16 * T), 16)
        qT = v3(take(8 * T), 8)
        kd = v3(take(2 * T), 2)
        vv = v3(take(2 * 128), 2)
        vb = take(128)
        prow, pc = take(128), take(16)
        oh, em = take(384), take(384)
        sk = take(16)
        st = take(96)
        s_ = take(4096)
        pT = v4(take(8 * 128), 2, 4)
        oT = v3(take(8 * T), 8)
        tm = take(32)
        after = [V.last, PE.last, A.last]
        bi = p["b_b_in"][0]
        t_p = small([(oh[0:32, :], p["c_oh"]), (em[0:16, :], p["c_em"]),
                     (st[0:32, 0:16], p["rel_bias"]),
                     (prow[0:8, :], bi[0:1024].rearrange("(a b) -> a b", b=128)),
                     (prow[8:9, 0:64], bi[1024:1088].unsqueeze(0)), (prow[8:9, 64:128], bi[1024:1088].unsqueeze(0)),
                     (prow[9:10, 0:64], bi[1088:1152].unsqueeze(0)), (prow[9:10, 64:128], bi[1088:1152].unsqueeze(0)),
                     (vb, bcast(bi[1152:1280], 128)), (sk, bcast(p["b_sinks"][0], 128))], after=after)
        t_gb = small([(gb[:, 0, :], bcast(p["ln_g"][1, 0], 128)), (gb[:, 1, :], bcast(p["ln_b"][1, 0], 128))], after=after)
        k = mm(bank[7][0:16, 0:384], st[0:32, 0:16], oh[0:32, :], True, True, after=[t_p, free[7]], mark=True)
        V(ve.tensor_tensor, em[0:16, :], em[0:16, :], bank[7][0:16, 0:384], ALU.add, after=[k])
        free[7] = V.last
        scr = nc.dram_tensor("scr_band", [16, 128, 384], F32, kind="Internal").ap()
        t_w = small([(scr, em[0:16, :].unsqueeze(1).broadcast_to([16, 128, 384]))], after=[V.last])
        band = bass.AP(tensor=scr.tensor, offset=127, ap=[[383, 128], [128 * 384, 16], [1, 256]])
        t_bias = small([(bias, band)], after=[t_w])
        k = tr(bank[6][:, 0:10], prow[0:10, :], after=[t_p, free[6]], mark=True)
        free[6] = V(ve.tensor_copy, pc[:, 0:10], bank[6][:, 0:10], after=[k])
        t_pc = V.last
        w = p["b_w_in"][0]

        def q_evac(i0, ps, m, tk):
            for j in range(m):
                V(ve.tensor_scalar, qT[:, i0 + j, :], ps[:, j, :], pc[:, i0 + j:i0 + j + 1], None, ALU.add, after=[tk, t_pc])
            return V.last
        fm_tiles(XT, w, 0, 8, 128, (0, 1, 2, 3), q_evac, x_ready)
        t_q = V.last
        wr = w[:, :].rearrange("(k p) c -> p k c", p=128)
        wk, t_wk, slot = load_views(3072, 128, (8, 384), [
            (lambda d: d[:, :, 0:64], wr[:, :, 1024:1088]), (lambda d: d[:, :, 64:128], wr[:, :, 1024:1088]),
            (lambda d: d[:, :, 128:192], wr[:, :, 1088:1152]), (lambda d: d[:, :, 192:256], wr[:, :, 1088:1152]),
            (lambda d: d[:, :, 256:384], wr[:, :, 1152:1280])])
        for kv in range(2):
            for kk in range(8):
                k = mm(bank[4][:, kv * T:(kv + 1) * T], wk[:, kk, kv * 128:kv * 128 + 128], XT[:, kk, :], kk == 0, kk == 7,
                       after=[t_wk, free[4]], mark=(kk == 7))
        for kv in range(2):
            V(ve.tensor_scalar, kd[:, kv, :], bank[4][:, kv * T:(kv + 1) * T], pc[:, 8 + kv:9 + kv], None, ALU.add, after=[k])
        free[4] = V.last
        for t in range(2):
            for kk in range(8):
                k = mm(bank[5][:, t * 128:t * 128 + 128], XT[:, kk, t * 128:(t + 1) * 128], wk[:, kk, 256:384], kk == 0, kk == 7,
                       after=[free[5]], mark=(kk == 7))
        V(ve.tensor_tensor, vv, v3(bank[5][:, 0:256], 2), vb.unsqueeze(1).broadcast_to([128, 2, 128]), ALU.add, after=[k])
        Ring.used[slot] = k
        free[5] = t_kv = V.last
        nT = 0
        pt_used = [None, None]
        for n in range(2):
            wd = 128 * (n + 1)
            nh = 512 // wd
            sv = s_[:, 0:16 * wd].rearrange("p (h w) -> p h w", h=16)
            toks = slice(n * 128, n * 128 + 128)
            m, nm, es, sm, rc = (st[:, 16 * i:16 * i + 16] for i in range(5))
            bt = bias[:, :, 256 - wd:256] if n == 0 else bias
            ib = 0
            for g in range(0, 16, 2 * nh):
                for par in range(2):
                    b = ib % 4
                    ib += 1
                    hs = [g + par + 2 * i for i in range(nh)]
                    for i, h in enumerate(hs):
                        k = mm(bank[b][:, i * wd:(i + 1) * wd], qT[64 * par:64 * par + 64, h // 2, toks],
                               kd[64 * par:64 * par + 64, h // 8, 0:wd], True, True, after=[t_q, t_kv, free[b]], mark=(i == nh - 1))
                    hv = slice(g + par, g + par + 2 * nh - 1, 2)
                    free[b] = V(ve.scalar_tensor_tensor, sv[:, hv, :], v3(bank[b][:, :], nh), 0.125, bt[:, hv, :],
                                ALU.mult, ALU.add, after=[k, t_bias, PE.last if n else None])
                V(ve.tensor_reduce, m[:, g:g + 2 * nh], sv[:, g:g + 2 * nh, :], AX_X, ALU.max, after=[V.last])
            V(ve.tensor_tensor, m, m, sk, ALU.max, after=[V.last, t_p])
            V(ve.tensor_scalar, nm, m, -1.0, None, ALU.mult, after=[V.last])
            V(ve.tensor_tensor, es, sk, m, ALU.subtract, after=[V.last])
            t_m = V.last
            A(ac.activation, es, es, ACT.Exp, after=[t_m])
            for h in range(16):
                A(ac.activation, sv[:, h, :], sv[:, h, :], ACT.Exp, bias=nm[:, h:h + 1], accum_out=sm[:, h:h + 1], after=[t_m])
            V(ve.tensor_tensor, rc, sm, es, ALU.add, after=[A.last])
            V(ve.reciprocal, rc, rc, after=[V.last])
            t_r = V.last
            nt = n + 1
            for g in range(0, 16, 4):
                for h in range(g, g + 4):
                    V(ve.tensor_scalar, sv[:, h, :], sv[:, h, :], rc[:, h:h + 1], None, ALU.mult, after=[t_r])
                t_pn = V.last
                ob = 6 + (g // 4) % 2
                for h2 in range(g, g + 4, 4 // nt):
                    b = 4 + nT % 2
                    q = 0
                    for h in range(h2, h2 + 4 // nt):
                        for kt in range(nt):
                            k = tr(bank[b][:, q * 128:(q + 1) * 128], sv[:, h, kt * 128:(kt + 1) * 128], after=[t_pn, free[b]], mark=(q == 3))
                            q += 1
                    free[b] = copy(pT[:, nT % 2, :, :], v3(bank[b][:, :], 4), after=[k, pt_used[nT % 2]])
                    q = 0
                    for h in range(h2, h2 + 4 // nt):
                        for kt in range(nt):
                            o = bank[ob][64 * (h % 2):64 * (h % 2) + 64, ((h - g) // 2) * 128:((h - g) // 2 + 1) * 128]
                            k = mm(o, vv[:, kt, (h // 8) * 64:(h // 8) * 64 + 64], pT[:, nT % 2, q, :], kt == 0, kt == nt - 1,
                                   after=[free[b], free[ob]], mark=(q == 3))
                            q += 1
                    pt_used[nT % 2] = k
                    nT += 1
                free[ob] = copy(oT[:, g // 2:g // 2 + 2, toks], v3(bank[ob][:, 0:256], 2), after=[k])
        t_o = [V.last, A.last]
        dump("swa_o", oT, t_o)
        out_proj(oT, p["b_w_out"][0], (0, 1, 2, 3), t_o)
        return residual_norm((0, 1, 2, 3), [PE.last] * 2, gb, t_gb, [tm[:, 0:16], tm[:, 16:32]])

    def moe(x_ready, x_rows):
        Stack.at = base
        gb = v3(take(2 * D), 2)
        wr = v3(take(64), 8)
        fa = v3(take(2 * D), 2)
        xg = take(2 * 1024).rearrange("p (a k s) -> p a k s", a=2, k=8)
        sg = v3(take(2 * 512), 2)
        hh = v3(take(2 * 512), 2)
        hT = take(2 * 512).rearrange("p (a j s) -> p a j s", a=2, j=4)
        y = take(1024)
        P_ = v4(take(2 * 256), 2, 2)
        PG = v3(take(256), 2)
        PT = v4(take(2 * 256), 2, 2)
        rt = take(256)
        tm = take(32)
        after = [V.last, PE.last, A.last]
        t_r = small([(wr, p["moe_router"][0].rearrange("(k p) e -> p k e", p=128))], after=after)
        t_gb = small([(gb[:, 0, :], bcast(p["ln_g"][1, 1], 128)), (gb[:, 1, :], bcast(p["ln_b"][1, 1], 128))], after=after)
        lg, sel, gate, rank, rank2 = (v3(rt[:, 16 * i:16 * i + 16], 2) for i in range(5))
        mx = v3(rt[:, 80:96], 2)
        ix = v3(rt[:, 96:112], 2)
        ixu = v3(rt[:, 112:128].bitcast(U32), 2)
        g01 = v3(rt[:, 128:132], 2)
        oh = v4(rt[:, 144:176], 2, 2)
        cnt = rt[:, 176:184]
        cm = rt[:, 184:185]
        flag = rt[:, 185:186].bitcast(I32)
        for t in range(2):
            for kk in range(8):
                k = mm(bank[7][:, 8 * t:8 * t + 8], XT[:, kk, t * 128:(t + 1) * 128], wr[:, kk, :], kk == 0, kk == 7,
                       after=[t_r, x_ready, free[7]], mark=(kk == 7))
        free[7] = V(ve.tensor_copy, lg, v3(bank[7][:, 0:16], 2), after=[k])
        for j in range(2):
            for t in range(2):
                V(ve.max, mx[:, t, :], lg[:, t, :], after=[V.last])
                V(ve.max_index, ixu[:, t, :], mx[:, t, :], lg[:, t, :], after=[V.last])
            V(ve.tensor_copy, ix, ixu, after=[V.last])
            V(ve.tensor_copy, g01[:, :, j:j + 1], mx[:, :, 0:1], after=[V.last])
            for t in range(2):
                V(ve.tensor_scalar, oh[:, j, t, :], C(C_IOTA)[:, 0:8], ix[:, t, 0:1], None, ALU.is_equal, after=[V.last])
            if j == 0:
                V(ve.scalar_tensor_tensor, lg, oh[:, 0, :, :], -3.0e38, lg, ALU.mult, ALU.add, after=[V.last])
        V(ve.tensor_tensor, g01[:, :, 1:2], g01[:, :, 1:2], g01[:, :, 0:1], ALU.subtract, after=[V.last])
        A(ac.activation, g01[:, :, 1:2], g01[:, :, 1:2], ACT.Exp, after=[V.last])
        V(ve.tensor_scalar, g01[:, :, 0:1], g01[:, :, 1:2], 1.0, None, ALU.add, after=[A.last])
        V(ve.reciprocal, g01[:, :, 0:1], g01[:, :, 0:1], after=[V.last])
        V(ve.tensor_tensor, g01[:, :, 1:2], g01[:, :, 1:2], g01[:, :, 0:1], ALU.mult, after=[V.last])
        V(ve.tensor_tensor, sel, oh[:, 0, :, :], oh[:, 1, :, :], ALU.add, after=[V.last])
        for t in range(2):
            V(ve.tensor_scalar, gate[:, t, :], oh[:, 0, t, :], g01[:, t, 0:1], None, ALU.mult, after=[V.last])
            V(ve.scalar_tensor_tensor, gate[:, t, :], oh[:, 1, t, :], g01[:, t, 1:2], gate[:, t, :], ALU.mult, ALU.add, after=[V.last])
        t_sel = V.last
        mm(bank[7][:, 0:8], C(C_LT), sel[:, 0, :], True, True, after=[t_sel, free[7]])
        mm(bank[7][:, 8:16], ones, sel[:, 0, :], True, False)
        mm(bank[7][:, 8:16], C(C_LT), sel[:, 1, :], False, True)
        mm(bank[7][:, 16:24], ones, sel[:, 0, :], True, False)
        k = mm(bank[7][:, 16:24], ones, sel[:, 1, :], False, True, mark=True)
        V(ve.tensor_copy, rank, v3(bank[7][:, 0:16], 2), after=[k])
        V(ve.tensor_copy, cnt, bank[7][:, 16:24], after=[k])
        free[7] = V.last
        V(ve.tensor_reduce, cm, cnt, AX_X, ALU.max, after=[V.last])
        V(ve.tensor_scalar, cm, cm, 128.0, None, ALU.is_gt, after=[V.last])
        V(ve.tensor_copy, flag, cm, after=[V.last])
        t_flag = V.last
        V(ve.tensor_scalar, rank2, rank, -128.0, None, ALU.add, after=[V.last])
        t_rank = V.last
        dump("moe_gate", gate, [t_rank])

        def experts(rk, first_pass):
            steps = [(e, g) for e in range(NE) for g in range(7)]
            xg_t, pt_t = [None] * NE, [None] * NE
            hu, tu, xu, pu = [None, None], [None, None], [None, None], [None, None]
            h_t, hT_t = [None] * len(steps), [None] * len(steps)
            yt = [None]

            def prep(e):
                a = e % 2
                for t in range(2):
                    V(ve.tensor_scalar, P_[:, a, t, :], C(C_IOTA), rk[:, t, e:e + 1], sel[:, t, e:e + 1], ALU.is_equal, ALU.mult,
                      after=[t_rank, xu[a]])
                    V(ve.tensor_scalar, PG[:, t, :], C(C_IOTA), rk[:, t, e:e + 1], gate[:, t, e:e + 1], ALU.is_equal, ALU.mult,
                      after=[t_rank, PE.last])
                t_P = V.last
                for half in range(2):
                    for j in range(4):
                        kk = 4 * half + j
                        for t in range(2):
                            k = mm(bank[7][:, j * 128:(j + 1) * 128], X[:, t, kk * 128:(kk + 1) * 128], P_[:, a, t, :], t == 0, t == 1,
                                   after=[t_P, free[7], x_rows], mark=(j == 3 and t == 1))
                    free[7] = A(ac.copy, xg[:, a, 4 * half:4 * half + 4, :], v3(bank[7][:, :], 4), after=[k, xu[a]])
                xg_t[e] = A.last
                for t in range(2):
                    k = tr(bank[7][:, t * 128:(t + 1) * 128], PG[:, t, :], after=[t_P, free[7]], mark=(t == 1))
                free[7] = A(ac.copy, PT[:, a, :, :], v3(bank[7][:, 0:256], 2), after=[k, pu[a]])
                pt_t[e] = A.last

            def gate_up(n):
                e, g = steps[n]
                a = e % 2
                ws = []
                for name in ("moe_w_gate", "moe_w_up"):
                    (w,), t_w, slot = load([(4096, 128, (8, 512), p[name][0, e][:, 512 * g:512 * g + 512].rearrange("(k p) c -> p k c", p=128))])
                    ws.append((w, t_w, slot))
                bb = 2 * (n % 2)
                for q, (w, t_w, slot) in enumerate(ws):
                    for kk in range(8):
                        k = mm(bank[bb + q][:, :], xg[:, a, kk, :], w[:, kk, :], kk == 0, kk == 7,
                               after=[t_w, xg_t[e], free[bb + q]], mark=(kk == 7))
                    Ring.used[slot] = k
                    if q == 0:
                        free[bb] = A(ac.activation, sg[:, n % 2, :], bank[bb][:, :], ACT.Silu, after=[k, h_t[n - 2] if n > 1 else None])
                xu[a] = k
                free[bb + 1] = V(ve.tensor_tensor, hh[:, n % 2, :], sg[:, n % 2, :], bank[bb + 1][:, :], ALU.mult, after=[A.last, k, hu[n % 2]])
                h_t[n] = V.last

            def turn(n):
                for j in range(4):
                    k = tr(bank[6][:, j * 128:(j + 1) * 128], hh[:, n % 2, j * 128:(j + 1) * 128], after=[h_t[n], free[6]], mark=(j == 3))
                hu[n % 2] = k
                free[6] = A(ac.copy, hT[:, n % 2, :, :], v3(bank[6][:, :], 4), after=[k, tu[n % 2]])
                hT_t[n] = A.last

            def down(n):
                e, g = steps[n]
                (w,), t_w, slot = load([(4096, 128, (4, 1024), p["moe_w_down"][0, e][512 * g:512 * g + 512, :].rearrange("(k p) c -> p k c", p=128))])
                for j in range(4):
                    for h in range(2):
                        k = mm(bank[4 + h][:, :], hT[:, n % 2, j, :], w[:, j, 512 * h:512 * h + 512], g == 0 and j == 0, g == 6 and j == 3,
                               after=[t_w, hT_t[n], free[4 + h]], mark=(j == 3))
                Ring.used[slot] = tu[n % 2] = k
                if g == 6:
                    free[4] = V(ve.tensor_copy, y[:, 0:512], bank[4][:, :], after=[k, yt[0]])
                    free[5] = A(ac.copy, y[:, 512:1024], bank[5][:, :], after=[k, yt[0]])

            def scatter(e):
                t_y = [free[4], free[5]]
                for t in range(2):
                    for h in range(2):
                        b = 6 + h
                        k = mm(bank[b][:, :], PT[:, e % 2, t, :], y[:, 512 * h:512 * h + 512], True, True,
                               after=[t_y, free[b], pt_t[e]], mark=True)
                        o = fa[:, t, 512 * h:512 * h + 512]
                        if first_pass and e == 0:
                            free[b] = V(ve.tensor_copy, o, bank[b][:, :], after=[k])
                        else:
                            free[b] = V(ve.tensor_tensor, o, o, bank[b][:, :], ALU.add, after=[k])
                yt[0] = pu[e % 2] = k

            prep(0)
            N = len(steps)
            for n in range(N + 3):
                if n < N:
                    gate_up(n)
                    if steps[n][1] == 4 and steps[n][0] + 1 < NE:
                        prep(steps[n][0] + 1)
                if 1 <= n <= N:
                    turn(n - 1)
                if 2 <= n <= N + 1:
                    down(n - 2)
                if n >= 3 and steps[n - 3][1] == 6:
                    scatter(steps[n - 3][0])
            return V.last

        experts(rank, True)

        saved = (list(free), list(Ring.used), list(Ring.count), Ring.n, Ring.s)
        before = [q.last for q in (PE, V, A)]
        outer = {}
        for nm, q in queues.items():
            q.wait(t_flag)
            outer[nm] = (q.sem, q.n, q.q, dict(q.seen))
            q.wait(before)
            q.sem, q.n, q.q = sem("o_" + nm), 0, []
        for nm, q in queues.items():
            q.wait([b for b in before])
        Ring.s, Ring.count, Ring.n = [sem(f"o_ring{i}") for i in range(RING)], [0] * RING, 0
        for b in range(8):
            free[b] = list(before)
        Ring.used[:] = [before[0]] * RING
        experts(rank2, False)
        ends = [q.last for q in queues.values() if q.n]
        for nm, q in queues.items():
            q.wait(ends)
            sub = q.q
            q.sem, q.n, q.q, q.seen = outer[nm]
            for w_ in before:
                q.wait(w_)
            q.q.append(("if", flag[0:1, :], sub))
        free[:], Ring.used[:], Ring.count[:] = saved[0], saved[1], saved[2]
        Ring.n, Ring.s = saved[3], saved[4]

        done = []
        for t in range(2):
            V(ve.scalar_tensor_tensor, X[:, t, :], X[:, t, :], ALPHA, fa[:, t, :], ALU.mult, ALU.add, after=[V.last, PE.last])
            done.append(norm_rows(X, X[:, t, :], t, gb, t_gb, tm[:, 16 * t:16 * t + 16], V.last))
        return done

    O_Q, O_K, O_V, O_GA, O_IQ, O_IK, O_IW, O_XR, O_GR, O_MA, O_MB = 0, 1024, 2048, 3072, 4096, 5120, 5184, 5200, 6608, 8016, 9040

    def rms_rows(o, t, g, t_g, tmp, sq, ready):
        A(ac.activation, sq, X[:, t, :], ACT.Square, accum_out=tmp[:, 0:1], after=[ready, V.last, PE.last])
        V(ve.tensor_scalar, tmp[:, 1:2], tmp[:, 0:1], 1.0 / D, EPS, ALU.mult, ALU.add, after=[A.last])
        A(ac.activation, tmp[:, 2:3], tmp[:, 1:2], ACT.Sqrt, after=[V.last])
        V(ve.reciprocal, tmp[:, 3:4], tmp[:, 2:3], after=[A.last])
        return V(ve.scalar_tensor_tensor, o, X[:, t, :], tmp[:, 3:4], g, ALU.mult, ALU.mult, after=[V.last, t_g])

    class B2:
        rot_used = [None, None]

    def second_setup():
        Stack.at = base
        B2.cosA, B2.sinA, B2.cosI, B2.sinI = (take(T) for _ in range(4))
        B2.prm = take(256)
        B2.keep = take(384)
        B2.tm = take(32)
        B2.base = Stack.at
        pos = take(T)
        an, kr, rr = take(T), take(T), take(T)
        cr = take(4)
        pr = take(2 * 88)
        u, d = take(32), take(32)
        after = [V.last, PE.last, A.last]
        t_p = small([(pos.bitcast(I32), bcast(p["positions_2"][0], 128)), (cr, p["c_rope"]),
                     (pr[:, 0:88], p["conv_w_2"].rearrange("l j (n c) -> (l j n) c", c=88)),
                     (pr[0:32, 88:176], p["conv_b_2"].rearrange("l (n c) -> (l n) c", c=88)),
                     (pr[32:64, 88:176], p["b_rg_2"].rearrange("l (n c) -> (l n) c", c=88)),
                     (pr[64:96, 88:176], p["b_ig_2"].rearrange("l (n c) -> (l n) c", c=88)),
                     (pr[96:128, 88:176], p["lru_lambda_2"].rearrange("l (n c) -> (l n) c", c=88))], after=after)
        for i in range(2):
            k = tr(bank[7][0:88, 128 * i:128 * i + 128], pr[:, 88 * i:88 * i + 88], after=[t_p, free[7]], mark=True)
        free[7] = V(ve.tensor_copy, B2.prm[0:88, :], bank[7][0:88, 0:256], after=[k])
        lam = B2.prm[0:88, 224:256]
        u, d = u[0:88, :], d[0:88, :]
        m = kr[0:88, 0:32]
        V(ve.tensor_scalar, u, lam, -1.0, None, ALU.mult, after=[V.last])
        V(ve.tensor_scalar, m, u, 0.0, None, ALU.max, after=[V.last])
        V(ve.tensor_tensor, lam, lam, u, ALU.min, after=[V.last])
        A(ac.activation, lam, lam, ACT.Exp, after=[V.last])
        log1p(lam, u, d, A.last)
        V(ve.tensor_tensor, lam, lam, m, ALU.add, after=[V.last])
        V(ve.tensor_scalar, lam, lam, -8.0, None, ALU.mult, after=[V.last])
        V(ve.tensor_copy, pos, pos.bitcast(I32), after=[V.last])
        magic = 12582912.0
        for i, (co, si) in enumerate(((B2.cosA, B2.sinA), (B2.cosI, B2.sinI))):
            V(ve.tensor_scalar, an, pos, cr[:, i:i + 1], None, ALU.mult, after=[V.last, A.last])
            V(ve.tensor_scalar, kr, an, 0.15915494309189535, magic, ALU.mult, ALU.add, after=[V.last])
            V(ve.tensor_scalar, kr, kr, magic, None, ALU.subtract, after=[V.last])
            for c in (6.28125, 0.0019350051879882812, 3.01991598196e-07):
                V(ve.scalar_tensor_tensor, an, kr, -c, an, ALU.mult, ALU.add, after=[V.last])
            V(ve.tensor_scalar, an, an, 3.1415925, -3.1415925, ALU.min, ALU.max, after=[V.last])
            A(ac.activation, si, an, ACT.Sin, after=[V.last])
            V(ve.tensor_scalar, rr, an, -1.0, None, ALU.mult, after=[V.last, A.last])
            V(ve.tensor_tensor, rr, rr, an, ALU.min, after=[V.last])
            V(ve.tensor_scalar, rr, rr, cr[:, 2:3], None, ALU.add, after=[V.last])
            A(ac.activation, co, rr, ACT.Sin, after=[V.last])
        return [V.last, A.last]

    def second(l, x_rows, t_tab):
        Stack.at = B2.base
        KT, QT = v3(take(8 * T), 8), v3(take(8 * T), 8)
        VV = v3(take(2 * D), 2)
        GA = v3(take(8 * T), 8)
        GR = take(11 * T)
        Stack_rnn = Stack.at
        IQ = v3(take(8 * T), 8)
        IK = take(T)
        iw = take(32)
        g_row = take(D)
        Stack_rl = Stack.at
        rl = v3(take(2 * 512), 2)
        s0, s1 = take(128), take(256)
        m8 = v3(take(16), 2)
        Stack.at = max(Stack.at, Stack_rnn + 5 * 1024)
        sx = v3(take(4 * 512), 4)
        rt_ = v3(take(2 * 512), 2)
        st = take(64)
        H = VV
        w = p["w_in_2"][l]
        wv = w[:, :].rearrange("(k p) c -> p k c", p=128)
        after = [V.last, PE.last, A.last]
        t_g = small([(g_row, bcast(p["norm_g_2"][l], 128))], after=after)
        hr = []
        for t in range(2):
            hr.append(rms_rows(H[:, t, :], t, g_row, t_g, B2.tm[:, 8 * t:8 * t + 8], GA[:, 0:4, :].rearrange("p a b -> p (a b)"), x_rows))
        x_ready = rows_to_cols(H, XT, hr)

        def rope(Xt, n, cos, sin, rotc, ready):
            for i in range(0, n, 2):
                m = min(2, n - i)
                b = 6 + (i // 2) % 2
                x2 = Xt[:, i:i + m, :]
                k = mm(bank[b][:, 0:m * T], rotc, x2.rearrange("p a b -> p (a b)"), True, True, after=[ready, free[b]], mark=True)
                r_ = rt_[:, (i // 2) % 2, 0:m * T].rearrange("p (a b) -> p a b", a=m)
                V(ve.tensor_tensor, r_, bank[b][:, 0:m * T].rearrange("p (a b) -> p a b", a=m), sin.unsqueeze(1).broadcast_to([128, m, T]),
                  ALU.mult, after=[k, t_tab, B2.rot_used[(i // 2) % 2]])
                free[b] = V.last
                V(ve.tensor_tensor, x2, x2, cos.unsqueeze(1).broadcast_to([128, m, T]), ALU.mult, after=[k, ready])
                B2.rot_used[(i // 2) % 2] = V(ve.tensor_tensor, x2, x2, r_, ALU.add, after=[V.last])
            return V.last

        wk, t_wk, slot = load_views(8 * 144, 128, (8, 144), [
            (lambda d: d[:, :, 0:64], wv[:, :, O_IK:O_IK + 64]), (lambda d: d[:, :, 64:128], wv[:, :, O_IK:O_IK + 64]),
            (lambda d: d[:, :, 128:144], wv[:, :, O_IW:O_IW + 16])])
        for kk in range(8):
            k = mm(bank[0][:, 0:T], wk[:, kk, 0:128], XT[:, kk, :], kk == 0, kk == 7, after=[t_wk, free[0], x_ready])
        for t in range(2):
            for kk in range(8):
                k = mm(bank[0][:, T + 16 * t:T + 16 * t + 16], XT[:, kk, t * 128:(t + 1) * 128], wk[:, kk, 128:144], kk == 0, kk == 7, mark=(kk == 7))
        Ring.used[slot] = k
        A(ac.copy, IK, bank[0][:, 0:T], after=[k])
        free[0] = A(ac.mul, iw, bank[0][:, T:T + 32], 0.03125)

        def to(dst):
            def f(i0, ps, m, tk):
                return A(ac.copy, dst[:, i0:i0 + m, :], ps, after=[tk])
            return f
        fm_tiles(XT, w, O_IQ, 8, 128, (0, 1, 2, 3), to(IQ), x_ready)
        t_iq = A.last
        rope(IK.unsqueeze(1), 1, B2.cosI, B2.sinI, C(C_ROTI), t_iq)
        t_iq = rope(IQ, 8, B2.cosI, B2.sinI, C(C_ROTI), t_iq)
        iwv = v3(iw, 2)
        ru = [None, None]
        nr = 0
        for n, sc in ((0, s0), (1, s1)):
            wd = 128 * (n + 1)
            nh = 512 // wd
            first = True
            for g in range(0, 16, 2 * nh):
                for par in range(2):
                    b = 4 + nr % 2
                    hs = [g + par + 2 * i for i in range(nh)]
                    for i, h in enumerate(hs):
                        k = mm(bank[b][:, i * wd:(i + 1) * wd], IQ[64 * par:64 * par + 64, h // 2, n * 128:n * 128 + 128],
                               IK[64 * par:64 * par + 64, 0:wd], True, True, after=[t_iq, free[b]], mark=(i == nh - 1))
                    free[b] = A(ac.activation, rl[:, nr % 2, :], bank[b][:, :], ACT.Relu, after=[k, ru[nr % 2]])
                    for i, h in enumerate(hs):
                        src = rl[:, nr % 2, i * wd:(i + 1) * wd]
                        if first:
                            V(ve.tensor_scalar, sc, src, iwv[:, n, h:h + 1], None, ALU.mult, after=[free[b]])
                            first = False
                        else:
                            V(ve.scalar_tensor_tensor, sc, src, iwv[:, n, h:h + 1], sc, ALU.mult, ALU.add, after=[free[b], V.last])
                    ru[nr % 2] = V.last
                    nr += 1
        tril = C(C_TRIL)
        keep = (B2.keep[:, 0:128], B2.keep[:, 128:384])
        bg = rl[:, 0, 0:128]
        V(ve.tensor_scalar, bg, tril, 1.0, 1.0e38, ALU.subtract, ALU.mult, after=[V.last])
        for sc in (s0, s1[:, 128:256]):
            V(ve.tensor_tensor, sc, sc, tril, ALU.mult, after=[V.last])
            V(ve.tensor_tensor, sc, sc, bg, ALU.add, after=[V.last])
        tv = [V.last, V.last]
        for r in range(8):
            for n, sc in ((0, s0), (1, s1)):
                tv[n] = V(ve.max, m8[:, n, :], sc, after=[tv[n]])
            for n, sc in ((0, s0), (1, s1)):
                tv[n] = V(ve.match_replace, sc, m8[:, n, :], sc, -3.0e38, after=[tv[n]])
        for n, sc in ((0, s0), (1, s1)):
            V(ve.tensor_scalar, sc, sc, -2.0e38, None, ALU.is_lt, after=[tv[n]])
            c_ = sc[:, 128 * n:128 * n + 128]
            V(ve.tensor_tensor, c_, c_, tril, ALU.mult, after=[V.last])
            V(ve.tensor_scalar, keep[n], sc, 1.0, -NEG, ALU.subtract, ALU.mult, after=[V.last])
        t_keep = V.last
        dump("keep", B2.keep, [t_keep])
        fm_tiles(XT, w, O_Q, 8, 128, (0, 1, 2, 3), to(QT), x_ready)
        fm_tiles(XT, w, O_K, 8, 128, (0, 1, 2, 3), to(KT), x_ready)
        t_qk = A.last
        t_qk = [rope(QT, 8, B2.cosA, B2.sinA, C(C_ROTA), t_qk), rope(KT, 8, B2.cosA, B2.sinA, C(C_ROTA), t_qk)]
        t_hfree = x_ready

        def v_evac(t, c, ps, tk):
            return A(ac.copy, VV[:, t, 512 * c:512 * c + 512], ps, after=[tk, t_hfree])
        rm_proj(XT, w, O_V, 1024, (0, 1, 2, 3), v_evac, x_ready)
        t_v = A.last
        GRv = v3(GR, 11)
        xr_d = nc.dram_tensor(f"scr_xr{l}", [1408, T], F32, kind="Internal").ap()
        hr_d = nc.dram_tensor(f"scr_hr{l}", [1408, T], F32, kind="Internal").ap()
        fm_tiles(XT, w, O_XR, 11, 128, (0, 1, 2, 3), to(GRv), x_ready)
        t_xr = small([(xr_d.rearrange("(i p) t -> p i t", p=128), GRv)], after=[A.last])

        def silu_to(dst, extra=None):
            def f(i0, ps, m, tk):
                return A(ac.activation, dst[:, i0:i0 + m, :], ps, ACT.Silu, after=[tk, extra])
            return f
        fm_tiles(XT, w, O_GA, 8, 128, (0, 1, 2, 3), silu_to(GA), x_ready)
        t_ga = A.last
        fm_tiles(XT, w, O_GR, 11, 128, (0, 1, 2, 3), silu_to(GRv, [t_xr]), x_ready)
        t_gr = A.last

        scale = 128.0 ** -0.5
        nu = 0
        sx_used, pt_used = [None] * 2, [None] * 2
        pTb = sx[:, 2:4, :]
        for n in range(2):
            wd, nt = 128 * (n + 1), n + 1
            nh = 512 // wd
            toks = slice(n * 128, n * 128 + 128)
            for g in range(0, 8, nh):
                a = nu % 2
                b, b2, ob = a, 2 + a, 4 + a
                nu += 1
                m, nm, sm = (st[:, 16 * a + 4 * i:16 * a + 4 * i + nh] for i in range(3))
                for i in range(nh):
                    k = mm(bank[b][:, i * wd:(i + 1) * wd], QT[:, g + i, toks], KT[:, g + i, 0:wd], True, True,
                           after=[t_qk, free[b]], mark=(i == nh - 1))
                sv = sx[:, a, :].rearrange("p (h w) -> p h w", h=nh)
                free[b] = V(ve.scalar_tensor_tensor, sv, v3(bank[b][:, :], nh), scale,
                            keep[n].unsqueeze(1).broadcast_to([128, nh, wd]), ALU.mult, ALU.add, after=[k, t_keep, sx_used[a]])
                V(ve.tensor_reduce, m, sv, AX_X, ALU.max, after=[V.last])
                V(ve.tensor_scalar, nm, m, -1.0, None, ALU.mult, after=[V.last])
                t_m = V.last
                for i in range(nh):
                    A(ac.activation, sv[:, i, :], sv[:, i, :], ACT.Exp, bias=nm[:, i:i + 1], accum_out=sm[:, i:i + 1], after=[t_m])
                V(ve.reciprocal, sm, sm, after=[A.last])
                t_r = V.last
                for i in range(nh):
                    V(ve.tensor_scalar, sv[:, i, :], sv[:, i, :], sm[:, i:i + 1], None, ALU.mult, after=[t_r])
                for q in range(4):
                    k = tr(bank[b2][:, q * 128:(q + 1) * 128], sx[:, a, q * 128:(q + 1) * 128], after=[V.last, free[b2]], mark=(q == 3))
                sx_used[a] = k
                free[b2] = A(ac.copy, pTb[:, a, :], bank[b2][:, :], after=[k, pt_used[a]])
                for i in range(nh):
                    for kt in range(nt):
                        q = i * nt + kt
                        k = mm(bank[ob][:, i * 128:(i + 1) * 128], VV[:, kt, (g + i) * 128:(g + i + 1) * 128],
                               pTb[:, a, q * 128:(q + 1) * 128], kt == 0, kt == nt - 1, after=[free[b2], free[ob], t_v], mark=(q == 3))
                pt_used[a] = k
                free[ob] = V(ve.tensor_tensor, GA[:, g:g + nh, toks], GA[:, g:g + nh, toks], v3(bank[ob][:, 0:nh * 128], nh), ALU.mult,
                             after=[k, t_ga])
        t_at = V.last
        dump("attn", GA, [t_at])
        YA, YB, MG = QT, VV.rearrange("p a b -> p (a b)").rearrange("p (a b) -> p a b", a=8), KT
        fm_tiles(GA, p["w_out_attn_2"][l], 0, 8, 128, (0, 1, 2, 3), to(YA), t_at)
        t_ya = A.last

        end = Stack.at
        Stack.at = Stack_rnn
        XC, RR, II, AA, TH = (v3(take(1024)[0:88, :], 4) for _ in range(5))
        Stack.at = end
        i_ = Ring.n % RING
        Ring.n += 1
        xs = ring[0:88, i_, :].rearrange("p (a b) -> p a b", a=16)
        SP.dma(sy.dma_start, xs, xr_d.rearrange("(n c) t -> c n t", c=88), Ring.s[i_], after=[Ring.used[i_], t_xr])
        Ring.count[i_] += 16
        t_xs = (Ring.s[i_], Ring.count[i_])
        wrg, t_wrg, wslot = load_views(2816, 88, (32, 88), [
            (lambda d: d[:, 0:16, :], p["w_rg_2"][l].rearrange("n c d -> c n d")),
            (lambda d: d[:, 16:32, :], p["w_ig_2"][l].rearrange("n c d -> c n d"))])
        prm = B2.prm[0:88, :]
        outs = []
        for g in range(4):
            t0 = [V.last, A.last, PE.last] if g == 0 else [outs[-1]]
            for j in range(4):
                n = 4 * g + j
                V(ve.tensor_scalar, XC[:, j, :], xs[:, n, :], prm[:, 64 * l + 48 + n:64 * l + 49 + n],
                  prm[:, 128 + 16 * l + n:129 + 16 * l + n], ALU.mult, ALU.add, after=[t_xs, t0])
            for s in (1, 2, 3):
                for j in range(4):
                    n = 4 * g + j
                    cidx = 64 * l + 16 * (3 - s) + n
                    V(ve.scalar_tensor_tensor, XC[:, j, s:], xs[:, n, 0:T - s], prm[:, cidx:cidx + 1], XC[:, j, s:],
                      ALU.mult, ALU.add, after=[V.last])
            t_xc = V.last
            for q, dst in ((0, RR), (1, II)):
                for h in range(2):
                    b = 4 + h + 2 * q
                    for j in (0, 1):
                        n = 4 * g + 2 * h + j
                        k = mm(bank[b][0:88, j * T:(j + 1) * T], wrg[:, 16 * q + n, :], XC[:, 2 * h + j, :], True, True,
                               after=[t_wrg, t_xc, free[b]], mark=(j == 1))
                    for j in (0, 1):
                        n = 4 * g + 2 * h + j
                        c0 = 128 + 32 * (q + 1) + 16 * l + n
                        free[b] = A(ac.activation, dst[:, 2 * h + j, :], bank[b][0:88, j * T:(j + 1) * T], ACT.Sigmoid,
                                    bias=prm[:, c0:c0 + 1], after=[k, t0])
            t_si = A.last
            for j in range(4):
                n = 4 * g + j
                c0 = 224 + 16 * l + n
                A(ac.activation, AA[:, j, :], RR[:, j, :], ACT.Exp, scale=prm[:, c0:c0 + 1], after=[t_si, t0])
                A(ac.activation, TH[:, j, :], RR[:, j, :], ACT.Tanh, scale=prm[:, c0:c0 + 1], after=[t_si, t0])
            V(ve.tensor_tensor, II, II, XC, ALU.mult, after=[t_si])
            V(ve.tensor_scalar, RR, TH, -1.0, 1.0, ALU.mult, ALU.add, after=[A.last])
            V(ve.reciprocal, RR, RR, after=[V.last])
            V(ve.scalar_tensor_tensor, TH, TH, -2.0, RR, ALU.mult, ALU.mult, after=[V.last])
            A(ac.activation, TH, TH, ACT.Sqrt, after=[V.last])
            V(ve.tensor_tensor, II, II, TH, ALU.mult, after=[A.last])
            t_u = V.last
            for j in range(4):
                V(ve.tensor_tensor_scan, XC[:, j, :], AA[:, j, :], II[:, j, :], 0.0, ALU.mult, ALU.add, after=[t_u])
            outs.append(small([(hr_d.rearrange("(n c) t -> c n t", c=88)[:, 4 * g:4 * g + 4, :], XC)], after=[V.last]))
        Ring.used[i_] = V.last
        Ring.used[wslot] = PE.last
        i_ = Ring.n % RING
        Ring.n += 1
        hv = ring[:, i_, 0:11 * T].rearrange("p (a b) -> p a b", a=11)
        SP.dma(sy.dma_start, hv, hr_d.rearrange("(i p) t -> p i t", p=128), Ring.s[i_], after=[Ring.used[i_], outs])
        Ring.count[i_] += 16
        t_hr = (Ring.s[i_], Ring.count[i_])
        V(ve.tensor_tensor, GRv, GRv, hv, ALU.mult, after=[t_hr, t_gr])
        Ring.used[i_] = V.last
        t_rn = V.last
        dump("rnn", GRv, [t_rn])
        fm_tiles(GRv, p["w_out_rnn_2"][l], 0, 8, 128, (0, 1, 2, 3), to(YB), t_rn, per=2, kt=11)
        t_yb = A.last
        sgm = sx[:, 0:2, :]
        su = [None, None]
        ctr = [0]

        def gate_a(i0, ps, m, tk):
            a = ctr[0] % 2
            ctr[0] += 1
            r = A(ac.activation, sgm[:, a, :], ps, ACT.Sigmoid, after=[tk, su[a]])
            V(ve.tensor_tensor, MG[:, i0:i0 + m, :], v3(sgm[:, a, :], 2), YA[:, i0:i0 + m, :], ALU.mult, after=[r, t_ya])
            su[a] = V.last
            return r

        def gate_b(i0, ps, m, tk):
            a = ctr[0] % 2
            ctr[0] += 1
            r = A(ac.activation, sgm[:, a, :], ps, ACT.Sigmoid, after=[tk, su[a]])
            V(ve.tensor_tensor, v3(sgm[:, a, :], 2), v3(sgm[:, a, :], 2), YB[:, i0:i0 + m, :], ALU.mult, after=[r, t_yb])
            V(ve.tensor_tensor, MG[:, i0:i0 + m, :], MG[:, i0:i0 + m, :], v3(sgm[:, a, :], 2), ALU.add, after=[V.last])
            su[a] = V.last
            return r
        fm_tiles(XT, w, O_MA, 8, 128, (0, 1, 2, 3), gate_a, x_ready)
        fm_tiles(XT, w, O_MB, 8, 128, (0, 1, 2, 3), gate_b, x_ready)
        out_proj(MG, p["w_o_2"][l], (4, 5, 6, 7), V.last)
        done = []
        for t in range(2):
            for h in range(2):
                b = 4 + 2 * t + h
                xs_ = X[:, t, 512 * h:512 * h + 512]
                free[b] = V(ve.tensor_tensor, xs_, xs_, bank[b][:, :], ALU.add, after=[PE.last])
            done.append(V.last)
        return done

    done = gdn(t_xt)
    dump("x_a", X, done)
    if stop >= 2:
        t_xt = rows_to_cols(X, XT, done)
        done = ffn(t_xt)
        dump("x_b", X, done)
    if stop >= 3:
        t_xt = rows_to_cols(X, XT, done)
        done = swa(t_xt)
        dump("x_c", X, done)
    if stop >= 4:
        t_xt = rows_to_cols(X, XT, done)
        done = moe(t_xt, done)
        dump("x_d", X, done)
    if stop >= 5:
        t_tab = second_setup()
        done = second(0, done, t_tab)
        dump("x_e", X, done)
    if stop >= 6:
        done = second(1, done, t_tab)
        Stack.at = B2.base
        g_row = take(D)
        sq = take(D)
        t_g = small([(g_row, bcast(p["final_g_2"], 128))], after=[V.last, PE.last, A.last])
        done = [rms_rows(X[:, t, :], t, g_row, t_g, B2.tm[:, 8 * t:8 * t + 8], sq, done) for t in range(2)]

    ov = out.rearrange("o (a p) d -> p (o a) d", p=128)
    t_out = small([(ov, X)], after=done, q=SP, name="s_out")
    SP.wait(t_out)

    with nc.Block() as block:
        @block.sync
        def _(e):
            emit(e, SP.q)

        @block.gpsimd
        def _(e):
            emit(e, G.q)

        @block.tensor
        def _(e):
            emit(e, PE.q)

        @block.scalar
        def _(e):
            emit(e, A.q)

        @block.vector
        def _(e):
            emit(e, V.q)


_INS = ['x', 'a_w_in', 'a_conv_w', 'a_a_log', 'a_dt_bias', 'a_norm_w', 'a_w_out', 'b_w_in', 'b_b_in', 'b_sinks',
        'b_w_out', 'rel_bias', 'ffn_w_gate', 'ffn_w_up', 'ffn_w_down', 'moe_router', 'moe_w_gate', 'moe_w_up',
        'moe_w_down', 'ln_g', 'ln_b', 'positions_2', 'norm_g_2', 'w_in_2', 'conv_w_2', 'conv_b_2', 'w_rg_2', 'b_rg_2',
        'w_ig_2', 'b_ig_2', 'lru_lambda_2', 'w_out_attn_2', 'w_out_rnn_2', 'w_o_2', 'final_g_2']

_BUCKET = [b for b, n in enumerate(
    [1, 1, 1, 1, 1, 1, 1, 1, 1, 1, 1, 1, 1, 1, 1, 1, 3, 2, 3, 3, 4, 4, 5, 6, 6, 7, 8, 10, 10, 12, 14, 15]) for _ in range(n)]


def constants():
    import numpy as np
    i = np.arange(128)
    f = np.float32
    col, row = i[None, :], i[:, None]
    eye = (row == col).astype(f)

    def rot(n):
        m = np.zeros((128, 128), f)
        for o in range(128):
            b, r = o // n * n, o % n
            if r < n // 2:
                m[b + r + n // 2, o] = -1.0
            else:
                m[b + r - n // 2, o] = 1.0
        return m
    main = [eye, np.ones((128, 128), f), rot(128), rot(64), (col <= row).astype(f), (row < col).astype(f),
            np.broadcast_to(col, (128, 128)).astype(f)]
    same = (row // 64 == col // 64)
    gdn = [(same & (row <= col)).astype(f), (same & (row > col)).astype(f), same.astype(f)]
    for lv in range(6):
        gdn.append(((row >> (lv + 1) == col >> (lv + 1)) & ((row >> lv) % 2 == 1) & ((col >> lv) % 2 == 0)).astype(f))
    oh = np.zeros((32, 384), f)
    em = np.full((16, 384), NEG, f)
    for y in range(128, 256):
        oh[_BUCKET[255 - y], y] = 1.0
        em[:, y] = 0.0
    ia = f(10000.0) ** (-np.arange(0, 128, 2, dtype=f) / f(128))
    ii = f(10000.0) ** (-np.arange(0, 64, 2, dtype=f) / f(64))
    rope = np.stack([np.tile(ia, 2), np.tile(ii, 4), np.full(128, np.pi / 2, f), np.zeros(128, f)], 1).astype(f)
    return {"c_main": np.concatenate(main, 1), "c_gdn": np.concatenate(gdn, 1), "c_oh": oh, "c_em": em, "c_rope": rope}


_CONSTS = ["c_main", "c_gdn", "c_oh", "c_em", "c_rope"]


def kernel(**inputs):
    import numpy as _np
    import concourse.bacc as _bacc
    from concourse import mybir as _mybir
    from concourse.bass_utils import run_bass_kernel_spmd as _run

    nc = _bacc.Bacc("TRN2", target_bir_lowering=False, num_devices=1)
    table = constants()
    arrays, args = {}, {}
    for name in _INS + _CONSTS:
        a = _np.ascontiguousarray(inputs[name] if name in _INS else table[name])
        arrays[f"in_{name}_dram"] = a
        args[name] = nc.dram_tensor(f"in_{name}_dram", a.shape, _mybir.dt.from_np(a.dtype), kind="ExternalInput").ap()
    out = nc.dram_tensor("out_0_dram", (1, 256, 1024), _mybir.dt.float32, kind="ExternalOutput").ap()
    program(nc, args, out)
    r = _run(nc, [arrays], core_ids=[0])
    return r.results[0]["out_0_dram"]
```

```python
from contextlib import ExitStack

import concourse.bass as bass
from concourse import mybir
from concourse.alu_op_type import AluOpType as ALU

F32 = mybir.dt.float32
I32 = mybir.dt.int32
U32 = mybir.dt.uint32
ACT = mybir.ActivationFunctionType
AX_X = mybir.AxisListType.X

T = 256
D = 1024
ALPHA = 4.0 ** 0.25
LN_EPS = 1e-5
EPS = 1e-6
NEG = -1.0e30
RING = 5
SLOT = 4096
WORK = 32600
NE = 8
FE = 3584

C_ID, C_ONE, C_ROTA, C_ROTI, C_TRIL, C_LT, C_IOTA = range(7)
G_CUM, G_STRICT, G_BLOCK, G_LEVEL = 0, 1, 2, 3


class Queue:

    def __init__(self, sem):
        self.sem, self.n, self.q, self.seen = sem, 0, [], {}

    def wait(self, *tokens):
        for t in tokens:
            if t is None:
                continue
            if isinstance(t, list):
                self.wait(*t)
                continue
            sem, val = t
            if self.seen.get(sem.name, 0) < val:
                self.seen[sem.name] = val
                self.q.append(("wait", sem, val))

    def __call__(self, fn, *args, after=(), mark=True, **kw):
        self.wait(*after)
        if mark:
            self.n += 1
        self.q.append(("op", fn, args, kw, self.sem if mark else None, 1))
        return (self.sem, self.n)

    def dma(self, fn, out, in_, sem, after=(), **kw):
        self.wait(*after)
        self.q.append(("op", fn, (out, in_), kw, sem, 16))

    @property
    def last(self):
        return (self.sem, self.n) if self.n else None


def emit(eng, q):
    for item in q:
        if item[0] == "wait":
            eng.wait_ge(item[1], item[2])
        elif item[0] == "op":
            ins = item[1](*item[2], **item[3])
            if item[4] is not None:
                ins.then_inc(item[4], item[5])
        else:
            flag = eng.value_load(item[1])
            with eng.If(flag > 0):
                emit(eng, item[2])


def program(nc, p, out, debug=None, stop=99):
    ctx = ExitStack()
    with ctx:
        _program(nc, ctx, p, out, debug or {}, stop)


def _program(nc, ctx, p, out, debug, stop):
    def sem(name):
        return ctx.enter_context(nc.semaphore(name))

    ring = ctx.enter_context(nc.sbuf_tensor("ring", [128, RING, SLOT], F32))
    work = ctx.enter_context(nc.sbuf_tensor("work", [128, WORK], F32))
    bank = [ctx.enter_context(nc.psum_tensor(f"bank{i}", [128, 512], F32)) for i in range(8)]

    PE, V, A, G, SP = (Queue(sem(n)) for n in ("s_pe", "s_dve", "s_act", "s_pool", "s_sp"))
    te, ve, ac, gp, sy = nc.tensor, nc.vector, nc.scalar, nc.gpsimd, nc.sync
    queues = {"PE": PE, "V": V, "A": A, "G": G, "SP": SP}

    class Stack:
        at = 0

    def take(n):
        a = Stack.at
        Stack.at += n
        assert Stack.at <= WORK, Stack.at
        return work[:, a:a + n]

    def take_top(n, at):
        return work[:, at - n:at]

    def v3(ap, a):
        return ap.rearrange("p (a b) -> p a b", a=a)

    def v4(ap, a, b):
        return ap.rearrange("p (a b c) -> p a b c", a=a, b=b)

    free = [None] * 8

    back = []

    def tick(n=1):
        for _ in range(n):
            if not back:
                return
            g = back.pop(0)
            try:
                next(g)
                back.append(g)
            except StopIteration:
                pass

    def finish(*gens):
        for g in gens:
            for _ in g:
                pass
            if g in back:
                back.remove(g)

    class Ring:
        n = 0
        s = [sem(f"s_ring{i}") for i in range(RING)]
        count = [0] * RING
        used = [None] * RING

    def load(parts):
        i = Ring.n % RING
        Ring.n += 1
        at, views = 0, []
        for cols, rows, shape, src in parts:
            dst = ring[0:rows, i, at:at + cols]
            if len(shape) == 2:
                dst = dst.rearrange("p (a b) -> p a b", a=shape[0])
            SP.dma(sy.dma_start, dst, src, Ring.s[i], after=[Ring.used[i]])
            Ring.count[i] += 16
            views.append(dst)
            at += cols
        assert at <= SLOT
        return views, (Ring.s[i], Ring.count[i]), i

    class Misc:
        n = 0

    def small(pairs, after=(), name=None, q=None):
        s = sem(name or f"s_m{Misc.n}")
        Misc.n += 1
        for dst, src in pairs:
            (q or G).dma((sy if q is SP else ac if q is A else gp).dma_start, dst, src, s, after=after)
        return (s, 16 * len(pairs))

    def mm(o, l, r, start, stop, after=(), mark=False, skip=False):
        return PE(te.matmul, o, l, r, start=start, stop=stop, skip_group_check=skip, after=after, mark=mark)

    def tr(o, i, after=(), mark=False):
        n = i.shape[0]
        return PE(te.transpose, o, i, ident[0:n, 0:n], after=after, mark=mark)

    def dump(name, ap, after):
        if name in debug:
            t = small([(debug[name], ap)], after=after, q=SP)
            dumps.append(t)
            for q in (PE, V, A, G):
                q.wait(t)
    dumps = []

    consts = take(7 * 128)
    X = v3(take(2 * D), 2)
    XT = v3(take(8 * T), 8)
    LNC = take(80)
    CWB = take(74)
    vb, sk = take(128), take(16)

    def C(k):
        return consts[:, k * 128:(k + 1) * 128]
    ident, ones = C(C_ID), C(C_ONE)
    base = Stack.at

    t_const = small([(consts, p["c_main"])], q=SP)
    t_x = small([(X, p["x"].rearrange("o (a p) d -> p (o a) d", p=128))], q=SP)

    class Alt:
        n = 0

    def copy(o, i, after=()):
        Alt.n += 1
        if Alt.n % 2:
            return V(ve.tensor_copy, o, i, after=after)
        return A(ac.copy, o, i, after=after)

    def rows_to_cols(src, dst, after, banks=(6, 7)):
        done = []
        for t in range(2):
            for g in range(2):
                b = banks[g]
                for j in range(4):
                    k = 4 * g + j
                    tk = tr(bank[b][:, j * 128:(j + 1) * 128], src[:, t, k * 128:(k + 1) * 128],
                            after=[after[t], free[b]] if j == 0 else (), mark=(j == 3))
                free[b] = copy(dst[:, 4 * g:4 * g + 4, t * 128:(t + 1) * 128], v3(bank[b][:, :], 4), after=[tk])
                done.append(free[b])
        return done

    def fm_tiles(xt, src, c0, n, width, banks, evac, x_ready, per=4, kt=8, ticks=0):
        first = True
        i = 0
        nb = 0
        while i < n:
            m4 = min(per, n - i)
            cols = m4 * width
            (w,), t_w, slot = load([(kt * cols, 128, (kt, cols),
                                     src[:, c0 + i * width:c0 + i * width + cols].rearrange("(k p) c -> p k c", p=128))])
            j = 0
            while j < m4:
                m2 = min(2, m4 - j)
                b = banks[nb % len(banks)]
                nb += 1
                for jj in range(m2):
                    for k in range(kt):
                        last = k == kt - 1 and jj == m2 - 1
                        tk = mm(bank[b][0:width, jj * T:(jj + 1) * T], w[:, k, (j + jj) * width:(j + jj + 1) * width],
                                xt[:, k, :], k == 0, k == kt - 1,
                                after=[t_w, free[b]] + ([x_ready] if first else []) if k == 0 and jj == 0 else (), mark=last)
                        first = False
                if j + m2 >= m4:
                    Ring.used[slot] = PE.last
                free[b] = evac(i + j, bank[b][0:width, 0:m2 * T].rearrange("p (a b) -> p a b", a=m2), m2, tk)
                j += m2
                tick(ticks)
            i += m4

    def rm_proj(xt, src, c0, n, banks, evac, x_ready, kt=8, ticks=0):
        nb = 0
        for c in range(n // 512):
            (w,), t_w, slot = load([(kt * 512, 128, (kt, 512),
                                     src[:, c0 + c * 512:c0 + (c + 1) * 512].rearrange("(k p) c -> p k c", p=128))])
            for t in range(2):
                b = banks[nb % len(banks)]
                nb += 1
                for k in range(kt):
                    tk = mm(bank[b][:, :], xt[:, k, t * 128:(t + 1) * 128], w[:, k, :], k == 0, k == kt - 1,
                            after=[t_w, free[b], x_ready] if k == 0 else (), mark=(k == kt - 1))
                if t == 1:
                    Ring.used[slot] = PE.last
                free[b] = evac(t, c, bank[b][:, :], tk)
                tick(ticks)

    def stats(y, tmp, ready):
        st, mv, rs = tmp[:, 0:12], tmp[:, 12:14], tmp[:, 14:16]
        for h in range(2):
            V(ve.bn_stats, st[:, 6 * h:6 * h + 6], y[:, 512 * h:512 * h + 512], after=[ready])
        V(ve.bn_aggr, mv, v3(st, 2), after=[V.last])
        V(ve.tensor_scalar, rs[:, 0:1], mv[:, 1:2], LN_EPS, None, ALU.add, after=[V.last])
        k = A(ac.activation, rs[:, 1:2], rs[:, 0:1], ACT.Sqrt, after=[V.last])
        V(ve.reciprocal, rs[:, 0:1], rs[:, 1:2], after=[k])
        return mv[:, 0:1], rs[:, 0:1]

    def cols_scaled(src, t, gcol, bcol, ready, banks=(6, 7)):
        for g in range(2):
            b = banks[g]
            for j in range(4):
                k_ = 4 * g + j
                tk = tr(bank[b][:, j * 128:(j + 1) * 128], src[:, k_ * 128:(k_ + 1) * 128],
                        after=[ready, free[b]] if j == 0 else (), mark=(j == 3))
            for j in range(4):
                k_ = 4 * g + j
                o, i = XT[:, k_, t * 128:(t + 1) * 128], bank[b][:, j * 128:(j + 1) * 128]
                gc_, bc_ = gcol[:, k_:k_ + 1], (bcol[:, k_:k_ + 1] if bcol is not None else 0.0)
                if g == 0:
                    if bcol is None:
                        V(ve.tensor_scalar, o, i, gc_, None, ALU.mult, after=[tk])
                    else:
                        V(ve.tensor_scalar, o, i, gc_, bc_, ALU.mult, ALU.add, after=[tk])
                elif bcol is None:
                    A(ac.activation, o, i, ACT.Copy, scale=gc_, after=[tk])
                else:
                    A(ac.activation, o, i, ACT.Identity, bias=bc_, scale=gc_, after=[tk])
            free[b] = (V if g == 0 else A).last

    def residual_norm(add, ln, gb, t_gb, tmps, cols=True):
        gcol, bcol = LNC[:, 8 * ln:8 * ln + 8], LNC[:, 32 + 8 * ln:40 + 8 * ln]
        xt_free = PE.last
        ready = []
        for t in range(2):
            y = X[:, t, :]
            mu, rs = stats(y, tmps[t], add(t))
            ready.append(V(ve.tensor_scalar, y, y, mu, rs, ALU.subtract, ALU.mult, after=[V.last]))
        for t in range(2):
            if cols:
                cols_scaled(X[:, t, :], t, gcol, bcol, [ready[t], xt_free])
        t_xt = [V.last, A.last]
        rows = []
        for t in range(2):
            y = X[:, t, :]
            V(ve.tensor_tensor, y, y, gb[:, 0, :], ALU.mult, after=[ready[t], t_gb, PE.last])
            rows.append(V(ve.tensor_tensor, y, y, gb[:, 1, :], ALU.add, after=[V.last]))
        return t_xt, rows

    def add_banks(banks4, toks):
        def add(t):
            for h in range(2):
                b = banks4[2 * t + h]
                xs = X[:, t, 512 * h:512 * h + 512]
                free[b] = V(ve.scalar_tensor_tensor, xs, xs, ALPHA, bank[b][:, :], ALU.mult, ALU.add, after=[toks[t], V.last])
            return V.last
        return add

    def bcast(src, n):
        return src.partition_broadcast(n)

    bi = p["b_b_in"][0]
    pw = work[:, WORK - 1400:WORK]
    pr1, pr2, oh, em, rb = pw[:, 0:128], pw[:, 128:256], pw[:, 256:640], pw[:, 640:1024], pw[:, 1024:1040]
    t_p1 = small([(pr1[0:32, :], p["ln_g"].rearrange("l i (a b) -> (l i a) b", b=128)),
                  (pr1[32:64, :], p["ln_b"].rearrange("l i (a b) -> (l i a) b", b=128)),
                  (pr1[64:80, :], p["norm_g_2"].rearrange("l (a b) -> (l a) b", b=128)),
                  (pr2[0:64, :], p["a_conv_w"][0].rearrange("j (i c) -> (j i) c", c=128)),
                  (pr2[64:72, :], bi[0:1024].rearrange("(a b) -> a b", b=128)),
                  (pr2[72:73, 0:64], bi[1024:1088].unsqueeze(0)), (pr2[72:73, 64:128], bi[1024:1088].unsqueeze(0)),
                  (pr2[73:74, 0:64], bi[1088:1152].unsqueeze(0)), (pr2[73:74, 64:128], bi[1088:1152].unsqueeze(0))], q=A)
    t_x0 = rows_to_cols(X, XT, [[t_const, t_x]] * 2)
    k = tr(bank[5][:, 0:80], pr1[0:80, :], after=[t_p1])
    k = tr(bank[5][:, 128:202], pr2[0:74, :], mark=True)
    V(ve.tensor_copy, LNC, bank[5][:, 0:80], after=[k])
    free[5] = t_par = V(ve.tensor_copy, CWB, bank[5][:, 128:202])

    def gdn(x_ready):
        Stack.at = base
        cg = take(9 * 128)

        def CG(k):
            return cg[:, k * 128:(k + 1) * 128]
        nw = take(128)
        ab = take(16)
        wba = v3(take(8 * 16), 8)
        cw = CWB
        gates = take(13 * 16)
        sq = v3(take(2 * T), 2)
        small_t = take(32)
        qkv = v3(take(16 * T), 16)
        Z = v3(take(2 * D), 2)
        t_p = small([(wba, p["a_w_in"][0][:, 3072:3088].rearrange("(k p) c -> p k c", p=128)),
                     (ab[:, 0:8], bcast(p["a_a_log"][0], 128)), (ab[:, 8:16], bcast(p["a_dt_bias"][0], 128)),
                     (cg, p["c_gdn"]), (nw, bcast(p["a_norm_w"][0], 128))], q=A)
        silu_done = []

        def conv(i0, ps, m, tk):
            for j in range(m):
                V(ve.tensor_scalar, qkv[:, i0 + j, :], ps[:, j, :], cw[:, 48 + i0 + j:49 + i0 + j], None, ALU.mult, after=[tk, t_par])
            for s in (1, 2, 3):
                kk = V.last
                for j in range(m):
                    i = i0 + j
                    o = qkv[:, i, :]
                    V(ve.scalar_tensor_tensor, o[:, s:], ps[:, j, 0:T - s], cw[:, 16 * (3 - s) + i:16 * (3 - s) + i + 1],
                      o[:, s:], ALU.mult, ALU.add, after=[(kk[0], kk[1] - m + 1 + j)])
            kk = V.last
            A(ac.activation, qkv[:, i0:i0 + m, :], qkv[:, i0:i0 + m, :], ACT.Silu, after=[kk])
            silu_done.append(A.last)
            return kk
        wi = p["a_w_in"][0]
        fm_tiles(XT, wi, 0, 8, 128, (0, 1, 2, 3), conv, x_ready)

        for t in range(2):
            for kk in range(8):
                k = mm(bank[4][:, 16 * t:16 * t + 16], XT[:, kk, t * 128:(t + 1) * 128], wba[:, kk, :], kk == 0, kk == 7,
                       mark=(kk == 7), after=[x_ready, t_p, free[4]])
        bav = v3(gates[:, 0:32], 2)
        free[4] = V(ve.tensor_copy, bav, v3(bank[4][:, 0:32], 2), after=[k])
        beta = v3(gates[:, 32:48], 2)
        g_, gc, egc, kds, t1, t2, t3 = (v3(gates[:, 48 + 16 * i:64 + 16 * i], 2) for i in range(7))
        dl = v3(gates[:, 160:192], 4)
        ea = gates[:, 192:200]
        gv = gates[:, 48:64]
        tg = {}

        def gate_steps():
            A(ac.activation, beta, bav[:, :, 0:8], ACT.Sigmoid, after=[V.last])
            tg["beta"] = A.last
            abx = ab[:, 8:16].unsqueeze(1).broadcast_to([128, 2, 8])
            V(ve.tensor_tensor, t1, bav[:, :, 8:16], abx, ALU.add, after=[V.last, t_p])
            V(ve.tensor_scalar, t2, t1, -1.0, None, ALU.mult, after=[V.last])
            V(ve.tensor_tensor, t2, t1, t2, ALU.min, after=[V.last])
            k = A(ac.activation, t2, t2, ACT.Exp, after=[V.last])
            A(ac.activation, ea, ab[:, 0:8], ACT.Exp, after=[t_p])
            t_ea = A.last
            log1p(t2, t3, g_, k)
            V(ve.tensor_scalar, t1, t1, 0.0, None, ALU.max, after=[V.last])
            V(ve.tensor_tensor, t1, t1, t2, ALU.add, after=[V.last])
            V(ve.tensor_scalar, ea, ea, -1.0, None, ALU.mult, after=[t_ea])
            t_g = V(ve.tensor_tensor, g_, t1, ea.unsqueeze(1).broadcast_to([128, 2, 8]), ALU.mult, after=[V.last])
            yield
            mm(bank[4][:, 0:16], CG(G_CUM), gv, True, True, after=[t_g, free[4]])
            mm(bank[4][:, 16:32], CG(G_BLOCK), gv, True, True)
            for c in range(4):
                r = 64 * (c % 2)
                k = mm(bank[6 + c % 2][:, 8 * (c // 2):8 * (c // 2) + 8], ones[r:r + 64, :], g_[r:r + 64, c // 2, :], True, True,
                       mark=(c == 3), after=[free[6 + c % 2]])
            V(ve.tensor_copy, gc, v3(bank[4][:, 0:16], 2), after=[k])
            V(ve.tensor_tensor, kds, v3(bank[4][:, 16:32], 2), gc, ALU.subtract, after=[V.last])
            free[4] = V.last
            A(ac.activation, kds, kds, ACT.Exp, after=[V.last])
            A(ac.activation, egc, gc, ACT.Exp)
            for c in range(2):
                free[6 + c] = A(ac.activation, dl[:, c::2, :], v3(bank[6 + c][:, 0:16], 2), ACT.Exp)
            V(ve.tensor_tensor, egc, egc, beta, ALU.mult, after=[A.last])
            tg["gates"] = V.last

        def norm_steps():
            t_q = None
            for i in range(0, 8, 2):
                b = 6 + (i // 2) % 2
                x2 = qkv[:, i:i + 2, :]
                xf = x2.rearrange("p a b -> p (a b)")
                V(ve.tensor_tensor, sq, x2, x2, ALU.mult, after=[silu_done[i // 2], t_q])
                t_q = mm(bank[b][:, :], ones, sq.rearrange("p a b -> p (a b)"), True, True, mark=True, after=[V.last, free[b]])
                V(ve.tensor_scalar, bank[b][:, :], bank[b][:, :], EPS, None, ALU.add, after=[t_q])
                k = A(ac.activation, bank[b][:, :], bank[b][:, :], ACT.Sqrt, after=[V.last])
                V(ve.reciprocal, bank[b][:, :], bank[b][:, :], after=[k])
                free[b] = V(ve.scalar_tensor_tensor, xf, xf, 128.0 ** -0.5 if i < 4 else 1.0, bank[b][:, :],
                            ALU.mult, ALU.mult, after=[V.last])
                yield
            tg["qk"] = V.last
        gs, ns = gate_steps(), norm_steps()
        back.extend([gs, ns])
        fm_tiles(XT, wi, 1024, 8, 128, (0, 1, 2, 3), lambda i0, ps, m, tk: conv(i0 + 8, ps, m, tk), x_ready, ticks=2)
        finish(gs, ns)
        t_qk, t_gates, t_beta = tg["qk"], tg["gates"], tg["beta"]
        dump("gdn_qkv", qkv, [t_qk, A.last])
        dump("gdn_gc", gc, [t_gates])

        def heads(ap):
            return ap.rearrange("p (h e) -> p h e", e=128)
        for q_ in (V, A, PE):
            q_.wait(t_band[0])
        AQ, AM, TM, KB, KD, VB, QD = (heads(take(2048)) for _ in range(7))
        KR = heads(take(1024))
        BB = [heads(take(512)) for _ in range(4)]
        S = heads(take(1024))
        OT = XT
        qk_flat = qkv.rearrange("p a b -> p (a b)")
        NW, TT = heads(qk_flat[:, 0:2048]), heads(qk_flat[:, 2048:4096])
        ready = {}

        def rows_steps():
            for t in range(2):
                ts = slice(t * 128, (t + 1) * 128)
                for kh in range(4):
                    k = tr(bank[4][:, kh * 128:(kh + 1) * 128], qkv[:, 4 + kh, ts], after=[t_qk, free[4], t_par], mark=(kh == 3))
                free[4] = A(ac.copy, KR[:, 4 * t:4 * t + 4, :], v3(bank[4][:, :], 4), after=[k])
                for h in range(8):
                    V(ve.tensor_scalar, KB[:, 8 * t + h, :], KR[:, 4 * t + h // 2, :], egc[:, t, h:h + 1], None, ALU.mult, after=[free[4], t_gates])
                yield
                for hg in range(2):
                    for j in range(4):
                        k = tr(bank[5][:, j * 128:(j + 1) * 128], qkv[:, 8 + 4 * hg + j, ts], after=[silu_done, free[5]], mark=(j == 3))
                    for j in range(4):
                        h = 4 * hg + j
                        A(ac.activation, VB[:, 8 * t + h, :], bank[5][:, j * 128:(j + 1) * 128], ACT.Copy, scale=beta[:, t, h:h + 1],
                          after=[k, t_beta])
                    free[5] = A.last
                    yield
            ready["v"] = PE.last

        def decay_steps():
            for t in range(2):
                ts = slice(t * 128, (t + 1) * 128)
                for kh in range(4):
                    kt_ = qkv[:, 4 + kh, ts]
                    mm(bank[2][:, kh * 128:(kh + 1) * 128], kt_, kt_, True, True, after=[free[2], free[3], t_qk])
                    t_kk = mm(bank[3][:, kh * 128:(kh + 1) * 128], kt_, qkv[:, kh, ts], True, True, mark=(kh == 3))
                for hg in range(2):
                    gi = 2 * t + hg
                    hs = slice(4 * gi, 4 * gi + 4)
                    b = 6 + hg
                    bb = BB[gi]
                    for j in range(4):
                        V(ve.tensor_scalar, bb[:, j, :], ones, g_[:, t, 4 * hg + j:4 * hg + j + 1], None, ALU.mult, after=[t_gates])
                    for j in range(4):
                        k = mm(bank[b][:, j * 128:(j + 1) * 128], bb[:, j, :], CG(G_CUM), True, True, after=[V.last, free[b]], mark=(j == 3))
                    R = v3(bank[b][:, :], 4)
                    gcb = gc[:, t, 4 * hg:4 * hg + 4].unsqueeze(2).broadcast_to([128, 4, 128])
                    A(ac.activation, bb, R, ACT.Exp, after=[k])
                    t_er = A.last
                    V(ve.tensor_tensor, AQ[:, hs, :], R, gcb, ALU.subtract, after=[t_er])
                    free[b] = V.last
                    V(ve.tensor_scalar, AM[:, hs, :], AQ[:, hs, :], 0.0, None, ALU.max, after=[V.last])
                    V(ve.tensor_scalar, AQ[:, hs, :], AQ[:, hs, :], 0.0, None, ALU.min, after=[V.last])
                    qh = qkv[:, 2 * hg:2 * hg + 2, ts].unsqueeze(2).broadcast_to([128, 2, 2, 128])
                    V(ve.tensor_tensor, QD[:, hs, :].rearrange("p (a b) e -> p a b e", b=2), bb.rearrange("p (a b) e -> p a b e", b=2),
                      qh, ALU.mult, after=[t_er, t_qk])
                    v_ = V.last
                    A(ac.activation, AM[:, hs, :], AM[:, hs, :], ACT.Exp, scale=-1.0, after=[v_])
                    t_e2 = A.last
                    A(ac.activation, AQ[:, hs, :], AQ[:, hs, :], ACT.Exp, after=[v_])
                    t_e1 = A.last
                    yield

                    def msk(i):
                        return CG(i).unsqueeze(1).broadcast_to([128, 4, 128])
                    V(ve.tensor_tensor, AM[:, hs, :], AM[:, hs, :], msk(G_STRICT), ALU.mult, after=[t_e2])
                    V(ve.tensor_tensor, AQ[:, hs, :], AQ[:, hs, :], msk(G_CUM), ALU.mult, after=[t_e1])
                    t_m2 = V.last
                    for j in range(4):
                        h = 4 * hg + j
                        V(ve.scalar_tensor_tensor, AM[:, 8 * t + h, :], bank[2][:, (h // 2) * 128:(h // 2 + 1) * 128], beta[:, t, h:h + 1],
                          AM[:, 8 * t + h, :], ALU.mult, ALU.mult, after=[t_m2, t_beta, t_kk])
                    ready["a", gi] = V.last
                    kq = v3(bank[3][:, 256 * hg:256 * hg + 256], 2).unsqueeze(2).broadcast_to([128, 2, 2, 128])
                    V(ve.tensor_tensor, AQ[:, hs, :].rearrange("p (a b) e -> p a b e", b=2),
                      AQ[:, hs, :].rearrange("p (a b) e -> p a b e", b=2), kq, ALU.mult, after=[t_m2, t_kk])
                    free[2] = free[3] = V.last
                    yield
            ready["aq"] = V.last
        rs_, ds_ = rows_steps(), decay_steps()
        back.extend([rs_, ds_])

        def z_evac(t, c, ps, tk):
            return A(ac.activation, Z[:, t, 512 * c:512 * c + 512], ps, ACT.Silu, after=[tk])
        rm_proj(XT, wi, 2048, 1024, (0, 1), z_evac, x_ready, ticks=3)
        t_z = A.last
        finish(rs_, ds_)
        dump("gdn_A", AM[:, 0:8, :], [V.last])
        dump("gdn_AQ", AQ[:, 0:8, :], [V.last])
        idb = ident.unsqueeze(1).broadcast_to([128, 4, 128])
        tt_r, b_used = [None] * 4, [None] * 4
        n1 = n2 = 0
        bset1, bset2 = (0, 1), (2, 3, 4, 5, 6, 7)
        for lv in range(6):
            t_bs, t_ms = [], []
            for gi in range(4):
                hs = slice(4 * gi, 4 * gi + 4)
                t_bs.append(V(ve.tensor_tensor, BB[gi], AM[:, hs, :], CG(G_LEVEL + lv).unsqueeze(1).broadcast_to([128, 4, 128]),
                              ALU.mult, after=[ready["a", gi], b_used[gi], tt_r[gi]]))
                b = bset1[n1 % 2]
                n1 += 1
                if lv == 0:
                    V(ve.tensor_tensor, TM[:, hs, :], idb, BB[gi], ALU.subtract, after=[V.last])
                    for j in range(4):
                        k = tr(bank[b][:, j * 128:(j + 1) * 128], BB[gi][:, j, :], after=[t_bs[gi], free[b]], mark=(j == 3))
                    free[b] = V(ve.tensor_tensor, TT[:, hs, :], idb, v3(bank[b][:, :], 4), ALU.subtract, after=[k, ready["v"]])
                    tt_r[gi] = V.last
                    b_used[gi] = k
                else:
                    for j in range(4):
                        k = mm(bank[b][:, j * 128:(j + 1) * 128], BB[gi][:, j, :], TT[:, 4 * gi + j, :], True, True,
                               after=[t_bs[gi], free[b], tt_r[gi]], mark=(j == 3))
                    free[b] = A(ac.copy, BB[gi], v3(bank[b][:, :], 4), after=[k])
                    t_ms.append(A.last)
            if lv == 0:
                continue
            for gi in range(4):
                hs = slice(4 * gi, 4 * gi + 4)
                if lv < 5:
                    b2 = bset2[n2 % 6]
                    n2 += 1
                    for j in range(4):
                        k = mm(bank[b2][:, j * 128:(j + 1) * 128], BB[gi][:, j, :], TM[:, 4 * gi + j, :], True, True,
                               after=[t_ms[gi], free[b2]], mark=(j == 3))
                b3 = bset2[n2 % 6]
                n2 += 1
                for j in range(4):
                    k3 = mm(bank[b3][:, j * 128:(j + 1) * 128], TM[:, 4 * gi + j, :], BB[gi][:, j, :], True, True,
                            after=[t_ms[gi], free[b3]], mark=(j == 3))
                b_used[gi] = k3
                free[b3] = V(ve.tensor_tensor, TT[:, hs, :], TT[:, hs, :], v3(bank[b3][:, :], 4), ALU.subtract, after=[k3])
                tt_r[gi] = V.last
                if lv < 5:
                    free[b2] = V(ve.tensor_tensor, TM[:, hs, :], TM[:, hs, :], v3(bank[b2][:, :], 4), ALU.subtract, after=[k3])
        t_inv = PE.last
        for gi in range(4):
            b = bset2[gi]
            for j in range(4):
                k = mm(bank[b][:, j * 128:(j + 1) * 128], KB[:, 4 * gi + j, :], TT[:, 4 * gi + j, :], True, True,
                       after=[tt_r[gi], free[b], ready["aq"]], mark=(j == 3))
            free[b] = A(ac.mul, NW[:, 4 * gi:4 * gi + 4, :], v3(bank[b][:, :], 4), -1.0, after=[k])
            ready["nw", gi] = A.last
        for i in range(16):
            V(ve.tensor_scalar, KD[:, i, :], KR[:, 4 * (i // 8) + (i % 8) // 2, :], kds[:, i // 8, i % 8:i % 8 + 1], None, ALU.mult)
        t_kd = V.last
        gb = v3(TM.rearrange("p a b -> p (a b)"), 2)
        t_gb = small([(gb[:, 0, :], bcast(p["ln_g"][0, 0], 128)), (gb[:, 1, :], bcast(p["ln_b"][0, 0], 128))], after=[t_inv, V.last])
        for t in range(2):
            zz = Z[:, t, :].rearrange("p (h e) -> p h e", h=8)
            V(ve.tensor_tensor, zz, zz, nw.unsqueeze(1).broadcast_to([128, 8, 128]), ALU.mult, after=[t_z, t_p])
        dump("gdn_TT", TT[:, 0:8, :], [V.last])
        def own(c, h):
            t, rs = c // 2, slice(64 * (c % 2), 64 * (c % 2) + 64)
            i = 8 * t + h
            mm(bank[h // 4][rs, (h % 4) * 128:(h % 4 + 1) * 128], TT[rs, i, rs], VB[rs, i, :], h % 4 == 0, False, skip=True,
               after=[free[h // 4], tt_r[2 * t + h // 4]], mark=(h % 4 == 3))

        O = AQ
        t_o_of = [None]

        def o_rows(t):
            sr = small_t[:, 8:16]
            ss = small_t[:, 0:8]
            Ot, Qt = O[:, 8 * t:8 * t + 8, :], QD[:, 8 * t:8 * t + 8, :]
            for hg in range(2):
                A(ac.copy, Ot[:, 4 * hg:4 * hg + 4, :], v3(bank[2 + hg][:, :], 4), after=[t_o_of[0]])
                free[2 + hg] = A.last
            yield
            V(ve.tensor_tensor, Qt, Ot, Ot, ALU.mult, after=[A.last, t_o_of[0]])
            V(ve.tensor_reduce, ss, Qt, AX_X, ALU.add, after=[V.last])
            V(ve.tensor_scalar, ss, ss, 1.0 / 128, EPS, ALU.mult, ALU.add, after=[V.last])
            A(ac.activation, sr, ss, ACT.Sqrt, after=[V.last])
            V(ve.tensor_tensor, Ot, Ot, Z[:, t, :].rearrange("p (h e) -> p h e", h=8), ALU.mult, after=[V.last])
            V(ve.reciprocal, ss, sr, after=[A.last])
            yield
            V(ve.tensor_tensor, Ot, Ot, ss.unsqueeze(2).broadcast_to([128, 8, 128]), ALU.mult, after=[V.last])
            k0 = V.last
            for g in range(2):
                b = 6 + g
                for j in range(4):
                    k = tr(bank[b][:, j * 128:(j + 1) * 128], Ot[:, 4 * g + j, :], after=[k0, free[b]], mark=(j == 3))
                free[b] = copy(OT[:, 4 * g:4 * g + 4, t * 128:(t + 1) * 128], v3(bank[b][:, :], 4), after=[k])
        for h in range(8):
            own(0, h)
        t_s = None
        for c in range(4):
            t, rs = c // 2, slice(64 * (c % 2), 64 * (c % 2) + 64)
            for h in range(8):
                o = bank[h // 4][rs, (h % 4) * 128:(h % 4 + 1) * 128]
                if c:
                    k = mm(o, NW[:, 8 * t + h, rs], S[:, h, :], False, h % 4 == 3, skip=True, after=[t_s, ready["nw", 2 * t + h // 4]],
                           mark=(h % 4 == 3))
                else:
                    k = PE.last
                if h % 4 == 3:
                    src, dst = v3(bank[h // 4][rs, :], 4), VB[rs, 8 * t + h - 3:8 * t + h + 1, :]
                    free[h // 4] = V(ve.tensor_copy, dst, src, after=[k]) if h == 3 else A(ac.copy, dst, src, after=[k])
            t_vn = [free[0], free[1]]
            if c:
                for h in range(8):
                    k = mm(bank[2 + h // 4][rs, (h % 4) * 128:(h % 4 + 1) * 128], QD[:, 8 * t + h, rs], S[:, h, :], h % 4 == 0, False,
                           skip=True, after=[free[2 + h // 4]], mark=(h == 7))
            if c < 3:
                for h in range(8):
                    b = 4 + h // 4
                    k = mm(bank[b][:, (h % 4) * 128:(h % 4 + 1) * 128], KD[rs, 8 * t + h, :], VB[rs, 8 * t + h, :], True, True,
                           after=[free[b], t_vn, t_kd], mark=(h % 4 == 3))
                    if h % 4 == 3:
                        for hh in range(h - 3, h + 1):
                            s_, ps = S[:, hh, :], bank[b][:, (hh % 4) * 128:(hh % 4 + 1) * 128]
                            if c:
                                V(ve.scalar_tensor_tensor, s_, s_, dl[:, c, hh:hh + 1], ps, ALU.mult, ALU.add, after=[k])
                            else:
                                V(ve.tensor_copy, s_, ps, after=[k])
                        free[b] = V.last
                t_s = V.last
            for h in range(8):
                i = 8 * t + h
                t_o = mm(bank[2 + h // 4][rs, (h % 4) * 128:(h % 4 + 1) * 128], AQ[rs, i, rs], VB[rs, i, :], c == 0 and h % 4 == 0,
                         h % 4 == 3, skip=True, after=[free[2 + h // 4], t_vn], mark=(h == 7))
            if c == 1:
                t_o_of[0] = t_o
                post = o_rows(0)
                next(post)
            if c < 3:
                for h in range(8):
                    own(c + 1, h)
            if c == 2:
                next(post)
                finish(post)
        t_o_of[0] = t_o
        finish(o_rows(1))
        t_ot = [V.last, A.last]
        dump("gdn_o", OT, t_ot)
        toks = out_proj(OT, p["a_w_out"][0], (0, 1, 2, 3), t_ot)
        return residual_norm(add_banks((0, 1, 2, 3), toks), 0, gb, t_gb, [sq[:, 0, 0:16], sq[:, 0, 16:32]])

    def log1p(y, u, d, ready):
        V(ve.tensor_scalar, u, y, 1.0, None, ALU.add, after=[ready])
        V(ve.tensor_scalar, d, u, 1.0, 1e-30, ALU.subtract, ALU.add, after=[V.last])
        A(ac.activation, u, u, ACT.Ln, after=[V.last])
        V(ve.reciprocal, d, d, after=[V.last])
        V(ve.tensor_scalar, u, u, 1e-30, None, ALU.add, after=[A.last])
        V(ve.tensor_tensor, u, u, d, ALU.mult, after=[V.last])
        V(ve.tensor_tensor, y, y, u, ALU.mult, after=[V.last])

    def out_proj(ot, w, banks4, ready):
        ld = [load([(4096, 128, (4, 1024), w[g * 512:(g + 1) * 512, :].rearrange("(k p) c -> p k c", p=128))]) for g in range(2)]
        toks = []
        for t in range(2):
            for g in range(2):
                (wv,), t_w, slot = ld[g]
                for j in range(4):
                    for h in range(2):
                        b = banks4[2 * t + h]
                        mm(bank[b][:, :], ot[:, 4 * g + j, t * 128:(t + 1) * 128], wv[:, j, 512 * h:512 * h + 512],
                           g == 0 and j == 0, g == 1 and j == 3, after=[t_w, ready, free[b]], mark=(j == 3 and h == 1))
                if t == 1:
                    Ring.used[slot] = PE.last
            toks.append(PE.last)
        return toks

    def ffn(x_ready):
        Stack.at = base
        gb = v3(take(2 * D), 2)
        t_gb = small([(gb[:, 0, :], bcast(p["ln_g"][0, 1], 128)), (gb[:, 1, :], bcast(p["ln_b"][0, 1], 128))],
                     after=[V.last, PE.last, A.last])
        sg = v4(take(4 * T), 2, 2)
        hT = take(2 * 4 * T).rearrange("p (a b c) -> p a b c", a=2, b=4)
        tm = take(32)
        groups = [(512 * i, 4) for i in range(5)] + [(2560, 2)]
        wg, wu, wd = p["ffn_w_gate"][0], p["ffn_w_up"][0], p["ffn_w_down"][0]
        h_ready = [None, None]
        h_used = [None, None]
        A_prev = [None, None]

        toks = [None, None]

        def down(gi):
            c0, m = groups[gi]
            (w,), t_w, slot = load([(m * 1024, 128, (m, 1024), wd[c0:c0 + m * 128, :].rearrange("(k p) c -> p k c", p=128))])
            for t in range(2):
                for j in range(m):
                    for h in range(2):
                        b = 2 * t + h
                        k = mm(bank[b][:, :], hT[:, gi % 2, j, t * 128:(t + 1) * 128], w[:, j, 512 * h:512 * h + 512],
                               gi == 0 and j == 0, gi == len(groups) - 1 and j == m - 1,
                               after=[t_w, h_ready[gi % 2], free[b]], mark=(j == m - 1))
                toks[t] = k
            h_used[gi % 2] = k
            Ring.used[slot] = k
        nb = 0
        for gi, (c0, m) in enumerate(groups):
            cols = m * 128
            (g1,), t_w, s1 = load([(8 * cols, 128, (8, cols), wg[:, c0:c0 + cols].rearrange("(k p) c -> p k c", p=128))])
            (u1,), t_u, s2 = load([(8 * cols, 128, (8, cols), wu[:, c0:c0 + cols].rearrange("(k p) c -> p k c", p=128))])
            for j in range(m):
                b = 4 + nb % 4
                for q, (w, tw) in enumerate(((g1, t_w), (u1, t_u))):
                    for k_ in range(8):
                        k = mm(bank[b][:, q * T:(q + 1) * T], w[:, k_, j * 128:(j + 1) * 128], XT[:, k_, :], k_ == 0, k_ == 7,
                               after=[tw, free[b], x_ready], mark=(k_ == 7))
                s_ = sg[:, nb % 2, 0, :]
                A(ac.activation, s_, bank[b][:, 0:T], ACT.Silu, after=[k, A_prev[nb % 2]])
                free[b] = V(ve.tensor_tensor, hT[:, gi % 2, j, :], s_, bank[b][:, T:2 * T], ALU.mult, after=[A.last, h_used[gi % 2]])
                A_prev[nb % 2] = V.last
                nb += 1
            Ring.used[s1] = Ring.used[s2] = PE.last
            h_ready[gi % 2] = V.last
            if gi:
                down(gi - 1)
        down(len(groups) - 1)
        return residual_norm(add_banks((0, 1, 2, 3), toks), 1, gb, t_gb, [tm[:, 0:16], tm[:, 16:32]])

    def attend(units, buf, st, pT, banks, qk, mask, scale, pv, extra=None, rows_ready=None):
        bq, bt, bo = banks
        n = len(units)
        tok = [{} for _ in range(n)]
        s_used, p_used = [None, None], [None, None]

        def stage1(i):
            hs, wd, key = units[i]
            nh, a = len(hs), i % 2
            b = bq[i % len(bq)]
            w1 = wd + (1 if extra else 0)
            sv = buf[a][:, 0:nh * w1].rearrange("p (h w) -> p h w", h=nh)
            m, nm, sm = (st[:, 16 * a + 4 * q:16 * a + 4 * q + nh] for q in range(3))
            for q in range(nh):
                k = qk(units[i], q, bank[b][:, q * wd:(q + 1) * wd], [free[b]], q == nh - 1)
            if extra:
                V(ve.tensor_copy, sv[:, :, wd], extra(units[i]), after=[s_used[a]])
            free[b] = V(ve.scalar_tensor_tensor, sv[:, :, 0:wd], v3(bank[b][:, :], nh), scale, mask(units[i]), ALU.mult, ALU.add,
                        after=[k, s_used[a], rows_ready])
            V(ve.tensor_reduce, m, sv, AX_X, ALU.max, after=[V.last])
            V(ve.tensor_scalar, nm, m, -1.0, None, ALU.mult, after=[V.last, tok[i - 2].get("exp") if i > 1 else None])
            t_m = V.last
            for q in range(nh):
                A(ac.activation, sv[:, q, :], sv[:, q, :], ACT.Exp, bias=nm[:, q:q + 1], accum_out=sm[:, q:q + 1],
                  after=[t_m, tok[i - 2].get("norm") if i > 1 else None])
            tok[i].update(exp=A.last, sv=sv, sm=sm)

        def stage2(i):
            hs, wd, key = units[i]
            nh, a, nt = len(hs), i % 2, wd // 128
            sv, sm = tok[i]["sv"], tok[i]["sm"]
            V(ve.reciprocal, sm, sm, after=[tok[i]["exp"]])
            t_r = V.last
            for q in range(nh):
                V(ve.tensor_scalar, sv[:, q, 0:wd], sv[:, q, 0:wd], sm[:, q:q + 1], None, ALU.mult, after=[t_r])
            tok[i]["norm"] = V.last
            b = bt[i % len(bt)]
            for q in range(4):
                k = tr(bank[b][:, q * 128:(q + 1) * 128], sv[:, q // nt, (q % nt) * 128:(q % nt + 1) * 128], after=[V.last, free[b]],
                       mark=(q == 3))
            s_used[a] = k
            free[b] = A(ac.copy, pT[:, a, :], bank[b][:, :], after=[k, p_used[a]])
            tok[i]["pT"] = A.last

        def stage3(i):
            b = bo[i % len(bo)]
            p_used[i % 2] = pv(units[i], pT[:, i % 2, :], tok[i]["pT"], b)
        for i in range(n + 2):
            if i < n:
                stage1(i)
            if 1 <= i <= n:
                stage2(i - 1)
            if i >= 2:
                stage3(i - 2)
            yield

    def load_views(cols, rows, shape, parts):
        i = Ring.n % RING
        Ring.n += 1
        dst = ring[0:rows, i, 0:cols].rearrange("p (a b) -> p a b", a=shape[0])
        for cut, src in parts:
            SP.dma(sy.dma_start, cut(dst), src, Ring.s[i], after=[Ring.used[i]])
            Ring.count[i] += 16
        return dst, (Ring.s[i], Ring.count[i]), i

    def band():
        t_p = small([(oh[0:32, :], p["c_oh"]), (em[0:16, :], p["c_em"]), (rb[0:32, :], p["rel_bias"]),
                     (vb, bcast(bi[1152:1280], 128)), (sk, bcast(p["b_sinks"][0], 128))])
        k = mm(bank[4][0:16, 0:384], rb[0:32, :], oh[0:32, :], True, True, after=[t_p, free[4]], mark=True)
        free[4] = V(ve.tensor_tensor, em[0:16, :], em[0:16, :], bank[4][0:16, 0:384], ALU.add, after=[k])
        scr = nc.dram_tensor("scr_band", [16, 128, 384], F32, kind="Internal").ap()
        t_w = small([(scr, em[0:16, :].unsqueeze(1).broadcast_to([16, 128, 384]))], after=[V.last])
        return t_w, bass.AP(tensor=scr.tensor, offset=127, ap=[[383, 128], [128 * 384, 16], [1, 256]])

    bias = v3(take_top(16 * T, WORK), 16)

    def swa_loads(after):
        gb = v3(take_top(2 * D, WORK - 16 * T), 2)
        t_bias = small([(bias, t_band[1])], after=[t_band[0], after])
        t_gb = small([(gb[:, 0, :], bcast(p["ln_g"][1, 0], 128)), (gb[:, 1, :], bcast(p["ln_b"][1, 0], 128))], after=[after])
        return gb, t_bias, t_gb

    def swa(x_ready, loaded):
        gb, t_bias, t_gb = loaded
        Stack.at = base
        qT = v3(take(8 * T), 8)
        kd = v3(take(2 * T), 2)
        vv = v3(take(2 * 128), 2)
        st = take(32)
        buf = [take(516), take(516)]
        pT = v3(take(2 * 512), 2)
        oT = v3(take(8 * T), 8)
        tm = take(32)
        pc = CWB[:, 64:74]
        w = p["b_w_in"][0]
        wr = w[:, :].rearrange("(k p) c -> p k c", p=128)
        wk, t_wk, slot = load_views(3072, 128, (8, 384), [
            (lambda d: d[:, :, 0:64], wr[:, :, 1024:1088]), (lambda d: d[:, :, 64:128], wr[:, :, 1024:1088]),
            (lambda d: d[:, :, 128:192], wr[:, :, 1088:1152]), (lambda d: d[:, :, 192:256], wr[:, :, 1088:1152]),
            (lambda d: d[:, :, 256:384], wr[:, :, 1152:1280])])
        for kv in range(2):
            for kk in range(8):
                k = mm(bank[4][:, kv * T:(kv + 1) * T], wk[:, kk, kv * 128:kv * 128 + 128], XT[:, kk, :], kk == 0, kk == 7,
                       after=[t_wk, free[4], x_ready], mark=(kk == 7))
        for kv in range(2):
            V(ve.tensor_scalar, kd[:, kv, :], bank[4][:, kv * T:(kv + 1) * T], pc[:, 8 + kv:9 + kv], None, ALU.add, after=[k])
        free[4] = V.last
        for t in range(2):
            for kk in range(8):
                k = mm(bank[5][:, t * 128:t * 128 + 128], XT[:, kk, t * 128:(t + 1) * 128], wk[:, kk, 256:384], kk == 0, kk == 7,
                       after=[free[5]], mark=(kk == 7))
        V(ve.tensor_tensor, vv, v3(bank[5][:, 0:256], 2), vb.unsqueeze(1).broadcast_to([128, 2, 128]), ALU.add, after=[k])
        Ring.used[slot] = k
        free[5] = t_kv = V.last
        q_ready = [None] * 4

        def q_evac(i0, ps, m, tk):
            for j in range(m):
                V(ve.tensor_scalar, qT[:, i0 + j, :], ps[:, j, :], pc[:, i0 + j:i0 + j + 1], None, ALU.add, after=[tk])
            q_ready[i0 // 2] = V.last
            return V.last
        units = [([g + par, g + par + 2], 256, (1, par)) for g in range(0, 16, 4) for par in range(2)]
        units += [([g + par + 2 * i for i in range(4)], 128, (0, par)) for g in (0, 8) for par in range(2)]

        def qk(u, q, o, after, mark):
            (hs, wd, (n, par)) = u
            h = hs[q]
            r = slice(64 * par, 64 * par + 64)
            return mm(o, qT[r, h // 2, n * 128:n * 128 + 128], kd[r, h // 8, 0:wd], True, True,
                      after=after + [q_ready[h // 4], t_kv, free[4]], mark=mark)

        def mask(u):
            hs, wd, (n, par) = u
            hv = slice(hs[0], hs[-1] + 1, 2)
            return bias[:, hv, 128:256] if n == 0 else bias[:, hv, :]

        def pv(u, pt, t_pt, ob):
            hs, wd, (n, par) = u
            nt = wd // 128
            r = slice(64 * par, 64 * par + 64)
            for q in range(4):
                i, kt = q // nt, q % nt
                kvh = hs[i] // 8
                k = mm(bank[ob][r, i * 128:(i + 1) * 128], vv[:, kt, kvh * 64:kvh * 64 + 64], pt[:, q * 128:(q + 1) * 128],
                       kt == 0, kt == nt - 1, after=[t_pt, free[ob]], mark=(q == 3))
            nh = len(hs)
            free[ob] = V(ve.tensor_copy, oT[r, hs[0] // 2:hs[0] // 2 + nh, n * 128:n * 128 + 128],
                         bank[ob][r, 0:nh * 128].rearrange("p (a b) -> p a b", a=nh), after=[k])
            return k

        def sinks(u):
            return sk[:, slice(u[0][0], u[0][-1] + 1, 2)]
        g = attend(units, buf, st, pT, ((2, 3), (4, 5), (6, 7)), qk, mask, 0.125, pv, extra=sinks, rows_ready=t_bias)
        back.append(g)
        fm_tiles(XT, w, 0, 8, 128, (0, 1), q_evac, x_ready, ticks=2)
        finish(g)
        t_o = [V.last, A.last]
        dump("swa_o", oT, t_o)
        toks = out_proj(oT, p["b_w_out"][0], (0, 1, 2, 3), t_o)
        return residual_norm(add_banks((0, 1, 2, 3), toks), 2, gb, t_gb, [tm[:, 0:16], tm[:, 16:32]])

    class B2:
        rot_used = [None, None]
    Stack.at = base
    B2.cosA, B2.sinA, B2.cosI, B2.sinI = (take(T) for _ in range(4))
    B2.prm = take(256)
    B2.keep = take(384)
    B2.tm = take(32)
    B2.flag = take(8)[:, 0:1].bitcast(I32)
    B2.base = Stack.at

    def moe(x_ready, x_rows, setup):
        Stack.at = B2.base
        gb = v3(take(2 * D), 2)
        wr = v3(take(64), 8)
        fa = v3(take(2 * D), 2)
        xg = take(2 * 1024).rearrange("p (a k s) -> p a k s", a=2, k=8)
        sg = v3(take(2 * 512), 2)
        hh = v3(take(2 * 512), 2)
        hT = take(2 * 512).rearrange("p (a j s) -> p a j s", a=2, j=4)
        y = take(1024)
        P_ = v4(take(2 * 256), 2, 2)
        PG = v3(take(256), 2)
        PT = v4(take(2 * 256), 2, 2)
        rt = take(256)
        tm = take(32)
        B2.tmp = take(4 * T + 4 + 176 + 64)
        after = [V.last, PE.last, A.last]
        t_r = small([(wr, p["moe_router"][0].rearrange("(k p) e -> p k e", p=128))], after=after)
        t_gb = small([(gb[:, 0, :], bcast(p["ln_g"][1, 1], 128)), (gb[:, 1, :], bcast(p["ln_b"][1, 1], 128))], after=after)
        lg, sel, gate, rank, rank2 = (v3(rt[:, 16 * i:16 * i + 16], 2) for i in range(5))
        mx = v3(rt[:, 80:96], 2)
        ix = v3(rt[:, 96:112], 2)
        ixu = v3(rt[:, 112:128].bitcast(U32), 2)
        g01 = v3(rt[:, 128:132], 2)
        oh = v4(rt[:, 144:176], 2, 2)
        cnt = rt[:, 176:184]
        cm = rt[:, 184:185]
        flag = B2.flag
        for t in range(2):
            for kk in range(8):
                k = mm(bank[7][:, 8 * t:8 * t + 8], XT[:, kk, t * 128:(t + 1) * 128], wr[:, kk, :], kk == 0, kk == 7,
                       after=[t_r, x_ready, free[7]], mark=(kk == 7))
        free[7] = V(ve.tensor_copy, lg, v3(bank[7][:, 0:16], 2), after=[k])
        for j in range(2):
            for t in range(2):
                V(ve.max, mx[:, t, :], lg[:, t, :], after=[V.last])
                V(ve.max_index, ixu[:, t, :], mx[:, t, :], lg[:, t, :], after=[V.last])
            V(ve.tensor_copy, ix, ixu, after=[V.last])
            V(ve.tensor_copy, g01[:, :, j:j + 1], mx[:, :, 0:1], after=[V.last])
            for t in range(2):
                V(ve.tensor_scalar, oh[:, j, t, :], C(C_IOTA)[:, 0:8], ix[:, t, 0:1], None, ALU.is_equal, after=[V.last])
            if j == 0:
                V(ve.scalar_tensor_tensor, lg, oh[:, 0, :, :], -3.0e38, lg, ALU.mult, ALU.add, after=[V.last])
        V(ve.tensor_tensor, g01[:, :, 1:2], g01[:, :, 1:2], g01[:, :, 0:1], ALU.subtract, after=[V.last])
        A(ac.activation, g01[:, :, 1:2], g01[:, :, 1:2], ACT.Exp, after=[V.last])
        V(ve.tensor_scalar, g01[:, :, 0:1], g01[:, :, 1:2], 1.0, None, ALU.add, after=[A.last])
        V(ve.reciprocal, g01[:, :, 0:1], g01[:, :, 0:1], after=[V.last])
        V(ve.tensor_tensor, g01[:, :, 1:2], g01[:, :, 1:2], g01[:, :, 0:1], ALU.mult, after=[V.last])
        V(ve.tensor_tensor, sel, oh[:, 0, :, :], oh[:, 1, :, :], ALU.add, after=[V.last])
        for t in range(2):
            V(ve.tensor_scalar, gate[:, t, :], oh[:, 0, t, :], g01[:, t, 0:1], None, ALU.mult, after=[V.last])
            V(ve.scalar_tensor_tensor, gate[:, t, :], oh[:, 1, t, :], g01[:, t, 1:2], gate[:, t, :], ALU.mult, ALU.add, after=[V.last])
        t_sel = V.last
        mm(bank[7][:, 0:8], C(C_LT), sel[:, 0, :], True, True, after=[t_sel, free[7]])
        mm(bank[7][:, 8:16], ones, sel[:, 0, :], True, False)
        mm(bank[7][:, 8:16], C(C_LT), sel[:, 1, :], False, True)
        mm(bank[7][:, 16:24], ones, sel[:, 0, :], True, False)
        k = mm(bank[7][:, 16:24], ones, sel[:, 1, :], False, True, mark=True)
        V(ve.tensor_copy, rank, v3(bank[7][:, 0:16], 2), after=[k])
        V(ve.tensor_copy, cnt, bank[7][:, 16:24], after=[k])
        free[7] = V.last
        V(ve.tensor_reduce, cm, cnt, AX_X, ALU.max, after=[V.last])
        V(ve.tensor_scalar, cm, cm, 128.0, None, ALU.is_gt, after=[V.last])
        V(ve.tensor_copy, flag, cm, after=[V.last])
        t_flag = V.last
        V(ve.tensor_scalar, rank2, rank, -128.0, None, ALU.add, after=[V.last])
        t_rank = V.last
        dump("moe_gate", gate, [t_rank])

        def experts(rk, first_pass):
            steps = [(e, g) for e in range(NE) for g in range(7)]
            xg_t, pt_t = [None] * NE, [None] * NE
            hu, tu, xu, pu = [None, None], [None, None], [None, None], [None, None]
            h_t, hT_t = [None] * len(steps), [None] * len(steps)
            yt = [None]

            def prep(e):
                a = e % 2
                for t in range(2):
                    V(ve.tensor_scalar, P_[:, a, t, :], C(C_IOTA), rk[:, t, e:e + 1], sel[:, t, e:e + 1], ALU.is_equal, ALU.mult,
                      after=[t_rank, xu[a]])
                    V(ve.tensor_scalar, PG[:, t, :], C(C_IOTA), rk[:, t, e:e + 1], gate[:, t, e:e + 1], ALU.is_equal, ALU.mult,
                      after=[t_rank, PE.last])
                t_P = V.last
                for half in range(2):
                    for j in range(4):
                        kk = 4 * half + j
                        for t in range(2):
                            k = mm(bank[7][:, j * 128:(j + 1) * 128], X[:, t, kk * 128:(kk + 1) * 128], P_[:, a, t, :], t == 0, t == 1,
                                   after=[t_P, free[7], x_rows], mark=(j == 3 and t == 1))
                    free[7] = A(ac.copy, xg[:, a, 4 * half:4 * half + 4, :], v3(bank[7][:, :], 4), after=[k, xu[a]])
                xg_t[e] = A.last
                for t in range(2):
                    k = tr(bank[7][:, t * 128:(t + 1) * 128], PG[:, t, :], after=[t_P, free[7]], mark=(t == 1))
                free[7] = A(ac.copy, PT[:, a, :, :], v3(bank[7][:, 0:256], 2), after=[k, pu[a]])
                pt_t[e] = A.last

            def gate_up(n):
                e, g = steps[n]
                a = e % 2
                ws = []
                for name in ("moe_w_gate", "moe_w_up"):
                    (w,), t_w, slot = load([(4096, 128, (8, 512), p[name][0, e][:, 512 * g:512 * g + 512].rearrange("(k p) c -> p k c", p=128))])
                    ws.append((w, t_w, slot))
                bb = 2 * (n % 2)
                for q, (w, t_w, slot) in enumerate(ws):
                    for kk in range(8):
                        k = mm(bank[bb + q][:, :], xg[:, a, kk, :], w[:, kk, :], kk == 0, kk == 7,
                               after=[t_w, xg_t[e], free[bb + q]], mark=(kk == 7))
                    Ring.used[slot] = k
                    if q == 0:
                        free[bb] = A(ac.activation, sg[:, n % 2, :], bank[bb][:, :], ACT.Silu, after=[k, h_t[n - 2] if n > 1 else None])
                xu[a] = k
                free[bb + 1] = V(ve.tensor_tensor, hh[:, n % 2, :], sg[:, n % 2, :], bank[bb + 1][:, :], ALU.mult, after=[A.last, k, hu[n % 2]])
                h_t[n] = V.last

            def turn(n):
                for j in range(4):
                    k = tr(bank[6][:, j * 128:(j + 1) * 128], hh[:, n % 2, j * 128:(j + 1) * 128], after=[h_t[n], free[6]], mark=(j == 3))
                hu[n % 2] = k
                free[6] = A(ac.copy, hT[:, n % 2, :, :], v3(bank[6][:, :], 4), after=[k, tu[n % 2]])
                hT_t[n] = A.last

            def down(n):
                e, g = steps[n]
                (w,), t_w, slot = load([(4096, 128, (4, 1024), p["moe_w_down"][0, e][512 * g:512 * g + 512, :].rearrange("(k p) c -> p k c", p=128))])
                for j in range(4):
                    for h in range(2):
                        k = mm(bank[4 + h][:, :], hT[:, n % 2, j, :], w[:, j, 512 * h:512 * h + 512], g == 0 and j == 0, g == 6 and j == 3,
                               after=[t_w, hT_t[n], free[4 + h]], mark=(j == 3))
                Ring.used[slot] = tu[n % 2] = k
                if g == 6:
                    free[4] = V(ve.tensor_copy, y[:, 0:512], bank[4][:, :], after=[k, yt[0]])
                    free[5] = A(ac.copy, y[:, 512:1024], bank[5][:, :], after=[k, yt[0]])

            def scatter(e):
                t_y = [free[4], free[5]]
                for t in range(2):
                    for h in range(2):
                        b = 6 + h
                        k = mm(bank[b][:, :], PT[:, e % 2, t, :], y[:, 512 * h:512 * h + 512], True, True,
                               after=[t_y, free[b], pt_t[e]], mark=True)
                        o = fa[:, t, 512 * h:512 * h + 512]
                        if first_pass and e == 0:
                            free[b] = V(ve.tensor_copy, o, bank[b][:, :], after=[k])
                        else:
                            free[b] = V(ve.tensor_tensor, o, o, bank[b][:, :], ALU.add, after=[k])
                yt[0] = pu[e % 2] = k

            prep(0)
            N = len(steps)
            for n in range(N + 3):
                if n < N:
                    gate_up(n)
                    if steps[n][1] == 4 and steps[n][0] + 1 < NE:
                        prep(steps[n][0] + 1)
                if first_pass and n > 2:
                    tick()
                if 1 <= n <= N:
                    turn(n - 1)
                if 2 <= n <= N + 1:
                    down(n - 2)
                if n >= 3 and steps[n - 3][1] == 6:
                    scatter(steps[n - 3][0])
            return V.last

        back.append(setup)
        experts(rank, True)
        finish(setup)

        saved = (list(free), list(Ring.used), list(Ring.count), Ring.n, Ring.s)
        before = [q.last for q in (PE, V, A)]
        outer = {}
        for nm, q in queues.items():
            q.wait(t_flag)
            outer[nm] = (q.sem, q.n, q.q, dict(q.seen))
            q.wait(before)
            q.sem, q.n, q.q = sem("o_" + nm), 0, []
        for nm, q in queues.items():
            q.wait([b for b in before])
        Ring.s, Ring.count, Ring.n = [sem(f"o_ring{i}") for i in range(RING)], [0] * RING, 0
        for b in range(8):
            free[b] = list(before)
        Ring.used[:] = [before[0]] * RING
        experts(rank2, False)
        ends = [q.last for q in queues.values() if q.n]
        for nm, q in queues.items():
            q.wait(ends)
            sub = q.q
            q.sem, q.n, q.q, q.seen = outer[nm]
            for w_ in before:
                q.wait(w_)
            q.q.append(("if", flag[0:1, :], sub))
        free[:], Ring.used[:], Ring.count[:] = saved[0], saved[1], saved[2]
        Ring.n, Ring.s = saved[3], saved[4]

        def add(t):
            return V(ve.scalar_tensor_tensor, X[:, t, :], X[:, t, :], ALPHA, fa[:, t, :], ALU.mult, ALU.add, after=[V.last, PE.last])
        return residual_norm(add, 3, gb, t_gb, [tm[:, 0:16], tm[:, 16:32]], cols=False)[1]

    O_Q, O_K, O_V, O_GA, O_IQ, O_IK, O_IW, O_XR, O_GR, O_MA, O_MB = 0, 1024, 2048, 3072, 4096, 5120, 5184, 5200, 6608, 8016, 9040

    def rms_rows(o, t, g, t_g, tmp, sq, ready):
        A(ac.activation, sq, X[:, t, :], ACT.Square, accum_out=tmp[:, 0:1], after=[ready, V.last, PE.last])
        V(ve.tensor_scalar, tmp[:, 1:2], tmp[:, 0:1], 1.0 / D, EPS, ALU.mult, ALU.add, after=[A.last])
        A(ac.activation, tmp[:, 2:3], tmp[:, 1:2], ACT.Sqrt, after=[V.last])
        V(ve.reciprocal, tmp[:, 3:4], tmp[:, 2:3], after=[A.last])
        return V(ve.scalar_tensor_tensor, o, X[:, t, :], tmp[:, 3:4], g, ALU.mult, ALU.mult, after=[V.last, t_g])

    def second_setup():
        z = B2.tmp
        pos, an, kr, rr = (z[:, T * i:T * i + T] for i in range(4))
        cr, pr = z[:, 4 * T:4 * T + 4], z[:, 4 * T + 4:4 * T + 180]
        u, d = z[:, 4 * T + 180:4 * T + 212], z[:, 4 * T + 212:4 * T + 244]
        after = [V.last, PE.last, A.last]
        t_p = small([(pos.bitcast(I32), bcast(p["positions_2"][0], 128)), (cr, p["c_rope"]),
                     (pr[:, 0:88], p["conv_w_2"].rearrange("l j (n c) -> (l j n) c", c=88)),
                     (pr[0:32, 88:176], p["conv_b_2"].rearrange("l (n c) -> (l n) c", c=88)),
                     (pr[32:64, 88:176], p["b_rg_2"].rearrange("l (n c) -> (l n) c", c=88)),
                     (pr[64:96, 88:176], p["b_ig_2"].rearrange("l (n c) -> (l n) c", c=88)),
                     (pr[96:128, 88:176], p["lru_lambda_2"].rearrange("l (n c) -> (l n) c", c=88))], after=after)
        yield
        for i in range(2):
            k = tr(bank[7][0:88, 128 * i:128 * i + 128], pr[:, 88 * i:88 * i + 88], after=[t_p, free[7]], mark=True)
        free[7] = V(ve.tensor_copy, B2.prm[0:88, :], bank[7][0:88, 0:256], after=[k])
        lam = B2.prm[0:88, 224:256]
        u, d = u[0:88, :], d[0:88, :]
        m = kr[0:88, 0:32]
        V(ve.tensor_scalar, u, lam, -1.0, None, ALU.mult, after=[V.last])
        V(ve.tensor_scalar, m, u, 0.0, None, ALU.max, after=[V.last])
        V(ve.tensor_tensor, lam, lam, u, ALU.min, after=[V.last])
        A(ac.activation, lam, lam, ACT.Exp, after=[V.last])
        log1p(lam, u, d, A.last)
        V(ve.tensor_tensor, lam, lam, m, ALU.add, after=[V.last])
        V(ve.tensor_scalar, lam, lam, -8.0, None, ALU.mult, after=[V.last])
        V(ve.tensor_copy, pos, pos.bitcast(I32), after=[V.last])
        yield
        magic = 12582912.0
        for i, (co, si) in enumerate(((B2.cosA, B2.sinA), (B2.cosI, B2.sinI))):
            V(ve.tensor_scalar, an, pos, cr[:, i:i + 1], None, ALU.mult, after=[V.last, A.last])
            V(ve.tensor_scalar, kr, an, 0.15915494309189535, magic, ALU.mult, ALU.add, after=[V.last])
            V(ve.tensor_scalar, kr, kr, magic, None, ALU.subtract, after=[V.last])
            for c in (6.28125, 0.0019350051879882812, 3.01991598196e-07):
                V(ve.scalar_tensor_tensor, an, kr, -c, an, ALU.mult, ALU.add, after=[V.last])
            V(ve.tensor_scalar, an, an, 3.1415925, -3.1415925, ALU.min, ALU.max, after=[V.last])
            A(ac.activation, si, an, ACT.Sin, after=[V.last])
            V(ve.tensor_scalar, rr, an, -1.0, None, ALU.mult, after=[V.last, A.last])
            V(ve.tensor_tensor, rr, rr, an, ALU.min, after=[V.last])
            V(ve.tensor_scalar, rr, rr, cr[:, 2:3], None, ALU.add, after=[V.last])
            A(ac.activation, co, rr, ACT.Sin, after=[V.last])
            yield
        B2.t_tab = [V.last, A.last]

    def second(l, x_rows):
        t_tab = B2.t_tab
        Stack.at = B2.base
        KT, QT = v3(take(8 * T), 8), v3(take(8 * T), 8)
        VV = v3(take(2 * D), 2)
        GA = v3(take(8 * T), 8)
        GR = take(11 * T)
        IQf = take(8 * T)
        IQ = v3(IQf, 8)
        IK = take(T)
        iw = take(32)
        rl = v3(take(2 * 512), 2)
        s0, s1 = take(128), take(256)
        m8 = v3(take(16), 2)
        XC, AA, TH, XS = (v3(take(1024)[0:88, :], 4) for _ in range(4))
        RR, II = (v3(IQf[:, 1024 * i:1024 * i + 1024][0:88, :], 4) for i in range(2))
        WR = take(2 * 4 * 88)[0:88, :].rearrange("p (a c d) -> p a c d", a=2, c=4)
        bufs = [take(512), take(512)]
        pTb = v3(take(2 * 512), 2)
        rt_ = v3(take(2 * 512), 2)
        sgm = v3(take(2 * 512), 2)
        st = take(32)
        H = VV
        w = p["w_in_2"][l]
        wv = w[:, :].rearrange("(k p) c -> p k c", p=128)
        ng = LNC[:, 64 + 8 * l:72 + 8 * l]
        for t in range(2):
            tmp = B2.tm[:, 8 * t:8 * t + 8]
            A(ac.activation, GA[:, 0:4, :].rearrange("p a b -> p (a b)"), X[:, t, :], ACT.Square, accum_out=tmp[:, 0:1],
              after=[x_rows[t], PE.last])
            V(ve.tensor_scalar, tmp[:, 1:2], tmp[:, 0:1], 1.0 / D, EPS, ALU.mult, ALU.add, after=[A.last])
            A(ac.activation, tmp[:, 2:3], tmp[:, 1:2], ACT.Sqrt, after=[V.last])
            V(ve.reciprocal, tmp[:, 3:4], tmp[:, 2:3], after=[A.last])
            V(ve.tensor_scalar, H[:, t, :], X[:, t, :], tmp[:, 3:4], None, ALU.mult, after=[V.last, PE.last])
            cols_scaled(H[:, t, :], t, ng, None, [V.last, PE.last])
        x_ready = [V.last, A.last]
        tk_ = {}

        def rope(Xt, n, cos, sin, rotc, ready, name):
            for i in range(0, n, 2):
                m = min(2, n - i)
                b = 6 + (i // 2) % 2
                x2 = Xt[:, i:i + m, :]
                k = mm(bank[b][:, 0:m * T], rotc, x2.rearrange("p a b -> p (a b)"), True, True, after=[ready, free[b]], mark=True)
                r_ = rt_[:, (i // 2) % 2, 0:m * T].rearrange("p (a b) -> p a b", a=m)
                V(ve.tensor_tensor, r_, bank[b][:, 0:m * T].rearrange("p (a b) -> p a b", a=m), sin.unsqueeze(1).broadcast_to([128, m, T]),
                  ALU.mult, after=[k, t_tab, B2.rot_used[(i // 2) % 2]])
                free[b] = V.last
                V(ve.tensor_tensor, x2, x2, cos.unsqueeze(1).broadcast_to([128, m, T]), ALU.mult, after=[k, ready])
                B2.rot_used[(i // 2) % 2] = V(ve.tensor_tensor, x2, x2, r_, ALU.add, after=[V.last])
                yield
            tk_[name] = V.last

        wk, t_wk, slot = load_views(8 * 144, 128, (8, 144), [
            (lambda d: d[:, :, 0:64], wv[:, :, O_IK:O_IK + 64]), (lambda d: d[:, :, 64:128], wv[:, :, O_IK:O_IK + 64]),
            (lambda d: d[:, :, 128:144], wv[:, :, O_IW:O_IW + 16])])
        for kk in range(8):
            k = mm(bank[2][:, 0:T], wk[:, kk, 0:128], XT[:, kk, :], kk == 0, kk == 7, after=[t_wk, free[2], x_ready])
        for t in range(2):
            for kk in range(8):
                k = mm(bank[2][:, T + 16 * t:T + 16 * t + 16], XT[:, kk, t * 128:(t + 1) * 128], wk[:, kk, 128:144], kk == 0, kk == 7, mark=(kk == 7))
        Ring.used[slot] = k
        A(ac.copy, IK, bank[2][:, 0:T], after=[k])
        free[2] = A(ac.mul, iw, bank[2][:, T:T + 32], 0.03125)

        def to(dst, extra=None):
            def f(i0, ps, m, tk):
                return A(ac.copy, dst[:, i0:i0 + m, :], ps, after=[tk, extra])
            return f
        fm_tiles(XT, w, O_IQ, 8, 128, (0, 1), to(IQ), x_ready)
        t_iq = A.last
        iwv = v3(iw, 2)
        tril = C(C_TRIL)
        keep = (B2.keep[:, 0:128], B2.keep[:, 128:384])

        def index_steps():
            yield from rope(IK.unsqueeze(1), 1, B2.cosI, B2.sinI, C(C_ROTI), t_iq, "ik")
            yield from rope(IQ, 8, B2.cosI, B2.sinI, C(C_ROTI), t_iq, "iq")
            ru = [None, None]
            nr = 0
            for n, sc in ((1, s1), (0, s0)):
                wd = 128 * (n + 1)
                nh = 512 // wd
                first = True
                for g in range(0, 16, 2 * nh):
                    for par in range(2):
                        b = 4 + nr % 2
                        hs = [g + par + 2 * i for i in range(nh)]
                        for i, h in enumerate(hs):
                            k = mm(bank[b][:, i * wd:(i + 1) * wd], IQ[64 * par:64 * par + 64, h // 2, n * 128:n * 128 + 128],
                                   IK[64 * par:64 * par + 64, 0:wd], True, True, after=[tk_["iq"], free[b]], mark=(i == nh - 1))
                        free[b] = A(ac.activation, rl[:, nr % 2, :], bank[b][:, :], ACT.Relu, after=[k, ru[nr % 2]])
                        for i, h in enumerate(hs):
                            src = rl[:, nr % 2, i * wd:(i + 1) * wd]
                            if first:
                                V(ve.tensor_scalar, sc, src, iwv[:, n, h:h + 1], None, ALU.mult, after=[free[b]])
                                first = False
                            else:
                                V(ve.scalar_tensor_tensor, sc, src, iwv[:, n, h:h + 1], sc, ALU.mult, ALU.add, after=[free[b], V.last])
                        ru[nr % 2] = V.last
                        nr += 1
                        yield
            tk_["idx"] = PE.last
            bg = rl[:, 0, 0:128]
            V(ve.tensor_scalar, bg, tril, 1.0, 1.0e38, ALU.subtract, ALU.mult, after=[V.last])
            for sc in (s0, s1[:, 128:256]):
                V(ve.tensor_tensor, sc, sc, tril, ALU.mult, after=[V.last])
                V(ve.tensor_tensor, sc, sc, bg, ALU.add, after=[V.last])
            tv = [V.last, V.last]
            for r in range(8):
                for n, sc in ((0, s0), (1, s1)):
                    tv[n] = V(ve.max, m8[:, n, :], sc, after=[tv[n]])
                for n, sc in ((0, s0), (1, s1)):
                    tv[n] = V(ve.match_replace, sc, m8[:, n, :], sc, -3.0e38, after=[tv[n]])
                if r % 2:
                    yield
            for n, sc in ((0, s0), (1, s1)):
                V(ve.tensor_scalar, sc, sc, -2.0e38, None, ALU.is_lt, after=[tv[n]])
                c_ = sc[:, 128 * n:128 * n + 128]
                V(ve.tensor_tensor, c_, c_, tril, ALU.mult, after=[V.last])
                V(ve.tensor_scalar, keep[n], sc, 1.0, -NEG, ALU.subtract, ALU.mult, after=[V.last])
            tk_["keep"] = V.last
        ix = index_steps()
        back.append(ix)
        GRv = v3(GR, 11)
        xr_d = nc.dram_tensor(f"scr_xr{l}", [1408, T], F32, kind="Internal").ap()
        hr_d = nc.dram_tensor(f"scr_hr{l}", [1408, T], F32, kind="Internal").ap()
        fm_tiles(XT, w, O_XR, 11, 128, (0, 1), to(GRv), x_ready, ticks=2)
        t_xr = small([(xr_d.rearrange("(i p) t -> p i t", p=128), GRv)], after=[A.last])
        fm_tiles(XT, w, O_Q, 8, 128, (0, 1), to(QT), x_ready, ticks=2)
        t_q = A.last
        fm_tiles(XT, w, O_K, 8, 128, (0, 1), to(KT), x_ready, ticks=2)
        t_k = A.last
        finish(ix)
        dump("keep", B2.keep, [tk_["keep"]])

        t_gate = {}

        def attention_steps():
            yield from rope(QT, 8, B2.cosA, B2.sinA, C(C_ROTA), t_q, "q")
            yield from rope(KT, 8, B2.cosA, B2.sinA, C(C_ROTA), t_k, "k")
            tk_["ropes"] = True
            units = [([g, g + 1, g + 2, g + 3], 128, 0) for g in (0, 4)] + [([g, g + 1], 256, 1) for g in (0, 2, 4, 6)]

            def qk(u, q, o, after, mark):
                hs, wd, n = u
                return mm(o, QT[:, hs[q], n * 128:n * 128 + 128], KT[:, hs[q], 0:wd], True, True,
                          after=after + [tk_["q"], tk_["k"]], mark=mark)

            def mask(u):
                return keep[u[2]].unsqueeze(1).broadcast_to([128, len(u[0]), u[1]])

            def pv(u, pt, t_pt, ob):
                hs, wd, n = u
                nt, nh = wd // 128, len(hs)
                for q in range(4):
                    i, kt = q // nt, q % nt
                    k = mm(bank[ob][:, i * 128:(i + 1) * 128], VV[:, kt, hs[i] * 128:(hs[i] + 1) * 128], pt[:, q * 128:(q + 1) * 128],
                           kt == 0, kt == nt - 1, after=[t_pt, free[ob], t_gate["v"]], mark=(q == 3))
                ga = GA[:, hs[0]:hs[0] + nh, n * 128:n * 128 + 128]
                free[ob] = V(ve.tensor_tensor, ga, ga, v3(bank[ob][:, 0:nh * 128], nh), ALU.mult, after=[k, t_gate["ga"]])
                return k
            yield from attend(units, bufs, st, pTb, ((2, 3), (4,), (5,)), qk, mask, 128.0 ** -0.5, pv, rows_ready=tk_["keep"])
            tk_["at"] = V.last

        prm = B2.prm[0:88, :]
        xr_v = xr_d.rearrange("(n c) t -> c n t", c=88)
        hr_v = hr_d.rearrange("(n c) t -> c n t", c=88)
        hr_out = []

        def rnn_steps():
            g_free = [tk_["keep"], tk_["idx"], V.last, A.last, PE.last]
            for g in range(4):
                t_l = small([(XS, xr_v[:, 4 * g:4 * g + 4, :]),
                             (WR[:, 0], p["w_rg_2"][l].rearrange("n c d -> c n d")[:, 4 * g:4 * g + 4, :]),
                             (WR[:, 1], p["w_ig_2"][l].rearrange("n c d -> c n d")[:, 4 * g:4 * g + 4, :])], after=[t_xr, g_free])
                yield
                for j in range(4):
                    n = 4 * g + j
                    V(ve.tensor_scalar, XC[:, j, :], XS[:, j, :], prm[:, 64 * l + 48 + n:64 * l + 49 + n],
                      prm[:, 128 + 16 * l + n:129 + 16 * l + n], ALU.mult, ALU.add, after=[t_l, g_free, hr_out])
                for s in (1, 2, 3):
                    kk = V.last
                    for j in range(4):
                        n = 4 * g + j
                        cidx = 64 * l + 16 * (3 - s) + n
                        V(ve.scalar_tensor_tensor, XC[:, j, s:], XS[:, j, 0:T - s], prm[:, cidx:cidx + 1], XC[:, j, s:],
                          ALU.mult, ALU.add, after=[(kk[0], kk[1] - 3 + j)])
                t_xc = V.last
                yield
                for h in range(2):
                    for q, dst in ((0, RR), (1, II)):
                        b = 6 + q
                        for j in (0, 1):
                            k = mm(bank[b][0:88, j * T:(j + 1) * T], WR[:, q, 2 * h + j, :], XC[:, 2 * h + j, :], True, True,
                                   after=[t_xc, free[b]], mark=(j == 1))
                        for j in (0, 1):
                            n = 4 * g + 2 * h + j
                            c0 = 128 + 32 * (q + 1) + 16 * l + n
                            free[b] = A(ac.activation, dst[:, 2 * h + j, :], bank[b][0:88, j * T:(j + 1) * T], ACT.Sigmoid,
                                        bias=prm[:, c0:c0 + 1], after=[k, g_free])
                    yield
                t_si = A.last
                for j in range(4):
                    c0 = 224 + 16 * l + 4 * g + j
                    A(ac.activation, AA[:, j, :], RR[:, j, :], ACT.Exp, scale=prm[:, c0:c0 + 1], after=[t_si, g_free])
                    A(ac.activation, TH[:, j, :], RR[:, j, :], ACT.Tanh, scale=prm[:, c0:c0 + 1], after=[t_si, g_free])
                t_th = A.last
                V(ve.tensor_tensor, II, II, XC, ALU.mult, after=[t_si, t_xc])
                V(ve.tensor_scalar, RR, TH, -1.0, 1.0, ALU.mult, ALU.add, after=[t_th])
                yield
                V(ve.reciprocal, RR, RR, after=[V.last])
                V(ve.scalar_tensor_tensor, TH, TH, -2.0, RR, ALU.mult, ALU.mult, after=[V.last])
                A(ac.activation, TH, TH, ACT.Sqrt, after=[V.last])
                t_sq = A.last
                yield
                V(ve.tensor_tensor, II, II, TH, ALU.mult, after=[t_sq])
                t_u = V.last
                for j in range(4):
                    V(ve.tensor_tensor_scan, XC[:, j, :], AA[:, j, :], II[:, j, :], 0.0, ALU.mult, ALU.add, after=[t_u])
                g_free = [V.last, A.last, k]
                hr_out.append(small([(hr_v[:, 4 * g:4 * g + 4, :], XC)], after=[V.last]))
                yield
        at, rn = attention_steps(), rnn_steps()
        back.append(at)
        rm_proj(XT, w, O_V, 1024, (0, 1), lambda t, c, ps, tk: A(ac.copy, VV[:, t, 512 * c:512 * c + 512], ps, after=[tk, x_ready]),
                x_ready, ticks=2)
        t_gate["v"] = A.last

        def silu_to(dst, extra=None):
            def f(i0, ps, m, tk):
                return A(ac.activation, dst[:, i0:i0 + m, :], ps, ACT.Silu, after=[tk, extra])
            return f
        back.insert(0, rn)
        back.remove(at)
        fm_tiles(XT, w, O_GA, 8, 128, (0, 1), silu_to(GA), x_ready, ticks=1)
        t_gate["ga"] = A.last
        back.append(at)
        fm_tiles(XT, w, O_GR, 11, 128, (0, 1), silu_to(GRv, [t_xr]), x_ready, ticks=2)
        t_gr = A.last
        sgs = [None, None]
        ctr = [0]
        finish(at)
        t_at = tk_["at"]
        dump("attn", GA, [t_at])
        YA, YB, MG = QT, VV.rearrange("p a b -> p (a b)").rearrange("p (a b) -> p a b", a=8), KT
        t_ma0 = PE.last
        fm_tiles(GA, p["w_out_attn_2"][l], 0, 8, 128, (0, 1), to(YA, PE.last), t_at, ticks=2)
        t_ya = A.last

        def gate(b_side, Y, ty):
            def f(i0, ps, m, tk):
                a = ctr[0] % 2
                ctr[0] += 1
                r = A(ac.activation, sgm[:, a, :], ps, ACT.Sigmoid, after=[tk, sgs[a]])
                if not b_side:
                    V(ve.tensor_tensor, MG[:, i0:i0 + m, :], v3(sgm[:, a, :], 2), Y[:, i0:i0 + m, :], ALU.mult, after=[r, ty, t_ma0])
                else:
                    V(ve.tensor_tensor, v3(sgm[:, a, :], 2), v3(sgm[:, a, :], 2), Y[:, i0:i0 + m, :], ALU.mult, after=[r, ty])
                    V(ve.tensor_tensor, MG[:, i0:i0 + m, :], MG[:, i0:i0 + m, :], v3(sgm[:, a, :], 2), ALU.add, after=[V.last])
                sgs[a] = V.last
                return r
            return f
        fm_tiles(XT, w, O_MA, 8, 128, (0, 1), gate(False, YA, t_ya), x_ready, ticks=2)
        finish(rn)
        i_ = Ring.n % RING
        Ring.n += 1
        hv = ring[:, i_, 0:11 * T].rearrange("p (a b) -> p a b", a=11)
        SP.dma(sy.dma_start, hv, hr_d.rearrange("(i p) t -> p i t", p=128), Ring.s[i_], after=[Ring.used[i_], hr_out])
        Ring.count[i_] += 16
        t_hr = (Ring.s[i_], Ring.count[i_])
        V(ve.tensor_tensor, GRv, GRv, hv, ALU.mult, after=[t_hr, t_gr])
        Ring.used[i_] = V.last
        t_rn = V.last
        dump("rnn", GRv, [t_rn])
        fm_tiles(GRv, p["w_out_rnn_2"][l], 0, 8, 128, (0, 1), to(YB, PE.last), t_rn, per=2, kt=11)
        t_yb = A.last
        fm_tiles(XT, w, O_MB, 8, 128, (0, 1), gate(True, YB, t_yb), x_ready)
        toks = out_proj(MG, p["w_o_2"][l], (4, 5, 6, 7), V.last)
        done = []
        for t in range(2):
            for h in range(2):
                b = 4 + 2 * t + h
                xs_ = X[:, t, 512 * h:512 * h + 512]
                free[b] = V(ve.tensor_tensor, xs_, xs_, bank[b][:, :], ALU.add, after=[toks[t]])
            done.append(V.last)
        return done

    def final_norm(rows):
        Stack.at = B2.base
        g_row = take(D)
        sq = take(D)
        t_g = small([(g_row, bcast(p["final_g_2"], 128))], after=[V.last, PE.last, A.last])
        return [rms_rows(X[:, t, :], t, g_row, t_g, B2.tm[:, 8 * t:8 * t + 8], sq, rows[t]) for t in range(2)]

    t_band = band()
    t_xt, rows = gdn(t_x0)
    dump("x_a", X, rows)
    done = rows
    if stop >= 2:
        loaded = swa_loads([V.last, PE.last, A.last])
        t_xt, rows = ffn(t_xt)
        dump("x_b", X, rows)
    if stop >= 3:
        t_xt, rows = swa(t_xt, loaded)
        dump("x_c", X, rows)
    if stop >= 4:
        rows = moe(t_xt, rows, second_setup())
        dump("x_d", X, rows)
    if stop >= 5:
        rows = second(0, rows)
        dump("x_e", X, rows)
    if stop >= 6:
        rows = second(1, rows)
        rows = final_norm(rows)
    done = rows

    ov = out.rearrange("o (a p) d -> p (o a) d", p=128)
    t_out = small([(ov, X)], after=done, q=SP, name="s_out")
    SP.wait(t_out)

    with nc.Block() as block:
        @block.sync
        def _(e):
            emit(e, SP.q)

        @block.gpsimd
        def _(e):
            emit(e, G.q)

        @block.tensor
        def _(e):
            emit(e, PE.q)

        @block.scalar
        def _(e):
            emit(e, A.q)

        @block.vector
        def _(e):
            emit(e, V.q)


_INS = ['x', 'a_w_in', 'a_conv_w', 'a_a_log', 'a_dt_bias', 'a_norm_w', 'a_w_out', 'b_w_in', 'b_b_in', 'b_sinks',
        'b_w_out', 'rel_bias', 'ffn_w_gate', 'ffn_w_up', 'ffn_w_down', 'moe_router', 'moe_w_gate', 'moe_w_up',
        'moe_w_down', 'ln_g', 'ln_b', 'positions_2', 'norm_g_2', 'w_in_2', 'conv_w_2', 'conv_b_2', 'w_rg_2', 'b_rg_2',
        'w_ig_2', 'b_ig_2', 'lru_lambda_2', 'w_out_attn_2', 'w_out_rnn_2', 'w_o_2', 'final_g_2']

_BUCKET = [b for b, n in enumerate(
    [1, 1, 1, 1, 1, 1, 1, 1, 1, 1, 1, 1, 1, 1, 1, 1, 3, 2, 3, 3, 4, 4, 5, 6, 6, 7, 8, 10, 10, 12, 14, 15]) for _ in range(n)]


def constants():
    import numpy as np
    i = np.arange(128)
    f = np.float32
    col, row = i[None, :], i[:, None]
    eye = (row == col).astype(f)

    def rot(n):
        m = np.zeros((128, 128), f)
        for o in range(128):
            b, r = o // n * n, o % n
            if r < n // 2:
                m[b + r + n // 2, o] = -1.0
            else:
                m[b + r - n // 2, o] = 1.0
        return m
    main = [eye, np.ones((128, 128), f), rot(128), rot(64), (col <= row).astype(f), (row < col).astype(f),
            np.broadcast_to(col, (128, 128)).astype(f)]
    same = (row // 64 == col // 64)
    gdn = [(same & (row <= col)).astype(f), (same & (row > col)).astype(f), same.astype(f)]
    for lv in range(6):
        gdn.append(((row >> (lv + 1) == col >> (lv + 1)) & ((row >> lv) % 2 == 1) & ((col >> lv) % 2 == 0)).astype(f))
    oh = np.zeros((32, 384), f)
    em = np.full((16, 384), NEG, f)
    for y in range(128, 256):
        oh[_BUCKET[255 - y], y] = 1.0
        em[:, y] = 0.0
    ia = f(10000.0) ** (-np.arange(0, 128, 2, dtype=f) / f(128))
    ii = f(10000.0) ** (-np.arange(0, 64, 2, dtype=f) / f(64))
    rope = np.stack([np.tile(ia, 2), np.tile(ii, 4), np.full(128, np.pi / 2, f), np.zeros(128, f)], 1).astype(f)
    return {"c_main": np.concatenate(main, 1), "c_gdn": np.concatenate(gdn, 1), "c_oh": oh, "c_em": em, "c_rope": rope}


_CONSTS = ["c_main", "c_gdn", "c_oh", "c_em", "c_rope"]


def kernel(**inputs):
    import numpy as _np
    import concourse.bacc as _bacc
    from concourse import mybir as _mybir
    from concourse.bass_utils import run_bass_kernel_spmd as _run

    nc = _bacc.Bacc("TRN2", target_bir_lowering=False, num_devices=1)
    table = constants()
    arrays, args = {}, {}
    for name in _INS + _CONSTS:
        a = _np.ascontiguousarray(inputs[name] if name in _INS else table[name])
        arrays[f"in_{name}_dram"] = a
        args[name] = nc.dram_tensor(f"in_{name}_dram", a.shape, _mybir.dt.from_np(a.dtype), kind="ExternalInput").ap()
    out = nc.dram_tensor("out_0_dram", (1, 256, 1024), _mybir.dt.float32, kind="ExternalOutput").ap()
    program(nc, args, out)
    r = _run(nc, [arrays], core_ids=[0])
    return r.results[0]["out_0_dram"]
```

```python
from contextlib import ExitStack

import concourse.bass as bass
from concourse import mybir
from concourse.alu_op_type import AluOpType as ALU

F32 = mybir.dt.float32
F32R = mybir.dt.float32r
I32 = mybir.dt.int32
U32 = mybir.dt.uint32
ACT = mybir.ActivationFunctionType
ALL = slice(None)
AX_X = mybir.AxisListType.X

T = 256
D = 1024
ALPHA = 4.0 ** 0.25
LN_EPS = 1e-5
EPS = 1e-6
NEG = -1.0e30
RAW = 6
PIECES = 5
WORK = 26560
NE = 8
FE = 3584

C_ID, C_ONE, C_ROTA, C_ROTI, C_TRIL, C_LT, C_IOTA = range(7)
G_CUM, G_STRICT, G_BLOCK, G_LEVEL = 0, 1, 2, 3


class Queue:

    def __init__(self, sem):
        self.sem, self.n, self.q, self.seen = sem, 0, [], {}

    def wait(self, *tokens):
        for t in tokens:
            if t is None:
                continue
            if isinstance(t, list):
                self.wait(*t)
                continue
            sem, val = t
            if self.seen.get(sem.name, 0) < val:
                self.seen[sem.name] = val
                self.q.append(("wait", sem, val))

    def __call__(self, fn, *args, after=(), mark=True, **kw):
        self.wait(*after)
        if mark:
            self.n += 1
        self.q.append(("op", fn, args, kw, self.sem if mark else None, 1))
        return (self.sem, self.n)

    def dma(self, fn, out, in_, sem, after=(), **kw):
        self.wait(*after)
        self.q.append(("op", fn, (out, in_), kw, sem, 16))

    @property
    def last(self):
        return (self.sem, self.n) if self.n else None


def emit(eng, q):
    for item in q:
        if item[0] == "wait":
            eng.wait_ge(item[1], item[2])
        elif item[0] == "op":
            ins = item[1](*item[2], **item[3])
            if item[4] is not None:
                ins.then_inc(item[4], item[5])
        else:
            flag = eng.value_load(item[1])
            with eng.If(flag > 0):
                emit(eng, item[2])


def program(nc, p, out, debug=None, stop=99):
    plans, made = {"main": [], "more": []}, {}
    with ExitStack() as ctx:
        for final in (False, True):
            _program(nc, ctx, p, out, debug or {}, stop, plans, made, final)


def _program(nc, ctx, p, out, debug, stop, plans, made, final):
    def once(name, make):
        if name not in made:
            made[name] = make()
        return made[name]

    def sem(name):
        return once(name, lambda: ctx.enter_context(nc.semaphore(name)))

    def sbuf(name, shape, dtype):
        return once(name, lambda: ctx.enter_context(nc.sbuf_tensor(name, shape, dtype)))

    def dram(name, shape):
        return once(name, lambda: nc.dram_tensor(name, shape, F32, kind="Internal").ap())

    raw = sbuf("raw", [128, RAW, 2048], F32)
    parts_ = sbuf("parts", [128, PIECES, 2, 1024], F32R)
    cols_ = sbuf("cols", [128, 2, 8 * T], F32R)
    work = sbuf("work", [128, WORK], F32)
    bank = [once(f"bank{i}", lambda i=i: ctx.enter_context(nc.psum_tensor(f"bank{i}", [128, 512], F32))) for i in range(8)]

    PE, V, A, G, SP = (Queue(sem(n)) for n in ("s_pe", "s_dve", "s_act", "s_pool", "s_sp"))
    te, ve, ac, gp, sy = nc.tensor, nc.vector, nc.scalar, nc.gpsimd, nc.sync
    queues = {"PE": PE, "V": V, "A": A, "G": G, "SP": SP}

    class Stack:
        at = 0

    def take(n):
        a = Stack.at
        Stack.at += n
        assert Stack.at <= WORK, Stack.at
        return work[:, a:a + n]

    def take_top(n, at):
        return work[:, at - n:at]

    def v3(ap, a):
        return ap.rearrange("p (a b) -> p a b", a=a)

    def v4(ap, a, b):
        return ap.rearrange("p (a b c) -> p a b c", a=a, b=b)

    free = [None] * 8

    back = []

    def tick(n=1):
        for _ in range(n):
            if not back:
                return
            g = back.pop(0)
            try:
                next(g)
                back.append(g)
            except StopIteration:
                pass

    def finish(*gens):
        for g in gens:
            for _ in g:
                pass
            if g in back:
                back.remove(g)

    def split(dst, src, after=()):
        k = A(ac.copy, dst[0], src, after=after)
        return V(ve.tensor_tensor, dst[1], src, dst[0].bitcast(F32), ALU.subtract, after=[*after, k])

    class Stream:

        def __init__(self, plan, prefix, before):
            self.plan = plan
            self.pos = self.loaded = 0
            self.sems = [sem(f"{prefix}{i}") for i in range(RAW)]
            self.count = [0] * RAW
            self.raw_free = [before] * RAW
            self.held = [None] * RAW
            self.slots = {i: before for i in range(PIECES)}
            self.next = (0, 0)
            self.at = {}
            self.limit = PIECES
            self.bars = 0

        def open(self, shape, parts, cuts=None):
            if not final:
                self.plan.append(("chunk", shape, parts, cuts, self.limit))
            i = self.pos
            assert self.plan[i][1] == shape
            self.pos += 1
            self.pump()
            return [(i, j) for j in range(len(cuts) if cuts else 1)]

        def barrier(self):
            if not final:
                self.plan.append(("bar",))
            assert self.plan[self.pos][0] == "bar"
            self.pos += 1

        def restrict(self, n):
            for i in range(n, self.limit):
                assert i in self.slots
                del self.slots[i]
            for i in range(self.limit, n):
                self.slots[i] = [PE.last, V.last, A.last]
            self.limit = n

        def view(self, i):
            _, (a, b), _, _, _ = self.plan[i]
            return raw[:, self.at[i], 0:a * b].rearrange("p (a b) -> p a b", a=a)

        def pump(self):
            moved = True
            while moved:
                moved = False
                i = self.loaded
                if i < len(self.plan):
                    if self.plan[i][0] == "bar":
                        if self.pos > i:
                            self.loaded += 1
                            moved = True
                            continue
                    else:
                        free_ = [s for s in range(RAW) if self.held[s] is None]
                        if free_:
                            s = min(free_, key=lambda s: self.stamp(s))
                            _, (a, b), parts, cuts, lim = self.plan[i]
                            self.at[i] = s
                            self.held[s] = i
                            dst = raw[:, s, 0:a * b].rearrange("p (a b) -> p a b", a=a)
                            for cut, src in parts:
                                SP.dma(sy.dma_start, cut(dst), src, self.sems[s], after=[self.raw_free[s]])
                                self.count[s] += 16
                            self.arrive[i] = (self.sems[s], self.count[s])
                            self.loaded += 1
                            moved = True
                i, j = self.next
                if i < self.loaded:
                    if self.plan[i][0] == "bar" or self.plan[i][3] is None:
                        self.next = (i + 1, 0)
                        moved = True
                        continue
                    cuts, lim = self.plan[i][3], self.plan[i][4]
                    ok = [x for x in self.slots if x < lim]
                    if ok:
                        x = min(ok, key=lambda x: self.order.get(x, -1))
                        used = self.slots.pop(x)
                        src = cuts[j](self.view(i))
                        a, b = src.shape[1], src.shape[2]
                        dst = tuple(v3(parts_[:, x, q, 0:a * b], a) for q in range(2))
                        t = split(dst, src, after=[used, self.arrive[i]])
                        self.ready[i, j] = (x, dst, t)
                        moved = True
                        if j + 1 == len(cuts):
                            self.release_raw(i, [A.last, t])
                            self.next = (i + 1, 0)
                        else:
                            self.next = (i, j + 1)

        def stamp(self, s):
            return self.stamps.get(s, -1)

        def release_raw(self, i, tokens):
            s = self.at[i]
            self.held[s] = None
            self.raw_free[s] = tokens
            self.stamps[s] = i

        def get(self, key):
            self.pump()
            _, dst, t = self.ready[key]
            return dst, t

        def done(self, key, token):
            x, _, _ = self.ready.pop(key)
            self.order[x] = self.tick = self.tick + 1
            if x < self.limit:
                self.slots[x] = token
            self.pump()

        def get_raw(self, key):
            self.pump()
            return self.view(key[0]), self.arrive[key[0]]

        def done_raw(self, key, token):
            self.release_raw(key[0], token)
            self.pump()

    def new_stream(name, prefix, before):
        s = Stream(plans[name], prefix, before)
        s.arrive, s.ready, s.order, s.stamps, s.tick = {}, {}, {}, {}, 0
        return s
    streams = {}
    streams["main"] = streams["now"] = new_stream("main", "s_raw", None)

    def whole(d):
        return d

    def rows_of(src, k0, k1):
        return src[128 * k0:128 * k1, :].rearrange("(k p) c -> p k c", p=128)

    class Misc:
        n = 0

    def small(pairs, after=(), name=None, q=None):
        s = sem(name or f"s_m{Misc.n}")
        Misc.n += 1
        for dst, src in pairs:
            (q or G).dma((sy if q is SP else ac if q is A else gp).dma_start, dst, src, s, after=after)
        return (s, 16 * len(pairs))

    def mm(o, l, r, start, stop, after=(), mark=False, skip=False):
        return PE(te.matmul, o, l, r, start=start, stop=stop, skip_group_check=skip, after=after, mark=mark)

    def mm3(o, l, r, start, stop, after=(), mark=False):
        PE(te.matmul, o, l[0], r[0], start=start, stop=False, after=after, mark=False)
        PE(te.matmul, o, l[0], r[1], start=False, stop=False, mark=False)
        return PE(te.matmul, o, l[1], r[0], start=False, stop=stop, mark=mark)

    def sl(pair, *idx):
        return tuple(x[idx] for x in pair)

    def tr(o, i, after=(), mark=False):
        n = i.shape[0]
        return PE(te.transpose, o, i, ident[0:n, 0:n], after=after, mark=mark)

    def dump(name, ap, after):
        if name in debug:
            t = small([(debug[name], ap)], after=after, q=SP)
            dumps.append(t)
            for q in (PE, V, A, G):
                q.wait(t)
    dumps = []

    consts = take(7 * 128)
    X = v3(take(2 * D), 2)
    XT = tuple(v3(cols_[:, i, :], 8) for i in range(2))
    LNC = take(80)
    CWB = take(74)
    vb, sk = take(128), take(16)

    def C(k):
        return consts[:, k * 128:(k + 1) * 128]
    ident, ones = C(C_ID), C(C_ONE)
    base = Stack.at

    t_const = small([(consts, p["c_main"])], q=SP)
    t_x = small([(X, p["x"].rearrange("o (a p) d -> p (o a) d", p=128))], q=SP)

    def rows_to_cols(src, dst, after, banks=(6, 7)):
        done = []
        for t in range(2):
            for g in range(2):
                b = banks[g]
                for j in range(4):
                    k = 4 * g + j
                    tk = tr(bank[b][:, j * 128:(j + 1) * 128], src[:, t, k * 128:(k + 1) * 128],
                            after=[after[t], free[b]] if j == 0 else (), mark=(j == 3))
                free[b] = split(sl(dst, ALL, slice(4 * g, 4 * g + 4), slice(t * 128, (t + 1) * 128)), v3(bank[b][:, :], 4), [tk])
                done.append(free[b])
        return done

    def fm_tiles(xt, src, c0, n, banks, evac, x_ready, kt=8, ticks=0, split_=True):
        W = streams["now"]
        per = 2 if kt == 8 else 1
        for nb, i in enumerate(range(0, n, 2)):
            m = min(2, n - i)
            b = banks[nb % len(banks)]
            keys = []
            for j in range(0, m, per):
                c = c0 + (i + j) * 128
                w_ = min(per, m - j)
                cuts = [lambda d, q=q: d[:, :, q * 128:(q + 1) * 128] for q in range(w_)] if split_ else None
                keys.append(W.open((kt, w_ * 128), [(whole, rows_of(src, 0, kt)[:, :, c:c + w_ * 128])], cuts))
            for j in range(m):
                key = keys[j // per][j % per if split_ else 0]
                (w, t_w) = W.get(key) if split_ else W.get_raw(key)
                o = bank[b][:, j * T:(j + 1) * T]
                for k in range(kt):
                    aft = [t_w, free[b], x_ready] if k == 0 else ()
                    if split_:
                        tk = mm3(o, sl(w, ALL, k), sl(xt, ALL, k), k == 0, k == kt - 1, aft, k == kt - 1)
                    else:
                        q = j % per
                        tk = mm(o, w[:, k, q * 128:(q + 1) * 128], xt[:, k, :], k == 0, k == kt - 1, aft, k == kt - 1)
                if split_:
                    W.done(key, tk)
                elif j % per == per - 1 or j == m - 1:
                    W.done_raw(key, tk)
                if j + 1 < m:
                    tick(ticks // 2)
            free[b] = evac(i, bank[b][:, 0:m * T].rearrange("p (a b) -> p a b", a=m), m, tk)
            tick(ticks - ticks // 2 if m == 2 else ticks)

    def rm_proj(xt, src, c0, n, banks, evac, x_ready, ticks=0):
        W = streams["now"]
        for c in range(n // 512):
            for kh in range(2):
                keys = W.open((4, 512), [(whole, rows_of(src, 4 * kh, 4 * kh + 4)[:, :, c0 + c * 512:c0 + (c + 1) * 512])],
                              [lambda d, q=q: d[:, 2 * q:2 * q + 2, :] for q in range(2)])
                for q, key in enumerate(keys):
                    w, t_w = W.get(key)
                    for i in range(2):
                        k = 4 * kh + 2 * q + i
                        for t in range(2):
                            tk = mm3(bank[banks[t]][:, :], sl(xt, ALL, k, slice(t * 128, (t + 1) * 128)), sl(w, ALL, i), k == 0, k == 7,
                                     [t_w, free[banks[t]], x_ready], mark=(i == 1))
                            if k == 7:
                                tok_t = tk
                                if t == 0:
                                    tok0 = tk
                    W.done(key, tk)
            for t, tk in ((0, tok0), (1, tok_t)):
                free[banks[t]] = evac(t, c, bank[banks[t]][:, :], tk)
                tick(ticks)

    def stats(y, tmp, ready):
        st, mv, rs = tmp[:, 0:12], tmp[:, 12:14], tmp[:, 14:16]
        for h in range(2):
            V(ve.bn_stats, st[:, 6 * h:6 * h + 6], y[:, 512 * h:512 * h + 512], after=[ready])
        V(ve.bn_aggr, mv, v3(st, 2), after=[V.last])
        V(ve.tensor_scalar, rs[:, 0:1], mv[:, 1:2], LN_EPS, None, ALU.add, after=[V.last])
        k = A(ac.activation, rs[:, 1:2], rs[:, 0:1], ACT.Sqrt, after=[V.last])
        V(ve.reciprocal, rs[:, 0:1], rs[:, 1:2], after=[k])
        return mv[:, 0:1], rs[:, 0:1]

    def cols_scaled(src, t, gcol, bcol, ready, banks=(6, 7)):
        for g in range(2):
            b = banks[g]
            for j in range(4):
                k_ = 4 * g + j
                tk = tr(bank[b][:, j * 128:(j + 1) * 128], src[:, k_ * 128:(k_ + 1) * 128],
                        after=[ready, free[b]] if j == 0 else (), mark=(j == 3))
            for j in range(4):
                k_ = 4 * g + j
                o = bank[b][:, j * 128:(j + 1) * 128]
                gc_, bc_ = gcol[:, k_:k_ + 1], (bcol[:, k_:k_ + 1] if bcol is not None else 0.0)
                if g == 0:
                    if bcol is None:
                        V(ve.tensor_scalar, o, o, gc_, None, ALU.mult, after=[tk])
                    else:
                        V(ve.tensor_scalar, o, o, gc_, bc_, ALU.mult, ALU.add, after=[tk])
                elif bcol is None:
                    A(ac.activation, o, o, ACT.Copy, scale=gc_, after=[tk])
                else:
                    A(ac.activation, o, o, ACT.Identity, bias=bc_, scale=gc_, after=[tk])
            last = (V if g == 0 else A).last
            free[b] = split(sl(XT, ALL, slice(4 * g, 4 * g + 4), slice(t * 128, (t + 1) * 128)), v3(bank[b][:, :], 4), [last, ready])

    def residual_norm(add, ln, gb, t_gb, tmps, cols=True):
        gcol, bcol = LNC[:, 8 * ln:8 * ln + 8], LNC[:, 32 + 8 * ln:40 + 8 * ln]
        xt_free = PE.last
        ready = []
        for t in range(2):
            y = X[:, t, :]
            mu, rs = stats(y, tmps[t], add(t))
            ready.append(V(ve.tensor_scalar, y, y, mu, rs, ALU.subtract, ALU.mult, after=[V.last]))
        for t in range(2):
            if cols:
                cols_scaled(X[:, t, :], t, gcol, bcol, [ready[t], xt_free])
        t_xt = [V.last, A.last]
        rows = []
        for t in range(2):
            y = X[:, t, :]
            V(ve.tensor_tensor, y, y, gb[:, 0, :], ALU.mult, after=[ready[t], t_gb, PE.last])
            rows.append(V(ve.tensor_tensor, y, y, gb[:, 1, :], ALU.add, after=[V.last]))
        return t_xt, rows

    def add_banks(banks4, toks):
        def add(t):
            for h in range(2):
                b = banks4[2 * t + h]
                xs = X[:, t, 512 * h:512 * h + 512]
                free[b] = V(ve.scalar_tensor_tensor, xs, xs, ALPHA, bank[b][:, :], ALU.mult, ALU.add, after=[toks[t], V.last])
            return V.last
        return add

    def bcast(src, n):
        return src.partition_broadcast(n)

    bi = p["b_b_in"][0]
    pw = work[:, WORK - 1400:WORK]
    pr1, pr2, oh, em, rb = pw[:, 0:128], pw[:, 128:256], pw[:, 256:640], pw[:, 640:1024], pw[:, 1024:1040]
    t_p1 = small([(pr1[0:32, :], p["ln_g"].rearrange("l i (a b) -> (l i a) b", b=128)),
                  (pr1[32:64, :], p["ln_b"].rearrange("l i (a b) -> (l i a) b", b=128)),
                  (pr1[64:80, :], p["norm_g_2"].rearrange("l (a b) -> (l a) b", b=128)),
                  (pr2[0:64, :], p["a_conv_w"][0].rearrange("j (i c) -> (j i) c", c=128)),
                  (pr2[64:72, :], bi[0:1024].rearrange("(a b) -> a b", b=128)),
                  (pr2[72:73, 0:64], bi[1024:1088].unsqueeze(0)), (pr2[72:73, 64:128], bi[1024:1088].unsqueeze(0)),
                  (pr2[73:74, 0:64], bi[1088:1152].unsqueeze(0)), (pr2[73:74, 64:128], bi[1088:1152].unsqueeze(0))], q=A)
    SP.wait(t_p1)
    t_x0 = rows_to_cols(X, XT, [[t_const, t_x]] * 2)
    k = tr(bank[5][:, 0:80], pr1[0:80, :], after=[t_p1])
    k = tr(bank[5][:, 128:202], pr2[0:74, :], mark=True)
    V(ve.tensor_copy, LNC, bank[5][:, 0:80], after=[k])
    free[5] = t_par = V(ve.tensor_copy, CWB, bank[5][:, 128:202])

    def narrow(bk, src, n, x_ready, b):
        W = streams["now"]
        key, = W.open((8, n), [(whole, src)], [whole])
        w, t_w = W.get(key)
        for t in range(2):
            for kk in range(8):
                k = mm3(bk[:, n * t:n * t + n], sl(XT, ALL, kk, slice(t * 128, (t + 1) * 128)), sl(w, ALL, kk), kk == 0, kk == 7,
                        [t_w, x_ready, free[b]], mark=(kk == 7))
        W.done(key, k)
        return k

    def gdn(x_ready):
        Stack.at = base
        cg = take(9 * 128)

        def CG(k):
            return cg[:, k * 128:(k + 1) * 128]
        nw = take(128)
        ab = take(16)
        cw = CWB
        gates = take(13 * 16)
        sq = v3(take(2 * T), 2)
        small_t = take(32)
        qkv = v3(take(16 * T), 16)
        Z = v3(take(2 * D), 2)
        t_p = small([(ab[:, 0:8], bcast(p["a_a_log"][0], 128)), (ab[:, 8:16], bcast(p["a_dt_bias"][0], 128)),
                     (cg, p["c_gdn"]), (nw, bcast(p["a_norm_w"][0], 128))], q=A)
        silu_done = []

        def conv(i0, ps, m, tk):
            for j in range(m):
                first_tap = A(ac.activation, qkv[:, i0 + j, :], ps[:, j, :], ACT.Copy, scale=cw[:, 48 + i0 + j:49 + i0 + j], after=[tk, t_par])
            for s in (1, 2, 3):
                kk = V.last if s > 1 else first_tap
                for j in range(m):
                    i = i0 + j
                    o = qkv[:, i, :]
                    V(ve.scalar_tensor_tensor, o[:, s:], ps[:, j, 0:T - s], cw[:, 16 * (3 - s) + i:16 * (3 - s) + i + 1],
                      o[:, s:], ALU.mult, ALU.add, after=[(kk[0], kk[1] - m + 1 + j) if s > 1 else kk])
            kk = V.last
            A(ac.activation, qkv[:, i0:i0 + m, :], qkv[:, i0:i0 + m, :], ACT.Silu, after=[kk])
            silu_done.append(A.last)
            return kk
        wi = p["a_w_in"][0]
        fm_tiles(XT, wi, 0, 8, (0, 1, 2, 3), conv, x_ready)

        t_band.extend(band())
        k = narrow(bank[4], rows_of(wi, 0, 8)[:, :, 3072:3088], 16, x_ready, 4)
        bav = v3(gates[:, 0:32], 2)
        free[4] = V(ve.tensor_copy, bav, v3(bank[4][:, 0:32], 2), after=[k])
        beta = v3(gates[:, 32:48], 2)
        g_, gc, egc, kds, t1, t2, t3 = (v3(gates[:, 48 + 16 * i:64 + 16 * i], 2) for i in range(7))
        dl = v3(gates[:, 160:192], 4)
        ea = gates[:, 192:200]
        gv = gates[:, 48:64]
        tg = {}

        def gate_steps():
            A(ac.activation, beta, bav[:, :, 0:8], ACT.Sigmoid, after=[V.last])
            tg["beta"] = A.last
            abx = ab[:, 8:16].unsqueeze(1).broadcast_to([128, 2, 8])
            V(ve.tensor_tensor, t1, bav[:, :, 8:16], abx, ALU.add, after=[V.last, t_p])
            V(ve.tensor_scalar, t2, t1, -1.0, None, ALU.mult, after=[V.last])
            V(ve.tensor_tensor, t2, t1, t2, ALU.min, after=[V.last])
            k = A(ac.activation, t2, t2, ACT.Exp, after=[V.last])
            A(ac.activation, ea, ab[:, 0:8], ACT.Exp, after=[t_p])
            t_ea = A.last
            log1p(t2, t3, g_, k)
            V(ve.tensor_scalar, t1, t1, 0.0, None, ALU.max, after=[V.last])
            V(ve.tensor_tensor, t1, t1, t2, ALU.add, after=[V.last])
            V(ve.tensor_scalar, ea, ea, -1.0, None, ALU.mult, after=[t_ea])
            t_g = V(ve.tensor_tensor, g_, t1, ea.unsqueeze(1).broadcast_to([128, 2, 8]), ALU.mult, after=[V.last])
            yield
            mm(bank[4][:, 0:16], CG(G_CUM), gv, True, True, after=[t_g, free[4]])
            mm(bank[4][:, 16:32], CG(G_BLOCK), gv, True, True)
            for c in range(4):
                r = 64 * (c % 2)
                k = mm(bank[6 + c % 2][:, 8 * (c // 2):8 * (c // 2) + 8], ones[r:r + 64, :], g_[r:r + 64, c // 2, :], True, True,
                       mark=(c == 3), after=[free[6 + c % 2]])
            V(ve.tensor_copy, gc, v3(bank[4][:, 0:16], 2), after=[k])
            V(ve.tensor_tensor, kds, v3(bank[4][:, 16:32], 2), gc, ALU.subtract, after=[V.last])
            free[4] = V.last
            A(ac.activation, kds, kds, ACT.Exp, after=[V.last])
            A(ac.activation, egc, gc, ACT.Exp)
            for c in range(2):
                free[6 + c] = A(ac.activation, dl[:, c::2, :], v3(bank[6 + c][:, 0:16], 2), ACT.Exp)
            V(ve.tensor_tensor, egc, egc, beta, ALU.mult, after=[A.last])
            tg["gates"] = V.last

        def norm_steps():
            t_q = None
            for i in range(0, 8, 2):
                b = 6 + (i // 2) % 2
                x2 = qkv[:, i:i + 2, :]
                xf = x2.rearrange("p a b -> p (a b)")
                k = A(ac.activation, sq, x2, ACT.Square, after=[silu_done[i // 2], t_q])
                t_q = mm(bank[b][:, :], ones, sq.rearrange("p a b -> p (a b)"), True, True, mark=True, after=[k, free[b]])
                V(ve.tensor_scalar, bank[b][:, :], bank[b][:, :], EPS, None, ALU.add, after=[t_q])
                k = A(ac.activation, bank[b][:, :], bank[b][:, :], ACT.Sqrt, after=[V.last])
                V(ve.reciprocal, bank[b][:, :], bank[b][:, :], after=[k])
                free[b] = V(ve.scalar_tensor_tensor, xf, xf, 128.0 ** -0.5 if i < 4 else 1.0, bank[b][:, :],
                            ALU.mult, ALU.mult, after=[V.last])
                yield
            tg["qk"] = V.last
        gs, ns = gate_steps(), norm_steps()
        back.extend([gs, ns])
        fm_tiles(XT, wi, 1024, 8, (0, 1, 2, 3), lambda i0, ps, m, tk: conv(i0 + 8, ps, m, tk), x_ready, ticks=4)
        finish(gs, ns)
        t_qk, t_gates, t_beta = tg["qk"], tg["gates"], tg["beta"]
        dump("gdn_qkv", qkv, [t_qk, A.last])
        dump("gdn_gc", gc, [t_gates])

        def heads(ap):
            return ap.rearrange("p (h e) -> p h e", e=128)
        for q_ in (V, A, PE):
            q_.wait(t_band[0])
        AQ, AM, TM, KB, VB, QD = (heads(take(2048)) for _ in range(6))
        KD = AM
        S, KR = heads(X[:, 0, :]), heads(X[:, 1, :])
        BB = [heads(take(512)) for _ in range(4)]
        OT = XT
        qk_flat = qkv.rearrange("p a b -> p (a b)")
        NW, TT = heads(qk_flat[:, 0:2048]), heads(qk_flat[:, 2048:4096])
        ready = {}

        def rows_steps():
            for t in range(2):
                ts = slice(t * 128, (t + 1) * 128)
                for kh in range(4):
                    k = tr(bank[4][:, kh * 128:(kh + 1) * 128], qkv[:, 4 + kh, ts], after=[t_qk, free[4], t_par], mark=(kh == 3))
                free[4] = A(ac.copy, KR[:, 4 * t:4 * t + 4, :], v3(bank[4][:, :], 4), after=[k])
                for h in range(8):
                    V(ve.tensor_scalar, KB[:, 8 * t + h, :], KR[:, 4 * t + h // 2, :], egc[:, t, h:h + 1], None, ALU.mult, after=[free[4], t_gates])
                yield
                for hg in range(2):
                    for j in range(4):
                        k = tr(bank[5][:, j * 128:(j + 1) * 128], qkv[:, 8 + 4 * hg + j, ts], after=[silu_done, free[5]], mark=(j == 3))
                    for j in range(4):
                        h = 4 * hg + j
                        A(ac.activation, VB[:, 8 * t + h, :], bank[5][:, j * 128:(j + 1) * 128], ACT.Copy, scale=beta[:, t, h:h + 1],
                          after=[k, t_beta])
                    free[5] = A.last
                    yield
            ready["v"] = PE.last

        def decay_steps():
            for t in range(2):
                ts = slice(t * 128, (t + 1) * 128)
                for kh in range(4):
                    kt_ = qkv[:, 4 + kh, ts]
                    mm(bank[2][:, kh * 128:(kh + 1) * 128], kt_, kt_, True, True, after=[free[2], free[3], t_qk])
                    t_kk = mm(bank[3][:, kh * 128:(kh + 1) * 128], kt_, qkv[:, kh, ts], True, True, mark=(kh == 3))
                for hg in range(2):
                    gi = 2 * t + hg
                    hs = slice(4 * gi, 4 * gi + 4)
                    b = 6 + hg
                    bb = BB[gi]
                    for j in range(4):
                        V(ve.tensor_scalar, bb[:, j, :], ones, g_[:, t, 4 * hg + j:4 * hg + j + 1], None, ALU.mult, after=[t_gates])
                    for j in range(4):
                        k = mm(bank[b][:, j * 128:(j + 1) * 128], bb[:, j, :], CG(G_CUM), True, True, after=[V.last, free[b]], mark=(j == 3))
                    R = v3(bank[b][:, :], 4)
                    gcb = gc[:, t, 4 * hg:4 * hg + 4].unsqueeze(2).broadcast_to([128, 4, 128])
                    A(ac.activation, bb, R, ACT.Exp, after=[k])
                    t_er = A.last
                    V(ve.tensor_tensor, AQ[:, hs, :], R, gcb, ALU.subtract, after=[t_er])
                    free[b] = V.last
                    V(ve.tensor_scalar, AM[:, hs, :], AQ[:, hs, :], 0.0, None, ALU.max, after=[V.last])
                    V(ve.tensor_scalar, AQ[:, hs, :], AQ[:, hs, :], 0.0, None, ALU.min, after=[V.last])
                    qh = qkv[:, 2 * hg:2 * hg + 2, ts].unsqueeze(2).broadcast_to([128, 2, 2, 128])
                    V(ve.tensor_tensor, QD[:, hs, :].rearrange("p (a b) e -> p a b e", b=2), bb.rearrange("p (a b) e -> p a b e", b=2),
                      qh, ALU.mult, after=[t_er, t_qk])
                    v_ = V.last
                    A(ac.activation, AM[:, hs, :], AM[:, hs, :], ACT.Exp, scale=-1.0, after=[v_])
                    t_e2 = A.last
                    A(ac.activation, AQ[:, hs, :], AQ[:, hs, :], ACT.Exp, after=[v_])
                    t_e1 = A.last
                    yield

                    def msk(i):
                        return CG(i).unsqueeze(1).broadcast_to([128, 4, 128])
                    V(ve.tensor_tensor, AM[:, hs, :], AM[:, hs, :], msk(G_STRICT), ALU.mult, after=[t_e2])
                    V(ve.tensor_tensor, AQ[:, hs, :], AQ[:, hs, :], msk(G_CUM), ALU.mult, after=[t_e1])
                    t_m2 = V.last
                    for j in range(4):
                        h = 4 * hg + j
                        V(ve.scalar_tensor_tensor, AM[:, 8 * t + h, :], bank[2][:, (h // 2) * 128:(h // 2 + 1) * 128], beta[:, t, h:h + 1],
                          AM[:, 8 * t + h, :], ALU.mult, ALU.mult, after=[t_m2, t_beta, t_kk])
                    ready["a", gi] = V.last
                    kq = v3(bank[3][:, 256 * hg:256 * hg + 256], 2).unsqueeze(2).broadcast_to([128, 2, 2, 128])
                    V(ve.tensor_tensor, AQ[:, hs, :].rearrange("p (a b) e -> p a b e", b=2),
                      AQ[:, hs, :].rearrange("p (a b) e -> p a b e", b=2), kq, ALU.mult, after=[t_m2, t_kk])
                    free[2] = free[3] = V.last
                    yield
            ready["aq"] = V.last
        rs_, ds_ = rows_steps(), decay_steps()
        back.extend([rs_, ds_])

        def z_evac(t, c, ps, tk):
            return A(ac.activation, Z[:, t, 512 * c:512 * c + 512], ps, ACT.Silu, after=[tk])
        rm_proj(XT, wi, 2048, 1024, (0, 1), z_evac, x_ready, ticks=4)
        t_z, t_z0 = A.last, PE.last
        finish(rs_, ds_)
        dump("gdn_A", AM[:, 0:8, :], [V.last])
        dump("gdn_AQ", AQ[:, 0:8, :], [V.last])
        idb = ident.unsqueeze(1).broadcast_to([128, 4, 128])
        tt_r, b_used = [None] * 4, [None] * 4
        n1 = n2 = 0
        bset1, bset2 = (0, 1), (2, 3, 4, 5, 6, 7)
        for lv in range(6):
            t_bs, t_ms = [], []
            for gi in range(4):
                hs = slice(4 * gi, 4 * gi + 4)
                t_bs.append(V(ve.tensor_tensor, BB[gi], AM[:, hs, :], CG(G_LEVEL + lv).unsqueeze(1).broadcast_to([128, 4, 128]),
                              ALU.mult, after=[ready["a", gi], b_used[gi], tt_r[gi]]))
                b = bset1[n1 % 2]
                n1 += 1
                if lv == 0:
                    V(ve.tensor_tensor, TM[:, hs, :], idb, BB[gi], ALU.subtract, after=[V.last])
                    for j in range(4):
                        k = tr(bank[b][:, j * 128:(j + 1) * 128], BB[gi][:, j, :], after=[t_bs[gi], free[b]], mark=(j == 3))
                    free[b] = V(ve.tensor_tensor, TT[:, hs, :], idb, v3(bank[b][:, :], 4), ALU.subtract, after=[k, ready["v"]])
                    tt_r[gi] = V.last
                    b_used[gi] = k
                else:
                    for j in range(4):
                        k = mm(bank[b][:, j * 128:(j + 1) * 128], BB[gi][:, j, :], TT[:, 4 * gi + j, :], True, True,
                               after=[t_bs[gi], free[b], tt_r[gi]], mark=(j == 3))
                    free[b] = A(ac.copy, BB[gi], v3(bank[b][:, :], 4), after=[k])
                    t_ms.append(A.last)
            if lv == 0:
                continue
            for gi in range(4):
                hs = slice(4 * gi, 4 * gi + 4)
                if lv < 5:
                    b2 = bset2[n2 % 6]
                    n2 += 1
                    for j in range(4):
                        k = mm(bank[b2][:, j * 128:(j + 1) * 128], BB[gi][:, j, :], TM[:, 4 * gi + j, :], True, True,
                               after=[t_ms[gi], free[b2]], mark=(j == 3))
                b3 = bset2[n2 % 6]
                n2 += 1
                for j in range(4):
                    k3 = mm(bank[b3][:, j * 128:(j + 1) * 128], TM[:, 4 * gi + j, :], BB[gi][:, j, :], True, True,
                            after=[t_ms[gi], free[b3]], mark=(j == 3))
                b_used[gi] = k3
                free[b3] = V(ve.tensor_tensor, TT[:, hs, :], TT[:, hs, :], v3(bank[b3][:, :], 4), ALU.subtract, after=[k3])
                tt_r[gi] = V.last
                if lv < 5:
                    free[b2] = V(ve.tensor_tensor, TM[:, hs, :], TM[:, hs, :], v3(bank[b2][:, :], 4), ALU.subtract, after=[k3])
        t_inv = PE.last
        for gi in range(4):
            b = bset2[gi]
            for j in range(4):
                k = mm(bank[b][:, j * 128:(j + 1) * 128], KB[:, 4 * gi + j, :], TT[:, 4 * gi + j, :], True, True,
                       after=[tt_r[gi], free[b], ready["aq"]], mark=(j == 3))
            free[b] = A(ac.mul, NW[:, 4 * gi:4 * gi + 4, :], v3(bank[b][:, :], 4), -1.0, after=[k])
            ready["nw", gi] = A.last
        for i in range(16):
            V(ve.tensor_scalar, KD[:, i, :], KR[:, 4 * (i // 8) + (i % 8) // 2, :], kds[:, i // 8, i % 8:i % 8 + 1], None, ALU.mult, after=[t_bs])
        t_kd = V.last
        gb = v3(TM.rearrange("p a b -> p (a b)"), 2)
        t_gb = small([(gb[:, 0, :], bcast(p["ln_g"][0, 0], 128)), (gb[:, 1, :], bcast(p["ln_b"][0, 0], 128))], after=[t_inv, V.last])
        for t in range(2):
            zz = Z[:, t, :].rearrange("p (h e) -> p h e", h=8)
            V(ve.tensor_tensor, zz, zz, nw.unsqueeze(1).broadcast_to([128, 8, 128]), ALU.mult, after=[t_z, t_p])
        dump("gdn_TT", TT[:, 0:8, :], [V.last])
        def own(c, h):
            t, rs = c // 2, slice(64 * (c % 2), 64 * (c % 2) + 64)
            i = 8 * t + h
            mm(bank[h // 4][rs, (h % 4) * 128:(h % 4 + 1) * 128], TT[rs, i, rs], VB[rs, i, :], h % 4 == 0, False, skip=True,
               after=[free[h // 4], tt_r[2 * t + h // 4]], mark=(h % 4 == 3))

        O = AQ
        t_o_of = [None]

        def o_rows(t):
            sr = small_t[:, 8:16]
            ss = small_t[:, 0:8]
            Ot, Qt = O[:, 8 * t:8 * t + 8, :], QD[:, 8 * t:8 * t + 8, :]
            for hg in range(2):
                A(ac.copy, Ot[:, 4 * hg:4 * hg + 4, :], v3(bank[2 + hg][:, :], 4), after=[t_o_of[0]])
                free[2 + hg] = A.last
            yield
            V(ve.tensor_tensor, Qt, Ot, Ot, ALU.mult, after=[A.last, t_o_of[0]])
            V(ve.tensor_reduce, ss, Qt, AX_X, ALU.add, after=[V.last])
            V(ve.tensor_scalar, ss, ss, 1.0 / 128, EPS, ALU.mult, ALU.add, after=[V.last])
            A(ac.activation, sr, ss, ACT.Sqrt, after=[V.last])
            V(ve.tensor_tensor, Ot, Ot, Z[:, t, :].rearrange("p (h e) -> p h e", h=8), ALU.mult, after=[V.last])
            V(ve.reciprocal, ss, sr, after=[A.last])
            yield
            V(ve.tensor_tensor, Ot, Ot, ss.unsqueeze(2).broadcast_to([128, 8, 128]), ALU.mult, after=[V.last])
            k0 = V.last
            for g in range(2):
                b = 6 + g
                for j in range(4):
                    k = tr(bank[b][:, j * 128:(j + 1) * 128], Ot[:, 4 * g + j, :], after=[k0, free[b]], mark=(j == 3))
                free[b] = split(sl(OT, ALL, slice(4 * g, 4 * g + 4), slice(t * 128, (t + 1) * 128)), v3(bank[b][:, :], 4), [k, t_z0])
        for h in range(8):
            own(0, h)
        t_s = None
        for c in range(4):
            t, rs = c // 2, slice(64 * (c % 2), 64 * (c % 2) + 64)
            for h in range(8):
                o = bank[h // 4][rs, (h % 4) * 128:(h % 4 + 1) * 128]
                if c:
                    k = mm(o, NW[:, 8 * t + h, rs], S[:, h, :], False, h % 4 == 3, skip=True, after=[t_s, ready["nw", 2 * t + h // 4]],
                           mark=(h % 4 == 3))
                else:
                    k = PE.last
                if h % 4 == 3:
                    src, dst = v3(bank[h // 4][rs, :], 4), VB[rs, 8 * t + h - 3:8 * t + h + 1, :]
                    free[h // 4] = V(ve.tensor_copy, dst, src, after=[k]) if h == 3 else A(ac.copy, dst, src, after=[k])
            t_vn = [free[0], free[1]]
            if c:
                for h in range(8):
                    k = mm(bank[2 + h // 4][rs, (h % 4) * 128:(h % 4 + 1) * 128], QD[:, 8 * t + h, rs], S[:, h, :], h % 4 == 0, False,
                           skip=True, after=[free[2 + h // 4]], mark=(h == 7))
            if c < 3:
                for h in range(8):
                    b = 4 + h // 4
                    k = mm(bank[b][:, (h % 4) * 128:(h % 4 + 1) * 128], KD[rs, 8 * t + h, :], VB[rs, 8 * t + h, :], True, True,
                           after=[free[b], t_vn, t_kd], mark=(h % 4 == 3))
                    if h % 4 == 3:
                        for hh in range(h - 3, h + 1):
                            s_, ps = S[:, hh, :], bank[b][:, (hh % 4) * 128:(hh % 4 + 1) * 128]
                            if c:
                                V(ve.scalar_tensor_tensor, s_, s_, dl[:, c, hh:hh + 1], ps, ALU.mult, ALU.add, after=[k])
                            else:
                                V(ve.tensor_copy, s_, ps, after=[k])
                        free[b] = V.last
                t_s = V.last
            for h in range(8):
                i = 8 * t + h
                t_o = mm(bank[2 + h // 4][rs, (h % 4) * 128:(h % 4 + 1) * 128], AQ[rs, i, rs], VB[rs, i, :], c == 0 and h % 4 == 0,
                         h % 4 == 3, skip=True, after=[free[2 + h // 4], t_vn], mark=(h == 7))
            if c == 1:
                t_o_of[0] = t_o
                post = o_rows(0)
                next(post)
            if c < 3:
                for h in range(8):
                    own(c + 1, h)
            if c == 2:
                next(post)
                finish(post)
        t_o_of[0] = t_o
        t_xx = small([(X, p["x"].rearrange("o (a p) d -> p (o a) d", p=128))], after=[PE.last, V.last, A.last])
        finish(o_rows(1))
        t_ot = [V.last, A.last]
        dump("gdn_o", OT, t_ot)
        toks = out_proj(OT, p["a_w_out"][0], (0, 1, 2, 3), lambda k: t_ot)
        return residual_norm(add_banks((0, 1, 2, 3), [[k, t_xx] for k in toks]), 0, gb, t_gb, [sq[:, 0, 0:16], sq[:, 0, 16:32]])

    def log1p(y, u, d, ready):
        V(ve.tensor_scalar, u, y, 1.0, None, ALU.add, after=[ready])
        V(ve.tensor_scalar, d, u, 1.0, 1e-30, ALU.subtract, ALU.add, after=[V.last])
        A(ac.activation, u, u, ACT.Ln, after=[V.last])
        V(ve.reciprocal, d, d, after=[V.last])
        V(ve.tensor_scalar, u, u, 1e-30, None, ALU.add, after=[A.last])
        V(ve.tensor_tensor, u, u, d, ALU.mult, after=[V.last])
        V(ve.tensor_tensor, y, y, u, ALU.mult, after=[V.last])

    def out_proj(ot, w, banks4, ready):
        W = streams["now"]
        keys = []

        def step(k, t, w_, t_w, mark):
            for h in range(2):
                b = banks4[2 * t + h]
                tk = mm3(bank[b][:, :], sl(ot, ALL, k, slice(t * 128, (t + 1) * 128)), sl(w_, ALL, 0, slice(512 * h, 512 * h + 512)),
                         k == 0, k == 7, [t_w, ready(k), free[b]], mark=(mark and h == 1))
            return tk
        for g in range(2):
            keys += W.open((2, 1024), [(whole, rows_of(w, 2 * g, 2 * g + 2))], [lambda d, q=q: d[:, q:q + 1, :] for q in range(2)])
        for k in range(4):
            w_, t_w = W.get(keys[k])
            for t in range(2):
                tk = step(k, t, w_, t_w, t == 1)
            W.done(keys[k], tk)
        for g in range(2, 4):
            keys += W.open((2, 1024), [(whole, rows_of(w, 2 * g, 2 * g + 2))], [lambda d, q=q: d[:, q:q + 1, :] for q in range(2)])
        for k in range(4, 8):
            w_, t_w = W.get(keys[k])
            tok0 = step(k, 0, w_, t_w, k == 7)
        for k in range(4, 8):
            w_, t_w = W.get(keys[k])
            tok1 = step(k, 1, w_, t_w, True)
            W.done(keys[k], tok1)
        return [tok0, tok1]

    def ffn(x_ready):
        Stack.at = base
        gb = v3(take(2 * D), 2)
        t_gb = small([(gb[:, 0, :], bcast(p["ln_g"][0, 1], 128)), (gb[:, 1, :], bcast(p["ln_b"][0, 1], 128))],
                     after=[V.last, PE.last, A.last])
        sg = v3(take(2 * T), 2)
        W = streams["now"]
        W.restrict(3)
        hT = [tuple(v3(parts_[:, 3 + a, q, :], 4) for q in range(2)) for a in range(2)]
        tm = take(32)
        groups = [(512 * i, 4) for i in range(5)] + [(2560, 2)]
        wg, wu, wd = p["ffn_w_gate"][0], p["ffn_w_up"][0], p["ffn_w_down"][0]
        h_ready = [None, None]
        h_used = [PE.last, PE.last]
        s_used = [None, None]
        toks = [None, None]

        def down(gi):
            c0, m = groups[gi]
            last = gi == len(groups) - 1
            k0 = c0 // 128
            keys = []

            def step(j, t, w, t_w, mark):
                for h in range(2):
                    b = 2 * t + h
                    k = mm3(bank[b][:, :], sl(hT[gi % 2], ALL, j, slice(t * 128, (t + 1) * 128)), sl(w, ALL, 0, slice(512 * h, 512 * h + 512)),
                            gi == 0 and j == 0, last and j == m - 1, [t_w, h_ready[gi % 2], free[b]], mark=(mark and h == 1))
                return k
            for g in range(0, m, 2):
                keys = W.open((2, 1024), [(whole, rows_of(wd, k0 + g, k0 + g + 2))], [lambda d, q=q: d[:, q:q + 1, :] for q in range(2)])
                if last:
                    for q in range(2):
                        w, t_w = W.get(keys[q])
                        toks[0] = step(q, 0, w, t_w, q == 1)
                for q in range(2):
                    w, t_w = W.get(keys[q])
                    if not last:
                        step(g + q, 0, w, t_w, False)
                    toks[1] = step(g + q, 1, w, t_w, True)
                    W.done(keys[q], toks[1])
            h_used[gi % 2] = toks[1]
        nb = 0
        for gi, (c0, m) in enumerate(groups):
            for j in range(m):
                if j % 2 == 0:
                    c = c0 + j * 128
                    ks = [W.open((8, 256), [(whole, rows_of(x, 0, 8)[:, :, c:c + 256])],
                                 [lambda d, q=q: d[:, :, q * 128:(q + 1) * 128] for q in range(2)]) for x in (wg, wu)]
                b = 4 + nb % 4
                for q in range(2):
                    w, tw = W.get(ks[q][j % 2])
                    for k_ in range(8):
                        k = mm3(bank[b][:, q * T:(q + 1) * T], sl(w, ALL, k_), sl(XT, ALL, k_), k_ == 0, k_ == 7,
                                [tw, free[b], x_ready], mark=(k_ == 7))
                    W.done(ks[q][j % 2], k)
                s_ = sg[:, nb % 2, :]
                A(ac.activation, s_, bank[b][:, 0:T], ACT.Silu, after=[k, s_used[nb % 2]])
                free[b] = V(ve.tensor_tensor, s_, s_, bank[b][:, T:2 * T], ALU.mult, after=[A.last])
                s_used[nb % 2] = split(sl(hT[gi % 2], ALL, j), s_, [free[b], h_used[gi % 2]])
                nb += 1
            h_ready[gi % 2] = V.last
            if gi:
                down(gi - 1)
        down(len(groups) - 1)
        W.restrict(PIECES)
        return residual_norm(add_banks((0, 1, 2, 3), toks), 1, gb, t_gb, [tm[:, 0:16], tm[:, 16:32]])

    def attend(units, buf, st, pT, banks, qk, mask, scale, pv, extra=None, rows_ready=None):
        bq, bt, bo = banks
        n = len(units)
        tok = [{} for _ in range(n)]
        s_used, p_used = [None] * 3, [None, None]

        def stage1(i):
            hs, wd, key = units[i]
            nh, a = len(hs), i % 3
            b = bq[i % len(bq)]
            w1 = wd + (1 if extra else 0)
            sv = buf[a][:, 0:nh * w1].rearrange("p (h w) -> p h w", h=nh)
            m, nm, sm = (st[:, 16 * a + 4 * q:16 * a + 4 * q + nh] for q in range(3))
            for q in range(nh):
                k = qk(units[i], q, bank[b][:, q * wd:(q + 1) * wd], [free[b]], q == nh - 1)
            if extra:
                V(ve.tensor_copy, sv[:, :, wd], extra(units[i]), after=[s_used[a]])
            free[b] = V(ve.scalar_tensor_tensor, sv[:, :, 0:wd], v3(bank[b][:, :], nh), scale, mask(units[i]), ALU.mult, ALU.add,
                        after=[k, s_used[a], rows_ready])
            V(ve.tensor_reduce, m, sv, AX_X, ALU.max, after=[V.last])
            V(ve.tensor_scalar, nm, m, -1.0, None, ALU.mult, after=[V.last, tok[i - 3].get("exp") if i > 2 else None])
            t_m = V.last
            for q in range(nh):
                A(ac.activation, sv[:, q, :], sv[:, q, :], ACT.Exp, bias=nm[:, q:q + 1], accum_out=sm[:, q:q + 1],
                  after=[t_m, tok[i - 3].get("norm") if i > 2 else None])
            tok[i].update(exp=A.last, sv=sv, sm=sm)

        def stage2(i):
            hs, wd, key = units[i]
            nh = len(hs)
            sv, sm = tok[i]["sv"], tok[i]["sm"]
            V(ve.reciprocal, sm, sm, after=[tok[i]["exp"]])
            t_r = V.last
            for q in range(nh):
                V(ve.tensor_scalar, sv[:, q, 0:wd], sv[:, q, 0:wd], sm[:, q:q + 1], None, ALU.mult, after=[t_r])
            tok[i]["norm"] = V.last

        def stage3(i):
            hs, wd, key = units[i]
            a, nt, sv = i % 2, wd // 128, tok[i]["sv"]
            b = bt[i % len(bt)]
            for q in range(4):
                k = tr(bank[b][:, q * 128:(q + 1) * 128], sv[:, q // nt, (q % nt) * 128:(q % nt + 1) * 128], after=[tok[i]["norm"], free[b]],
                       mark=(q == 3))
            s_used[i % 3] = k
            free[b] = A(ac.copy, pT[:, a, :], bank[b][:, :], after=[k, p_used[a]])
            tok[i]["pT"] = A.last

        def stage4(i):
            b = bo[i % len(bo)]
            p_used[i % 2] = pv(units[i], pT[:, i % 2, :], tok[i]["pT"], b)
        for i in range(n + 3):
            if 2 <= i <= n + 1:
                stage3(i - 2)
            if i < n:
                stage1(i)
            if 1 <= i <= n:
                stage2(i - 1)
            if i >= 3:
                stage4(i - 3)
            yield

    def band():
        t_p = small([(oh[0:32, :], p["c_oh"]), (em[0:16, :], p["c_em"]), (rb[0:32, :], p["rel_bias"]),
                     (vb, bcast(bi[1152:1280], 128)), (sk, bcast(p["b_sinks"][0], 128))])
        k = mm(bank[5][0:16, 0:384], rb[0:32, :], oh[0:32, :], True, True, after=[t_p, free[5]], mark=True)
        free[5] = V(ve.tensor_tensor, em[0:16, :], em[0:16, :], bank[5][0:16, 0:384], ALU.add, after=[k])
        scr = dram("scr_band", [16, 128, 384])
        t_w = small([(scr, em[0:16, :].unsqueeze(1).broadcast_to([16, 128, 384]))], after=[V.last])
        return t_w, bass.AP(tensor=scr.tensor, offset=127, ap=[[383, 128], [128 * 384, 16], [1, 256]])

    bias = v3(take_top(16 * T, WORK), 16)

    def swa_loads(after):
        gb = v3(take_top(2 * D, WORK - 16 * T), 2)
        t_bias = small([(bias, t_band[1])], after=[t_band[0], after])
        t_gb = small([(gb[:, 0, :], bcast(p["ln_g"][1, 0], 128)), (gb[:, 1, :], bcast(p["ln_b"][1, 0], 128))], after=[after])
        return gb, t_bias, t_gb

    def swa(x_ready, loaded):
        gb, t_bias, t_gb = loaded
        Stack.at = base
        qT = v3(take(8 * T), 8)
        kd = v3(take(2 * T), 2)
        vv = v3(take(2 * 128), 2)
        st = take(48)
        buf = [take(516) for _ in range(3)]
        pT = v3(take(2 * 512), 2)
        oT = v3(take(8 * T), 8)
        tm = take(32)
        pc = CWB[:, 64:74]
        w = p["b_w_in"][0]
        wr = rows_of(w, 0, 8)
        W = streams["now"]
        keys = W.open((8, 256), [(lambda d, q=q, i=i: d[:, :, 128 * q + 64 * i:128 * q + 64 * i + 64], wr[:, :, 1024 + 64 * q:1088 + 64 * q])
                                 for q in range(2) for i in range(2)], [lambda d, q=q: d[:, :, q * 128:(q + 1) * 128] for q in range(2)])
        for kv in range(2):
            wk, t_wk = W.get(keys[kv])
            for kk in range(8):
                k = mm3(bank[4][:, kv * T:(kv + 1) * T], sl(wk, ALL, kk), sl(XT, ALL, kk), kk == 0, kk == 7,
                        [t_wk, free[4], x_ready], mark=(kk == 7))
            W.done(keys[kv], k)
        for kv in range(2):
            V(ve.tensor_scalar, kd[:, kv, :], bank[4][:, kv * T:(kv + 1) * T], pc[:, 8 + kv:9 + kv], None, ALU.add, after=[k])
        free[4] = V.last
        k = narrow(bank[5], wr[:, :, 1152:1280], 128, x_ready, 5)
        V(ve.tensor_tensor, vv, v3(bank[5][:, 0:256], 2), vb.unsqueeze(1).broadcast_to([128, 2, 128]), ALU.add, after=[k])
        free[5] = t_kv = V.last
        q_ready = [None] * 4

        def q_evac(i0, ps, m, tk):
            for j in range(m):
                V(ve.tensor_scalar, qT[:, i0 + j, :], ps[:, j, :], pc[:, i0 + j:i0 + j + 1], None, ALU.add, after=[tk])
            q_ready[i0 // 2] = V.last
            return V.last
        units = [([g + par, g + par + 2], 256, (1, par)) for g in range(0, 16, 4) for par in range(2)]
        units += [([g + par + 2 * i for i in range(4)], 128, (0, par)) for g in (0, 8) for par in range(2)]

        def qk(u, q, o, after, mark):
            (hs, wd, (n, par)) = u
            h = hs[q]
            assert q_ready[h // 4] is not None
            r = slice(64 * par, 64 * par + 64)
            return mm(o, qT[r, h // 2, n * 128:n * 128 + 128], kd[r, h // 8, 0:wd], True, True,
                      after=after + [q_ready[h // 4], t_kv, free[4]], mark=mark)

        def mask(u):
            hs, wd, (n, par) = u
            hv = slice(hs[0], hs[-1] + 1, 2)
            return bias[:, hv, 128:256] if n == 0 else bias[:, hv, :]

        def pv(u, pt, t_pt, ob):
            hs, wd, (n, par) = u
            nt = wd // 128
            r = slice(64 * par, 64 * par + 64)
            for q in range(4):
                i, kt = q // nt, q % nt
                kvh = hs[i] // 8
                k = mm(bank[ob][r, i * 128:(i + 1) * 128], vv[:, kt, kvh * 64:kvh * 64 + 64], pt[:, q * 128:(q + 1) * 128],
                       kt == 0, kt == nt - 1, after=[t_pt, free[ob]], mark=(q == 3))
            nh = len(hs)
            free[ob] = V(ve.tensor_copy, oT[r, hs[0] // 2:hs[0] // 2 + nh, n * 128:n * 128 + 128],
                         bank[ob][r, 0:nh * 128].rearrange("p (a b) -> p a b", a=nh), after=[k])
            return k

        def sinks(u):
            return sk[:, slice(u[0][0], u[0][-1] + 1, 2)]
        def attention():
            yield
            yield from attend(units, buf, st, pT, ((2, 3), (4, 5), (6, 7)), qk, mask, 0.125, pv, extra=sinks, rows_ready=t_bias)
        g = attention()
        back.append(g)
        fm_tiles(XT, w, 0, 8, (0, 1), q_evac, x_ready, ticks=2)
        finish(g)
        t_o = [V.last, A.last]
        dump("swa_o", oT, t_o)
        t_x = PE.last
        t_s = [split(sl(XT, ALL, slice(2 * i, 2 * i + 2)), oT[:, 2 * i:2 * i + 2, :], [t_x, t_o]) for i in range(4)]
        toks = out_proj(XT, p["b_w_out"][0], (0, 1, 2, 3), lambda k: t_s[k // 2])
        return residual_norm(add_banks((0, 1, 2, 3), toks), 2, gb, t_gb, [tm[:, 0:16], tm[:, 16:32]])

    class B2:
        rot_used = [None, None]
    Stack.at = base
    B2.cosA, B2.sinA, B2.cosI, B2.sinI = (take(T) for _ in range(4))
    B2.prm = take(256)
    B2.keep = take(384)
    B2.tm = take(32)
    B2.flag = take(8)[:, 0:1].bitcast(I32)
    B2.base = Stack.at

    def moe(x_ready, x_rows, setup):
        Stack.at = B2.base
        gb = v3(take(2 * D), 2)
        fa = v3(take(2 * D), 2)
        xg = [tuple(v3(cols_[:, q, 1024 * a:1024 * a + 1024], 8) for q in range(2)) for a in range(2)]
        sg = v3(take(2 * 512), 2)
        hh = v3(take(2 * 512), 2)
        hT = [tuple(v3(parts_[:, 4, q, 512 * a:512 * a + 512], 4) for q in range(2)) for a in range(2)]
        y = take(1024)
        P_ = v4(take(2 * 256), 2, 2)
        PG = v3(take(256), 2)
        PT = v4(take(2 * 256), 2, 2)
        rt = take(256)
        tm = take(32)
        B2.tmp = take(4 * T + 4 + 176 + 64)
        after = [V.last, PE.last, A.last]
        streams["now"].restrict(4)
        t_gb = small([(gb[:, 0, :], bcast(p["ln_g"][1, 1], 128)), (gb[:, 1, :], bcast(p["ln_b"][1, 1], 128))], after=after)
        lg, sel, gate, rank, rank2 = (v3(rt[:, 16 * i:16 * i + 16], 2) for i in range(5))
        mx = v3(rt[:, 80:96], 2)
        ix = v3(rt[:, 96:112], 2)
        ixu = v3(rt[:, 112:128].bitcast(U32), 2)
        g01 = v3(rt[:, 128:132], 2)
        oh = v4(rt[:, 144:176], 2, 2)
        cnt = rt[:, 176:184]
        cm = rt[:, 184:185]
        flag = B2.flag
        k = narrow(bank[7], rows_of(p["moe_router"][0], 0, 8), 8, x_ready, 7)
        t_router = k
        free[7] = V(ve.tensor_copy, lg, v3(bank[7][:, 0:16], 2), after=[k])
        for j in range(2):
            for t in range(2):
                V(ve.max, mx[:, t, :], lg[:, t, :], after=[V.last])
                V(ve.max_index, ixu[:, t, :], mx[:, t, :], lg[:, t, :], after=[V.last])
            V(ve.tensor_copy, ix, ixu, after=[V.last])
            V(ve.tensor_copy, g01[:, :, j:j + 1], mx[:, :, 0:1], after=[V.last])
            for t in range(2):
                V(ve.tensor_scalar, oh[:, j, t, :], C(C_IOTA)[:, 0:8], ix[:, t, 0:1], None, ALU.is_equal, after=[V.last])
            if j == 0:
                V(ve.scalar_tensor_tensor, lg, oh[:, 0, :, :], -3.0e38, lg, ALU.mult, ALU.add, after=[V.last])
        V(ve.tensor_tensor, g01[:, :, 1:2], g01[:, :, 1:2], g01[:, :, 0:1], ALU.subtract, after=[V.last])
        A(ac.activation, g01[:, :, 1:2], g01[:, :, 1:2], ACT.Exp, after=[V.last])
        V(ve.tensor_scalar, g01[:, :, 0:1], g01[:, :, 1:2], 1.0, None, ALU.add, after=[A.last])
        V(ve.reciprocal, g01[:, :, 0:1], g01[:, :, 0:1], after=[V.last])
        V(ve.tensor_tensor, g01[:, :, 1:2], g01[:, :, 1:2], g01[:, :, 0:1], ALU.mult, after=[V.last])
        V(ve.tensor_tensor, sel, oh[:, 0, :, :], oh[:, 1, :, :], ALU.add, after=[V.last])
        for t in range(2):
            V(ve.tensor_scalar, gate[:, t, :], oh[:, 0, t, :], g01[:, t, 0:1], None, ALU.mult, after=[V.last])
            V(ve.scalar_tensor_tensor, gate[:, t, :], oh[:, 1, t, :], g01[:, t, 1:2], gate[:, t, :], ALU.mult, ALU.add, after=[V.last])
        t_sel = V.last
        mm(bank[7][:, 0:8], C(C_LT), sel[:, 0, :], True, True, after=[t_sel, free[7]])
        mm(bank[7][:, 8:16], ones, sel[:, 0, :], True, False)
        mm(bank[7][:, 8:16], C(C_LT), sel[:, 1, :], False, True)
        mm(bank[7][:, 16:24], ones, sel[:, 0, :], True, False)
        k = mm(bank[7][:, 16:24], ones, sel[:, 1, :], False, True, mark=True)
        V(ve.tensor_copy, rank, v3(bank[7][:, 0:16], 2), after=[k])
        V(ve.tensor_copy, cnt, bank[7][:, 16:24], after=[k])
        free[7] = V.last
        V(ve.tensor_reduce, cm, cnt, AX_X, ALU.max, after=[V.last])
        V(ve.tensor_scalar, cm, cm, 128.0, None, ALU.is_gt, after=[V.last])
        V(ve.tensor_copy, flag, cm, after=[V.last])
        t_flag = V.last
        V(ve.tensor_scalar, rank2, rank, -128.0, None, ALU.add, after=[V.last])
        t_rank = V.last
        dump("moe_gate", gate, [t_rank])

        def experts(rk, first_pass):
            steps = [(e, g) for e in range(NE) for g in range(7)]
            xg_t, pt_t = [None] * NE, [None] * NE
            W = streams["now"]
            hu, tu, xu, pu = [None, None], [t_router, t_router], [t_router, t_router], [None, None]
            h_t, hT_t = [None] * len(steps), [None] * len(steps)
            yt = [None]

            def prep(e):
                a = e % 2
                for t in range(2):
                    V(ve.tensor_scalar, P_[:, a, t, :], C(C_IOTA), rk[:, t, e:e + 1], sel[:, t, e:e + 1], ALU.is_equal, ALU.mult,
                      after=[t_rank, xu[a]])
                    V(ve.tensor_scalar, PG[:, t, :], C(C_IOTA), rk[:, t, e:e + 1], gate[:, t, e:e + 1], ALU.is_equal, ALU.mult,
                      after=[t_rank, PE.last])
                t_P = V.last
                for half in range(2):
                    for j in range(4):
                        kk = 4 * half + j
                        for t in range(2):
                            k = mm(bank[7][:, j * 128:(j + 1) * 128], X[:, t, kk * 128:(kk + 1) * 128], P_[:, a, t, :], t == 0, t == 1,
                                   after=[t_P, free[7], x_rows], mark=(j == 3 and t == 1))
                    free[7] = split(sl(xg[a], ALL, slice(4 * half, 4 * half + 4)), v3(bank[7][:, :], 4), [k, xu[a]])
                xg_t[e] = free[7]
                for t in range(2):
                    k = tr(bank[7][:, t * 128:(t + 1) * 128], PG[:, t, :], after=[t_P, free[7]], mark=(t == 1))
                free[7] = A(ac.copy, PT[:, a, :, :], v3(bank[7][:, 0:256], 2), after=[k, pu[a]])
                pt_t[e] = A.last

            def gate_up(n):
                e, g = steps[n]
                a = e % 2
                bb = 2 * (n % 2)
                for q, name in enumerate(("moe_w_gate", "moe_w_up")):
                    src = p[name][0, e][:, 512 * g:512 * g + 512]
                    for kh in range(2):
                        keys = W.open((4, 512), [(whole, rows_of(src, 4 * kh, 4 * kh + 4))], [lambda d, i=i: d[:, 2 * i:2 * i + 2, :] for i in range(2)])
                        for key in keys:
                            w, t_w = W.get(key)
                            for i in range(2):
                                kk = 4 * kh + 2 * key[1] + i
                                k = mm3(bank[bb + q][:, :], sl(xg[a], ALL, kk), sl(w, ALL, i), kk == 0, kk == 7,
                                        [t_w, xg_t[e], free[bb + q]], mark=(i == 1))
                            W.done(key, k)
                    if q == 0:
                        free[bb] = A(ac.activation, sg[:, n % 2, :], bank[bb][:, :], ACT.Silu, after=[k, h_t[n - 2] if n > 1 else None])
                xu[a] = k
                free[bb + 1] = V(ve.tensor_tensor, hh[:, n % 2, :], sg[:, n % 2, :], bank[bb + 1][:, :], ALU.mult, after=[A.last, k, hu[n % 2]])
                h_t[n] = V.last

            def turn(n):
                for j in range(4):
                    k = tr(bank[6][:, j * 128:(j + 1) * 128], hh[:, n % 2, j * 128:(j + 1) * 128], after=[h_t[n], free[6]], mark=(j == 3))
                hu[n % 2] = k
                free[6] = hT_t[n] = split(hT[n % 2], v3(bank[6][:, :], 4), [k, tu[n % 2]])

            def down(n):
                e, g = steps[n]
                src = p["moe_w_down"][0, e][512 * g:512 * g + 512, :]
                for g2 in range(2):
                    for key in W.open((2, 1024), [(whole, rows_of(src, 2 * g2, 2 * g2 + 2))], [lambda d, i=i: d[:, i:i + 1, :] for i in range(2)]):
                        w, t_w = W.get(key)
                        j = 2 * g2 + key[1]
                        for h in range(2):
                            k = mm3(bank[4 + h][:, :], sl(hT[n % 2], ALL, j), sl(w, ALL, 0, slice(512 * h, 512 * h + 512)), g == 0 and j == 0,
                                    g == 6 and j == 3, [t_w, hT_t[n], free[4 + h]], mark=(h == 1 or j == 3))
                        W.done(key, k)
                tu[n % 2] = k
                if g == 6:
                    free[4] = V(ve.tensor_copy, y[:, 0:512], bank[4][:, :], after=[k, yt[0]])
                    free[5] = A(ac.copy, y[:, 512:1024], bank[5][:, :], after=[k, yt[0]])

            def scatter(e):
                t_y = [free[4], free[5]]
                for t in range(2):
                    for h in range(2):
                        b = 6 + h
                        k = mm(bank[b][:, :], PT[:, e % 2, t, :], y[:, 512 * h:512 * h + 512], True, True,
                               after=[t_y, free[b], pt_t[e]], mark=True)
                        o = fa[:, t, 512 * h:512 * h + 512]
                        if first_pass and e == 0:
                            free[b] = V(ve.tensor_copy, o, bank[b][:, :], after=[k])
                        else:
                            free[b] = V(ve.tensor_tensor, o, o, bank[b][:, :], ALU.add, after=[k])
                yt[0] = pu[e % 2] = k

            prep(0)
            N = len(steps)
            for n in range(N + 3):
                if n < N:
                    gate_up(n)
                    if steps[n][1] == 4 and steps[n][0] + 1 < NE:
                        prep(steps[n][0] + 1)
                if first_pass and n > 2:
                    tick()
                if 1 <= n <= N:
                    turn(n - 1)
                if 2 <= n <= N + 1:
                    down(n - 2)
                if n >= 3 and steps[n - 3][1] == 6:
                    scatter(steps[n - 3][0])
            return V.last

        back.append(setup)
        experts(rank, True)
        finish(setup)

        streams["now"].barrier()
        saved = list(free)
        before = [q.last for q in (PE, V, A)]
        outer = {}
        for nm, q in queues.items():
            q.wait(t_flag)
            outer[nm] = (q.sem, q.n, q.q, dict(q.seen))
            q.wait(before)
            q.sem, q.n, q.q = sem("o_" + nm), 0, []
        for nm, q in queues.items():
            q.wait([b for b in before])
        streams["now"] = new_stream("more", "o_raw", before)
        streams["now"].limit = 4
        del streams["now"].slots[4]
        for b in range(8):
            free[b] = list(before)
        experts(rank2, False)
        ends = [q.last for q in queues.values() if q.n]
        for nm, q in queues.items():
            q.wait(ends)
            sub = q.q
            q.sem, q.n, q.q, q.seen = outer[nm]
            for w_ in before:
                q.wait(w_)
            q.q.append(("if", flag[0:1, :], sub))
        free[:] = saved
        streams["now"] = streams["main"]
        streams["now"].restrict(PIECES)
        streams["now"].pump()

        def add(t):
            return V(ve.scalar_tensor_tensor, X[:, t, :], X[:, t, :], ALPHA, fa[:, t, :], ALU.mult, ALU.add, after=[V.last, PE.last])
        return residual_norm(add, 3, gb, t_gb, [tm[:, 0:16], tm[:, 16:32]], cols=False)[1]

    O_Q, O_K, O_V, O_GA, O_IQ, O_IK, O_IW, O_XR, O_GR, O_MA, O_MB = 0, 1024, 2048, 3072, 4096, 5120, 5184, 5200, 6608, 8016, 9040

    def rms_rows(o, t, g, t_g, tmp, sq, ready):
        A(ac.activation, sq, X[:, t, :], ACT.Square, accum_out=tmp[:, 0:1], after=[ready, V.last, PE.last])
        V(ve.tensor_scalar, tmp[:, 1:2], tmp[:, 0:1], 1.0 / D, EPS, ALU.mult, ALU.add, after=[A.last])
        A(ac.activation, tmp[:, 2:3], tmp[:, 1:2], ACT.Sqrt, after=[V.last])
        V(ve.reciprocal, tmp[:, 3:4], tmp[:, 2:3], after=[A.last])
        return V(ve.scalar_tensor_tensor, o, X[:, t, :], tmp[:, 3:4], g, ALU.mult, ALU.mult, after=[V.last, t_g])

    def second_setup():
        z = B2.tmp
        pos, an, kr, rr = (z[:, T * i:T * i + T] for i in range(4))
        cr, pr = z[:, 4 * T:4 * T + 4], z[:, 4 * T + 4:4 * T + 180]
        u, d = z[:, 4 * T + 180:4 * T + 212], z[:, 4 * T + 212:4 * T + 244]
        after = [V.last, PE.last, A.last]
        t_p = small([(pos.bitcast(I32), bcast(p["positions_2"][0], 128)), (cr, p["c_rope"]),
                     (pr[:, 0:88], p["conv_w_2"].rearrange("l j (n c) -> (l j n) c", c=88)),
                     (pr[0:32, 88:176], p["conv_b_2"].rearrange("l (n c) -> (l n) c", c=88)),
                     (pr[32:64, 88:176], p["b_rg_2"].rearrange("l (n c) -> (l n) c", c=88)),
                     (pr[64:96, 88:176], p["b_ig_2"].rearrange("l (n c) -> (l n) c", c=88)),
                     (pr[96:128, 88:176], p["lru_lambda_2"].rearrange("l (n c) -> (l n) c", c=88))], after=after)
        yield
        for i in range(2):
            k = tr(bank[7][0:88, 128 * i:128 * i + 128], pr[:, 88 * i:88 * i + 88], after=[t_p, free[7]], mark=True)
        free[7] = V(ve.tensor_copy, B2.prm[0:88, :], bank[7][0:88, 0:256], after=[k])
        lam = B2.prm[0:88, 224:256]
        u, d = u[0:88, :], d[0:88, :]
        m = kr[0:88, 0:32]
        V(ve.tensor_scalar, u, lam, -1.0, None, ALU.mult, after=[V.last])
        V(ve.tensor_scalar, m, u, 0.0, None, ALU.max, after=[V.last])
        V(ve.tensor_tensor, lam, lam, u, ALU.min, after=[V.last])
        A(ac.activation, lam, lam, ACT.Exp, after=[V.last])
        log1p(lam, u, d, A.last)
        V(ve.tensor_tensor, lam, lam, m, ALU.add, after=[V.last])
        V(ve.tensor_scalar, lam, lam, -8.0, None, ALU.mult, after=[V.last])
        V(ve.tensor_copy, pos, pos.bitcast(I32), after=[V.last])
        yield
        magic = 12582912.0
        for i, (co, si) in enumerate(((B2.cosA, B2.sinA), (B2.cosI, B2.sinI))):
            V(ve.tensor_scalar, an, pos, cr[:, i:i + 1], None, ALU.mult, after=[V.last, A.last])
            V(ve.tensor_scalar, kr, an, 0.15915494309189535, magic, ALU.mult, ALU.add, after=[V.last])
            V(ve.tensor_scalar, kr, kr, magic, None, ALU.subtract, after=[V.last])
            for c in (6.28125, 0.0019350051879882812, 3.01991598196e-07):
                V(ve.scalar_tensor_tensor, an, kr, -c, an, ALU.mult, ALU.add, after=[V.last])
            V(ve.tensor_scalar, an, an, 3.1415925, -3.1415925, ALU.min, ALU.max, after=[V.last])
            A(ac.activation, si, an, ACT.Sin, after=[V.last])
            V(ve.tensor_scalar, rr, an, -1.0, None, ALU.mult, after=[V.last, A.last])
            V(ve.tensor_tensor, rr, rr, an, ALU.min, after=[V.last])
            V(ve.tensor_scalar, rr, rr, cr[:, 2:3], None, ALU.add, after=[V.last])
            A(ac.activation, co, rr, ACT.Sin, after=[V.last])
            yield
        B2.t_tab = [V.last, A.last]

    def second(l, x_rows):
        t_tab = B2.t_tab
        Stack.at = B2.base
        KT, QT = v3(take(8 * T), 8), v3(take(8 * T), 8)
        VV = v3(take(2 * D), 2)
        GA = v3(take(8 * T), 8)
        GR = take(11 * T)
        IQf = take(8 * T)
        IQ = v3(IQf, 8)
        IK = take(T)
        iw = take(32)
        rl = v3(take(2 * 512), 2)
        sw = take(2 * 4 * 88)
        s0, s1 = sw[:, 0:128], sw[:, 128:384]
        m8 = v3(take(16), 2)
        rb_ = take(4096)
        XC, AA, TH, XS = (v3(rb_[0:88, 1024 * i:1024 * i + 1024], 4) for i in range(4))
        RR, II = (v3(IQf[:, 1024 * i:1024 * i + 1024][0:88, :], 4) for i in range(2))
        WR = sw[0:88, :].rearrange("p (a c d) -> p a c d", a=2, c=4)
        bufs = [rl[:, 0, :], rl[:, 1, :]]
        pTb = v3(take(2 * 512), 2)
        rt_ = v3(take(2 * 512), 2)
        bufs.append(rt_[:, 0, :])
        sgm = pTb
        st = take(48)
        H = VV
        w = p["w_in_2"][l]
        wv = w[:, :].rearrange("(k p) c -> p k c", p=128)
        ng = LNC[:, 64 + 8 * l:72 + 8 * l]
        for t in range(2):
            tmp = B2.tm[:, 8 * t:8 * t + 8]
            A(ac.activation, GA[:, 0:4, :].rearrange("p a b -> p (a b)"), X[:, t, :], ACT.Square, accum_out=tmp[:, 0:1],
              after=[x_rows[t], PE.last])
            V(ve.tensor_scalar, tmp[:, 1:2], tmp[:, 0:1], 1.0 / D, EPS, ALU.mult, ALU.add, after=[A.last])
            A(ac.activation, tmp[:, 2:3], tmp[:, 1:2], ACT.Sqrt, after=[V.last])
            V(ve.reciprocal, tmp[:, 3:4], tmp[:, 2:3], after=[A.last])
            V(ve.tensor_scalar, H[:, t, :], X[:, t, :], tmp[:, 3:4], None, ALU.mult, after=[V.last, PE.last])
            cols_scaled(H[:, t, :], t, ng, None, [V.last, PE.last])
        x_ready = [V.last, A.last]
        tk_ = {}

        def rope(Xt, n, cos, sin, rotc, ready, name):
            for i in range(0, n, 2):
                m = min(2, n - i)
                b = 6 + (i // 2) % 2
                x2 = Xt[:, i:i + m, :]
                k = mm(bank[b][:, 0:m * T], rotc, x2.rearrange("p a b -> p (a b)"), True, True, after=[ready, free[b]], mark=True)
                r_ = rt_[:, (i // 2) % 2, 0:m * T].rearrange("p (a b) -> p a b", a=m)
                V(ve.tensor_tensor, r_, bank[b][:, 0:m * T].rearrange("p (a b) -> p a b", a=m), sin.unsqueeze(1).broadcast_to([128, m, T]),
                  ALU.mult, after=[k, t_tab, B2.rot_used[(i // 2) % 2]])
                free[b] = V.last
                V(ve.tensor_tensor, x2, x2, cos.unsqueeze(1).broadcast_to([128, m, T]), ALU.mult, after=[k, ready])
                B2.rot_used[(i // 2) % 2] = V(ve.tensor_tensor, x2, x2, r_, ALU.add, after=[V.last])
                yield
            tk_[name] = V.last

        W = streams["now"]
        key, = W.open((8, 128), [(lambda d, i=i: d[:, :, 64 * i:64 * i + 64], wv[:, :, O_IK:O_IK + 64]) for i in range(2)], [whole])
        wk, t_wk = W.get(key)
        for kk in range(8):
            k = mm3(bank[2][:, 0:T], sl(wk, ALL, kk), sl(XT, ALL, kk), kk == 0, kk == 7, [t_wk, free[2], x_ready], mark=(kk == 7))
        W.done(key, k)
        k = narrow(bank[2][:, T:T + 32], wv[:, :, O_IW:O_IW + 16], 16, x_ready, 2)
        A(ac.copy, IK, bank[2][:, 0:T], after=[k])
        free[2] = A(ac.mul, iw, bank[2][:, T:T + 32], 0.03125)

        def to(dst, extra=None):
            def f(i0, ps, m, tk):
                return A(ac.copy, dst[:, i0:i0 + m, :], ps, after=[tk, extra])
            return f
        fm_tiles(XT, w, O_IQ, 8, (0, 1), to(IQ), x_ready)
        t_iq = A.last
        iwv = v3(iw, 2)
        tril = C(C_TRIL)
        keep = (B2.keep[:, 0:128], B2.keep[:, 128:384])

        def index_steps():
            yield from rope(IK.unsqueeze(1), 1, B2.cosI, B2.sinI, C(C_ROTI), t_iq, "ik")
            yield from rope(IQ, 8, B2.cosI, B2.sinI, C(C_ROTI), t_iq, "iq")
            ru = [None, None]
            nr = 0
            for n, sc in ((1, s1), (0, s0)):
                wd = 128 * (n + 1)
                nh = 512 // wd
                first = True
                for g in range(0, 16, 2 * nh):
                    for par in range(2):
                        b = 4 + nr % 2
                        hs = [g + par + 2 * i for i in range(nh)]
                        for i, h in enumerate(hs):
                            k = mm(bank[b][:, i * wd:(i + 1) * wd], IQ[64 * par:64 * par + 64, h // 2, n * 128:n * 128 + 128],
                                   IK[64 * par:64 * par + 64, 0:wd], True, True, after=[tk_["iq"], free[b]], mark=(i == nh - 1))
                        free[b] = A(ac.activation, rl[:, nr % 2, :], bank[b][:, :], ACT.Relu, after=[k, ru[nr % 2]])
                        for i, h in enumerate(hs):
                            src = rl[:, nr % 2, i * wd:(i + 1) * wd]
                            if first:
                                V(ve.tensor_scalar, sc, src, iwv[:, n, h:h + 1], None, ALU.mult, after=[free[b]])
                                first = False
                            else:
                                V(ve.scalar_tensor_tensor, sc, src, iwv[:, n, h:h + 1], sc, ALU.mult, ALU.add, after=[free[b], V.last])
                        ru[nr % 2] = V.last
                        nr += 1
                        yield
            tk_["idx"] = PE.last
            bg = rl[:, 0, 0:128]
            V(ve.tensor_scalar, bg, tril, 1.0, 1.0e38, ALU.subtract, ALU.mult, after=[V.last])
            for sc in (s0, s1[:, 128:256]):
                V(ve.tensor_tensor, sc, sc, tril, ALU.mult, after=[V.last])
                V(ve.tensor_tensor, sc, sc, bg, ALU.add, after=[V.last])
            tv = [V.last, V.last]
            for r in range(8):
                for n, sc in ((0, s0), (1, s1)):
                    tv[n] = V(ve.max, m8[:, n, :], sc, after=[tv[n]])
                for n, sc in ((0, s0), (1, s1)):
                    tv[n] = V(ve.match_replace, sc, m8[:, n, :], sc, -3.0e38, after=[tv[n]])
                if r % 2:
                    yield
            for n, sc in ((0, s0), (1, s1)):
                V(ve.tensor_scalar, sc, sc, -2.0e38, None, ALU.is_lt, after=[tv[n]])
                c_ = sc[:, 128 * n:128 * n + 128]
                V(ve.tensor_tensor, c_, c_, tril, ALU.mult, after=[V.last])
                V(ve.tensor_scalar, keep[n], sc, 1.0, -NEG, ALU.subtract, ALU.mult, after=[V.last])
            tk_["keep"] = V.last
        ix = index_steps()
        back.append(ix)
        GRv = v3(GR, 11)
        xr_d = dram(f"scr_xr{l}", [1408, T])
        hr_d = dram(f"scr_hr{l}", [1408, T])
        fm_tiles(XT, w, O_XR, 11, (0, 1), to(GRv), x_ready, ticks=2)
        t_xr = small([(xr_d.rearrange("(i p) t -> p i t", p=128), GRv)], after=[A.last])
        fm_tiles(XT, w, O_Q, 8, (0, 1), to(QT), x_ready, ticks=2)
        t_q = A.last
        fm_tiles(XT, w, O_K, 8, (0, 1), to(KT), x_ready, ticks=2)
        t_k = A.last
        finish(ix)
        dump("keep", B2.keep, [tk_["keep"]])

        t_gate = {}

        def attention_steps():
            yield from rope(QT, 8, B2.cosA, B2.sinA, C(C_ROTA), t_q, "q")
            yield from rope(KT, 8, B2.cosA, B2.sinA, C(C_ROTA), t_k, "k")
            tk_["ropes"] = True
            units = [([g, g + 1, g + 2, g + 3], 128, 0) for g in (0, 4)] + [([g, g + 1], 256, 1) for g in (0, 2, 4, 6)]

            def qk(u, q, o, after, mark):
                hs, wd, n = u
                return mm(o, QT[:, hs[q], n * 128:n * 128 + 128], KT[:, hs[q], 0:wd], True, True,
                          after=after + [tk_["q"], tk_["k"]], mark=mark)

            def mask(u):
                return keep[u[2]].unsqueeze(1).broadcast_to([128, len(u[0]), u[1]])

            def pv(u, pt, t_pt, ob):
                hs, wd, n = u
                nt, nh = wd // 128, len(hs)
                for q in range(4):
                    i, kt = q // nt, q % nt
                    k = mm(bank[ob][:, i * 128:(i + 1) * 128], VV[:, kt, hs[i] * 128:(hs[i] + 1) * 128], pt[:, q * 128:(q + 1) * 128],
                           kt == 0, kt == nt - 1, after=[t_pt, free[ob], t_gate["v"]], mark=(q == 3))
                ga = GA[:, hs[0]:hs[0] + nh, n * 128:n * 128 + 128]
                free[ob] = V(ve.tensor_tensor, ga, ga, v3(bank[ob][:, 0:nh * 128], nh), ALU.mult, after=[k, t_gate["ga"]])
                return k
            yield from attend(units, bufs, st, pTb, ((2, 3), (4,), (5,)), qk, mask, 128.0 ** -0.5, pv, rows_ready=tk_["keep"])
            tk_["at"] = V.last

        prm = B2.prm[0:88, :]
        xr_v = xr_d.rearrange("(n c) t -> c n t", c=88)
        hr_v = hr_d.rearrange("(n c) t -> c n t", c=88)
        hr_out = []

        def rnn_steps():
            g_free = [tk_["keep"], tk_["idx"], V.last, A.last, PE.last]
            def fetch(g, after):
                return small([(XS, xr_v[:, 4 * g:4 * g + 4, :]),
                              (WR[:, 0], p["w_rg_2"][l].rearrange("n c d -> c n d")[:, 4 * g:4 * g + 4, :]),
                              (WR[:, 1], p["w_ig_2"][l].rearrange("n c d -> c n d")[:, 4 * g:4 * g + 4, :])], after=after)
            t_l = fetch(0, [t_xr, g_free])
            yield
            yield
            for g in range(4):
                for j in range(4):
                    n = 4 * g + j
                    V(ve.tensor_scalar, XC[:, j, :], XS[:, j, :], prm[:, 64 * l + 48 + n:64 * l + 49 + n],
                      prm[:, 128 + 16 * l + n:129 + 16 * l + n], ALU.mult, ALU.add, after=[t_l, g_free])
                for s in (1, 2, 3):
                    kk = V.last
                    for j in range(4):
                        n = 4 * g + j
                        cidx = 64 * l + 16 * (3 - s) + n
                        V(ve.scalar_tensor_tensor, XC[:, j, s:], XS[:, j, 0:T - s], prm[:, cidx:cidx + 1], XC[:, j, s:],
                          ALU.mult, ALU.add, after=[(kk[0], kk[1] - 3 + j)])
                t_xc = V.last
                yield
                for h in range(2):
                    for q, dst in ((0, RR), (1, II)):
                        b = 6 + q
                        for j in (0, 1):
                            k = mm(bank[b][0:88, j * T:(j + 1) * T], WR[:, q, 2 * h + j, :], XC[:, 2 * h + j, :], True, True,
                                   after=[t_xc, free[b]], mark=(j == 1))
                        for j in (0, 1):
                            n = 4 * g + 2 * h + j
                            c0 = 128 + 32 * (q + 1) + 16 * l + n
                            free[b] = A(ac.activation, dst[:, 2 * h + j, :], bank[b][0:88, j * T:(j + 1) * T], ACT.Sigmoid,
                                        bias=prm[:, c0:c0 + 1], after=[k, g_free])
                    yield
                t_si = A.last
                if g < 3:
                    t_l = fetch(g + 1, [t_xc, PE.last])
                for j in range(4):
                    c0 = 224 + 16 * l + 4 * g + j
                    A(ac.activation, AA[:, j, :], RR[:, j, :], ACT.Exp, scale=prm[:, c0:c0 + 1], after=[t_si, g_free])
                    A(ac.activation, TH[:, j, :], RR[:, j, :], ACT.Tanh, scale=prm[:, c0:c0 + 1], after=[t_si, g_free, hr_out])
                t_th = A.last
                V(ve.tensor_tensor, II, II, XC, ALU.mult, after=[t_si, t_xc])
                V(ve.tensor_scalar, RR, TH, -1.0, 1.0, ALU.mult, ALU.add, after=[t_th])
                yield
                V(ve.reciprocal, RR, RR, after=[V.last])
                V(ve.scalar_tensor_tensor, TH, TH, -2.0, RR, ALU.mult, ALU.mult, after=[V.last])
                A(ac.activation, TH, TH, ACT.Sqrt, after=[V.last])
                t_sq = A.last
                yield
                V(ve.tensor_tensor, II, II, TH, ALU.mult, after=[t_sq])
                t_u = V.last
                for j in range(4):
                    V(ve.tensor_tensor_scan, TH[:, j, :], AA[:, j, :], II[:, j, :], 0.0, ALU.mult, ALU.add, after=[t_u])
                g_free = [V.last, A.last, k]
                hr_out.append(small([(hr_v[:, 4 * g:4 * g + 4, :], TH)], after=[V.last]))
                yield
            hv = v3(rb_[:, 0:11 * T], 11)
            t_hr = small([(hv, hr_d.rearrange("(i p) t -> p i t", p=128))], after=[hr_out, V.last, A.last, PE.last])
            yield
            yield
            tk_["rn"] = V(ve.tensor_tensor, GRv, GRv, hv, ALU.mult, after=[t_hr, tk_["gr"]])
        at, rn = attention_steps(), rnn_steps()
        next(rn)
        back.append(at)
        rm_proj(XT, w, O_V, 1024, (0, 1), lambda t, c, ps, tk: A(ac.copy, VV[:, t, 512 * c:512 * c + 512], ps, after=[tk, x_ready]),
                x_ready, ticks=2)
        t_gate["v"] = A.last

        def silu_to(dst, extra=None):
            def f(i0, ps, m, tk):
                return A(ac.activation, dst[:, i0:i0 + m, :], ps, ACT.Silu, after=[tk, extra])
            return f
        back.remove(at)
        back.append(rn)
        fm_tiles(XT, w, O_GA, 8, (0, 1), silu_to(GA), x_ready, ticks=1)
        t_gate["ga"] = A.last
        back.append(at)
        fm_tiles(XT, w, O_GR, 11, (0, 1), silu_to(GRv, [t_xr]), x_ready, ticks=2)
        tk_["gr"] = A.last
        ctr = [0]
        finish(at)
        sgs = [PE.last, PE.last]
        t_at = tk_["at"]
        dump("attn", GA, [t_at])
        YA, MG = QT, KT
        t_ma0 = PE.last
        fm_tiles(GA, p["w_out_attn_2"][l], 0, 8, (0, 1, 2, 3), to(YA, PE.last), t_at, ticks=2, split_=False)
        t_ya = A.last

        def gate_a(i0, ps, m, tk):
            a = ctr[0] % 2
            ctr[0] += 1
            r = A(ac.activation, sgm[:, a, :], ps, ACT.Sigmoid, after=[tk, sgs[a]])
            sgs[a] = V(ve.tensor_tensor, MG[:, i0:i0 + m, :], v3(sgm[:, a, :], 2), YA[:, i0:i0 + m, :], ALU.mult, after=[r, t_ya, t_ma0])
            return r
        fm_tiles(XT, w, O_MA, 8, (0, 1, 2, 3), gate_a, x_ready, ticks=2)
        SB, t_mg = YA, V.last

        def gate_b(i0, ps, m, tk):
            return A(ac.activation, SB[:, i0:i0 + m, :], ps, ACT.Sigmoid, after=[tk, t_mg])
        fm_tiles(XT, w, O_MB, 8, (0, 1, 2, 3), gate_b, x_ready, ticks=2)
        t_sb, t_x = A.last, PE.last
        finish(rn)
        dump("rnn", GRv, [tk_["rn"]])
        t_s = []

        def merge(i0, ps, m, tk):
            mg = MG[:, i0:i0 + m, :]
            a = ctr[0] % 2
            ctr[0] += 1
            sb = v3(sgm[:, a, :], 2)
            r = V(ve.tensor_tensor, sb, SB[:, i0:i0 + m, :], ps, ALU.mult, after=[tk, t_sb, sgs[a], V.last])
            V(ve.tensor_tensor, mg, mg, sb, ALU.add, after=[r])
            sgs[a] = V.last
            t_s.append(split(sl(XT, ALL, slice(i0, i0 + m)), mg, [V.last, t_x]))
            return r
        fm_tiles(GRv, p["w_out_rnn_2"][l], 0, 8, (0, 1, 2, 3), merge, tk_["rn"], kt=11, split_=False)
        toks = out_proj(XT, p["w_o_2"][l], (4, 5, 6, 7), lambda k: t_s[k // 2])
        done = []
        for t in range(2):
            for h in range(2):
                b = 4 + 2 * t + h
                xs_ = X[:, t, 512 * h:512 * h + 512]
                free[b] = V(ve.tensor_tensor, xs_, xs_, bank[b][:, :], ALU.add, after=[toks[t]])
            done.append(V.last)
        return done

    def final_norm(rows):
        Stack.at = B2.base
        g_row = take(D)
        sq = take(D)
        t_g = small([(g_row, bcast(p["final_g_2"], 128))], after=[V.last, PE.last, A.last])
        return [rms_rows(X[:, t, :], t, g_row, t_g, B2.tm[:, 8 * t:8 * t + 8], sq, rows[t]) for t in range(2)]

    t_band = []
    t_xt, rows = gdn(t_x0)
    dump("x_a", X, rows)
    done = rows
    if stop >= 2:
        loaded = swa_loads([V.last, PE.last, A.last])
        t_xt, rows = ffn(t_xt)
        dump("x_b", X, rows)
    if stop >= 3:
        t_xt, rows = swa(t_xt, loaded)
        dump("x_c", X, rows)
    if stop >= 4:
        rows = moe(t_xt, rows, second_setup())
        dump("x_d", X, rows)
    if stop >= 5:
        rows = second(0, rows)
        dump("x_e", X, rows)
    if stop >= 6:
        rows = second(1, rows)
        rows = final_norm(rows)
    done = rows

    ov = out.rearrange("o (a p) d -> p (o a) d", p=128)
    t_out = small([(ov, X)], after=done, q=SP, name="s_out")
    SP.wait(t_out)

    if not final:
        return
    with nc.Block() as block:
        @block.sync
        def _(e):
            emit(e, SP.q)

        @block.gpsimd
        def _(e):
            emit(e, G.q)

        @block.tensor
        def _(e):
            emit(e, PE.q)

        @block.scalar
        def _(e):
            emit(e, A.q)

        @block.vector
        def _(e):
            emit(e, V.q)


_INS = ['x', 'a_w_in', 'a_conv_w', 'a_a_log', 'a_dt_bias', 'a_norm_w', 'a_w_out', 'b_w_in', 'b_b_in', 'b_sinks',
        'b_w_out', 'rel_bias', 'ffn_w_gate', 'ffn_w_up', 'ffn_w_down', 'moe_router', 'moe_w_gate', 'moe_w_up',
        'moe_w_down', 'ln_g', 'ln_b', 'positions_2', 'norm_g_2', 'w_in_2', 'conv_w_2', 'conv_b_2', 'w_rg_2', 'b_rg_2',
        'w_ig_2', 'b_ig_2', 'lru_lambda_2', 'w_out_attn_2', 'w_out_rnn_2', 'w_o_2', 'final_g_2']

_BUCKET = [b for b, n in enumerate(
    [1, 1, 1, 1, 1, 1, 1, 1, 1, 1, 1, 1, 1, 1, 1, 1, 3, 2, 3, 3, 4, 4, 5, 6, 6, 7, 8, 10, 10, 12, 14, 15]) for _ in range(n)]


def constants():
    import numpy as np
    i = np.arange(128)
    f = np.float32
    col, row = i[None, :], i[:, None]
    eye = (row == col).astype(f)

    def rot(n):
        m = np.zeros((128, 128), f)
        for o in range(128):
            b, r = o // n * n, o % n
            if r < n // 2:
                m[b + r + n // 2, o] = -1.0
            else:
                m[b + r - n // 2, o] = 1.0
        return m
    main = [eye, np.ones((128, 128), f), rot(128), rot(64), (col <= row).astype(f), (row < col).astype(f),
            np.broadcast_to(col, (128, 128)).astype(f)]
    same = (row // 64 == col // 64)
    gdn = [(same & (row <= col)).astype(f), (same & (row > col)).astype(f), same.astype(f)]
    for lv in range(6):
        gdn.append(((row >> (lv + 1) == col >> (lv + 1)) & ((row >> lv) % 2 == 1) & ((col >> lv) % 2 == 0)).astype(f))
    oh = np.zeros((32, 384), f)
    em = np.full((16, 384), NEG, f)
    for y in range(128, 256):
        oh[_BUCKET[255 - y], y] = 1.0
        em[:, y] = 0.0
    ia = f(10000.0) ** (-np.arange(0, 128, 2, dtype=f) / f(128))
    ii = f(10000.0) ** (-np.arange(0, 64, 2, dtype=f) / f(64))
    rope = np.stack([np.tile(ia, 2), np.tile(ii, 4), np.full(128, np.pi / 2, f), np.zeros(128, f)], 1).astype(f)
    return {"c_main": np.concatenate(main, 1), "c_gdn": np.concatenate(gdn, 1), "c_oh": oh, "c_em": em, "c_rope": rope}


_CONSTS = ["c_main", "c_gdn", "c_oh", "c_em", "c_rope"]


def kernel(**inputs):
    import numpy as _np
    import concourse.bacc as _bacc
    from concourse import mybir as _mybir
    from concourse.bass_utils import run_bass_kernel_spmd as _run

    nc = _bacc.Bacc("TRN2", target_bir_lowering=False, num_devices=1)
    table = constants()
    arrays, args = {}, {}
    for name in _INS + _CONSTS:
        a = _np.ascontiguousarray(inputs[name] if name in _INS else table[name])
        arrays[f"in_{name}_dram"] = a
        args[name] = nc.dram_tensor(f"in_{name}_dram", a.shape, _mybir.dt.from_np(a.dtype), kind="ExternalInput").ap()
    out = nc.dram_tensor("out_0_dram", (1, 256, 1024), _mybir.dt.float32, kind="ExternalOutput").ap()
    program(nc, args, out)
    r = _run(nc, [arrays], core_ids=[0])
    return r.results[0]["out_0_dram"]
```
